# Optimizing a Trainium2 kernel written in Bass

```python
import jax, jax.numpy as jnp
from jax import lax
import numpy as np

D_MODEL = 2048
BATCH = 1
SEQ = 256
DEPTH = 2

N_MIXERS = 2
N_A_LAYERS = (DEPTH + 1) // 2
N_B_LAYERS = DEPTH // 2

HG_EXPAND = 128
HG_HEADS = D_MODEL // HG_EXPAND
HG_FDIM = HG_HEADS * HG_EXPAND
HG_VDIM = D_MODEL
HG_HEAD_V = HG_VDIM // HG_HEADS
HG_CHUNK = 64
HG_SUB = 16
LB_FLOOR = 1e-30

GM_WIDTH = D_MODEL
GM_GROUPS = 16
GM_GROUP_DIM = GM_WIDTH // GM_GROUPS
GM_CHUNK = 128

FFN_HIDDEN = -(-8 * D_MODEL // (3 * 256)) * 256

PLE_DIM = 256

EPS = 1e-6

kernel_name = "hgrn2_gmlp_interleaved_sandwich_ple"

def _rmsnorm(x, g):
    xf = x.astype(jnp.float32)
    y = xf * lax.rsqrt(jnp.mean(xf * xf, axis=-1, keepdims=True) + EPS)
    return (y * g.astype(jnp.float32)).astype(x.dtype)

def _layernorm(x, g, b):
    xf = x.astype(jnp.float32)
    mu = jnp.mean(xf, axis=-1, keepdims=True)
    xc = xf - mu
    y = xc * lax.rsqrt(jnp.mean(xc * xc, axis=-1, keepdims=True) + EPS)
    return (y * g.astype(jnp.float32) + b.astype(jnp.float32)).astype(x.dtype)

def _hgrn_lower_bounds(lb_logits):
    sm = jax.nn.softmax(lb_logits.astype(jnp.float32), axis=0)
    return jnp.cumsum(sm, axis=0) - sm[:1]

def _hgrn2_chunkwise(q, k, v, log_f):
    B, S, H, K = q.shape
    V = v.shape[-1]
    C, L = HG_CHUNK, HG_SUB
    n = C // L
    nc = S // C

    def to_chunks(t):
        return t.reshape(B, nc, C, H, t.shape[-1]).transpose(1, 0, 3, 2, 4)

    causal = jnp.tril(jnp.ones((L, L), dtype=bool))[:, :, None]
    sub_mask = jnp.tril(jnp.ones((n, n), dtype=bool), k=-1)[:, :, None, None]
    eye_n = jnp.eye(n, dtype=jnp.float32)[:, None, :, None]

    def step(state, inp):
        qc, kc, vc, gc = inp
        b = jnp.cumsum(gc, axis=2)
        o_inter = jnp.einsum('bhtk,bhkv->bhtv', qc * jnp.exp(b), state)
        qs = qc.reshape(B, H, n, L, K)
        ks = kc.reshape(B, H, n, L, K)
        bs = b.reshape(B, H, n, L, K)
        gs = gc.reshape(B, H, n, L, K)
        bstart = bs[:, :, :, :1, :] - gs[:, :, :, :1, :]
        qf = qs * jnp.exp(bs - bstart)
        expo = bstart[:, :, :, None] - bs[:, :, None]
        kf = jnp.where(sub_mask, ks[:, :, None] * jnp.exp(jnp.where(sub_mask, expo, 0.0)), 0.0)
        a_off = jnp.einsum('bhjtk,bhjisk->bhjtis', qf, kf)
        diff = bs[:, :, :, :, None, :] - bs[:, :, :, None, :, :]
        wdec = jnp.where(causal, jnp.exp(jnp.where(causal, diff, 0.0)), 0.0)
        a_diag = jnp.einsum('bhjtk,bhjsk,bhjtsk->bhjts', qs, ks, wdec)
        a = (a_off + a_diag[:, :, :, :, None, :] * eye_n).reshape(B, H, C, C)
        o_intra = jnp.einsum('bhts,bhsv->bhtv', a, vc)
        b_last = b[:, :, -1:, :]
        new_state = (jnp.exp(b_last[:, :, 0, :])[..., None] * state
                     + jnp.einsum('bhsk,bhsv->bhkv', kc * jnp.exp(b_last - b), vc))
        return new_state, o_inter + o_intra

    state0 = jnp.zeros((B, H, K, V), dtype=jnp.float32)
    _, o = lax.scan(step, state0, (to_chunks(q), to_chunks(k), to_chunks(v), to_chunks(log_f)))
    return o.transpose(1, 0, 3, 2, 4).reshape(B, S, H, V)

def _hgrn2_mixer(h, w_in, lb, out_norm, w_out):
    B, S, _ = h.shape
    proj = h @ w_in
    zq, zf, zi, zg = jnp.split(proj, [HG_FDIM, 2 * HG_FDIM, 2 * HG_FDIM + HG_VDIM], axis=-1)
    q = jax.nn.silu(zq.astype(jnp.float32))
    zf = zf.astype(jnp.float32)
    log_lb = jnp.log(jnp.maximum(lb, LB_FLOOR))
    log_f = jnp.logaddexp(log_lb, jnp.log1p(-lb) + jax.nn.log_sigmoid(zf))
    k = (1.0 - lb) * jax.nn.sigmoid(-zf)
    v = zi.astype(jnp.float32)
    heads = lambda t, d: t.reshape(B, S, HG_HEADS, d)
    o = _hgrn2_chunkwise(heads(q, HG_EXPAND), heads(k, HG_EXPAND),
                         heads(v, HG_HEAD_V), heads(log_f, HG_EXPAND))
    o = _rmsnorm(o, out_norm) * jax.nn.silu(heads(zg.astype(jnp.float32), HG_HEAD_V))
    return o.reshape(B, S, HG_VDIM).astype(h.dtype) @ w_out

def _chunk_gmlp_mixer(h, w_in, ln_g, ln_b, w_s, b_s, w_out):
    B, S, _ = h.shape
    z = jax.nn.gelu(h @ w_in, approximate=False)
    u, v = jnp.split(z, 2, axis=-1)
    v = _layernorm(v, ln_g, ln_b)
    v = v.reshape(B, S // GM_CHUNK, GM_CHUNK, GM_GROUPS, GM_GROUP_DIM)
    ws = w_s * jnp.tril(jnp.ones((GM_CHUNK, GM_CHUNK), dtype=w_s.dtype))
    sv = jnp.einsum('gts,bnsgc->bntgc', ws, v) + b_s.T[None, None, :, :, None]
    y = u * sv.reshape(B, S, GM_WIDTH)
    return y @ w_out

def _swiglu(h, w_gate, w_up, w_down):
    return (jax.nn.silu(h @ w_gate) * (h @ w_up)) @ w_down

def setup_inputs(seed: int = 0) -> dict:
    key = jax.random.key(seed)
    ks = jax.random.split(key, 24)
    f32 = jnp.float32
    nrm = lambda k, shape, s: (jax.random.normal(k, shape, f32) * s).astype(f32)
    gain = lambda k, shape: 1.0 + nrm(k, shape, 0.02)
    D = D_MODEL
    return {
        "x": nrm(ks[0], (BATCH, SEQ, D), 1.0),
        "p": nrm(ks[1], (DEPTH, BATCH, SEQ, PLE_DIM), 1.0),
        "hg_w_in": nrm(ks[2], (N_A_LAYERS, D, 2 * HG_FDIM + 2 * HG_VDIM), D ** -0.5),
        "hg_lb_logits": nrm(ks[3], (N_A_LAYERS, HG_FDIM), 0.5),
        "hg_out_norm": gain(ks[4], (N_A_LAYERS, HG_HEAD_V)),
        "hg_w_out": nrm(ks[5], (N_A_LAYERS, HG_VDIM, D), HG_VDIM ** -0.5),
        "gm_w_in": nrm(ks[6], (N_B_LAYERS, D, 2 * GM_WIDTH), D ** -0.5),
        "gm_ln_g": gain(ks[7], (N_B_LAYERS, GM_WIDTH)),
        "gm_ln_b": nrm(ks[8], (N_B_LAYERS, GM_WIDTH), 0.02),
        "gm_w_s": nrm(ks[9], (N_B_LAYERS, GM_GROUPS, GM_CHUNK, GM_CHUNK), GM_CHUNK ** -0.5),
        "gm_b_s": 1.0 + nrm(ks[10], (N_B_LAYERS, GM_GROUPS, GM_CHUNK), 0.1),
        "gm_w_out": nrm(ks[11], (N_B_LAYERS, GM_WIDTH, D), GM_WIDTH ** -0.5),
        "norm_mix_pre": gain(ks[12], (DEPTH, D)),
        "norm_mix_post": gain(ks[13], (DEPTH, D)),
        "norm_ffn_pre": gain(ks[14], (DEPTH, D)),
        "norm_ffn_post": gain(ks[15], (DEPTH, D)),
        "ffn_w_gate": nrm(ks[16], (DEPTH, D, FFN_HIDDEN), D ** -0.5),
        "ffn_w_up": nrm(ks[17], (DEPTH, D, FFN_HIDDEN), D ** -0.5),
        "ffn_w_down": nrm(ks[18], (DEPTH, FFN_HIDDEN, D), FFN_HIDDEN ** -0.5),
        "ple_w_proj": nrm(ks[19], (DEPTH, PLE_DIM, D), PLE_DIM ** -0.5),
        "ple_w_gate": nrm(ks[20], (DEPTH, D, D), D ** -0.5),
        "ple_norm": gain(ks[21], (DEPTH, D)),
    }

def reference(x, p, hg_w_in, hg_lb_logits, hg_out_norm, hg_w_out, gm_w_in, gm_ln_g, gm_ln_b,
              gm_w_s, gm_b_s, gm_w_out, norm_mix_pre, norm_mix_post, norm_ffn_pre, norm_ffn_post,
              ffn_w_gate, ffn_w_up, ffn_w_down, ple_w_proj, ple_w_gate, ple_norm):
    lbs = _hgrn_lower_bounds(hg_lb_logits)
    h = x
    for i in range(DEPTH):
        j = i // N_MIXERS
        a = _rmsnorm(h, norm_mix_pre[i])
        if i % N_MIXERS == 0:
            m = _hgrn2_mixer(a, hg_w_in[j], lbs[j], hg_out_norm[j], hg_w_out[j])
        else:
            m = _chunk_gmlp_mixer(a, gm_w_in[j], gm_ln_g[j], gm_ln_b[j], gm_w_s[j], gm_b_s[j],
                                  gm_w_out[j])
        h = h + _rmsnorm(m, norm_mix_post[i])
        f = _swiglu(_rmsnorm(h, norm_ffn_pre[i]), ffn_w_gate[i], ffn_w_up[i], ffn_w_down[i])
        h = h + _rmsnorm(f, norm_ffn_post[i])
        e = p[i].astype(h.dtype) @ ple_w_proj[i]
        gate = jax.nn.sigmoid(h @ ple_w_gate[i])
        h = h + _rmsnorm(e * gate, ple_norm[i])
    return h


_drawn_inputs = setup_inputs


def setup_inputs(seed=0):
    import zlib

    import numpy as np

    out = dict(_drawn_inputs(seed))
    spreads = {}
    factors = {'hg_out_norm': 3.448,
     'gm_ln_g': 200.0,
     'gm_ln_b': 200.0,
     'norm_mix_post': 3.066,
     'norm_ffn_pre': 2.798,
     'norm_ffn_post': 11.758,
     'ple_norm': 12.862,
     'gm_b_s': 38.096}
    for name, (base, spread) in spreads.items():
        noise = np.random.default_rng([zlib.crc32(name.encode()), seed]).standard_normal(out[name].shape)
        drawn = base * np.exp(spread * noise) if base else spread * noise
        out[name] = __import__('jax').numpy.asarray(drawn.astype(out[name].dtype))
    for name, factor in factors.items():
        out[name] = (out[name] * factor).astype(out[name].dtype)
    return out
```

```python
import concourse.bass as bass
from concourse import mybir
from contextlib import ExitStack

P = 128
STAGES = 8
RING = 4
BLOCK = 512
KU = 2


KINDS = ("unit", "task", "job", "piece", "rstd", "kq", "grp")


def plan(phases):
    at, count = {}, dict.fromkeys(KINDS, 0)
    for name, times, *sizes in phases:
        at[name] = dict(count)
        for key, n in zip(KINDS, sizes):
            count[key] += times * n
    return at


def layer_tail_phases(layer):
    return [(name + str(layer), *sizes) for name, *sizes in (
        ("mix_norm", 1, 0, 0, 8, 8, 2),
        ("ffn_first", 1, 16, 2, 1, 1),
        ("ffn_loop", 10, 24, 6, 2, 2),
        ("ffn_last", 1, 12, 8, 2, 2),
        ("ffn_norm", 1, 0, 0, 8, 8, 1),
        ("ple", 1, 32, 4))]


PHASES = [
    ("start", 1, 0, 0, 9, 8, 1),
    ("hg_first", 1, 32, 4, 5, 0, 0, 3, 0),
    ("hg_loop", 3, 32, 4, 14, 2, 1, 9, 1),
    ("hg_out", 1, 32, 4, 9, 2, 1, 6, 1),
    *layer_tail_phases(0),
    ("ple_norm0", 1, 0, 0, 8, 8, 2),
    ("gm_v", 1, 32, 4, 4),
    ("gm_u", 1, 32, 4, 9, 6, 1),
    ("gm_out", 1, 32, 4, 3, 2),
    *layer_tail_phases(1),
    ("ple_norm1", 1, 0, 0, 0, 0, 1),
]
AT = plan(PHASES)
SIZE = {name: dict(zip(KINDS, [*sizes, *[0] * (len(KINDS) - len(sizes))])) for name, _, *sizes in PHASES}
NORMS = {name: n for n, name in enumerate(
    ["mix_norm0", "ffn_norm0", "ple_norm0", "mix_norm1", "ffn_norm1", "ple_norm1"])}
PRE_NORMS = {name: n for n, name in enumerate(["start", "mix_norm0", "ple_norm0", "mix_norm1"])}
GAINS = {name: n for n, name in enumerate(["mix0", "ffn0", "ple0", "ln", "mix1", "ffn1", "ple1"])}


class Numbers:

    def __init__(self, phase, it=0):
        self.at, self.size, self.it = AT[phase], SIZE[phase], it

    def of(self, kind, k):
        base = self.at[kind] + k
        return base if isinstance(self.it, int) and self.it == 0 else self.it * self.size[kind] + base

    def first(self, kind, k):
        return self.at[kind] + k

    def rounds(self, kind, k, ring):
        base = self.first(kind, k) // ring + 1
        if isinstance(self.it, int) and self.it == 0:
            return base
        assert self.size[kind] % ring == 0
        return self.it * (self.size[kind] // ring) + base


def trunk(nc, x, p, hg_w_in, hg_lb_logits, hg_out_norm, hg_w_out, gm_w_in, gm_ln_g, gm_ln_b, gm_w_s,
          gm_b_s, gm_w_out, norm_mix_pre, norm_mix_post, norm_ffn_pre, norm_ffn_post, ffn_w_gate,
          ffn_w_up, ffn_w_down, ple_w_proj, ple_w_gate, ple_norm, out):
    f32, f32r, i32 = mybir.dt.float32, mybir.dt.float32r, mybir.dt.int32
    ALU, ACT, AX = mybir.AluOpType, mybir.ActivationFunctionType, mybir.AxisListType

    D = x.shape[2]
    T = x.shape[1]
    NT = T // P
    KT = D // P
    NB = D // BLOCK
    HB = ffn_w_gate.shape[2] // BLOCK
    HD = hg_out_norm.shape[1]
    HG = BLOCK // HD
    GC = BLOCK // P
    LEVELS = [1 << i for i in range(7)]
    EPS, LB_FLOOR = 1e-6, 1e-30
    UW = KU * BLOCK
    PLE_K = p.shape[3] // P
    assert (D, T, HB, HD, PLE_K) == (2048, 256, 11, P, KU)

    ctx = ExitStack()
    with ctx:
        def sb(name, shape, dt=f32):
            return ctx.enter_context(nc.sbuf_tensor(name, shape, dt))

        def pb(name):
            return ctx.enter_context(nc.psum_tensor(name, [P, NT, BLOCK], f32))

        def sem(name):
            return ctx.enter_context(nc.semaphore(name))

        stage = sb("stage", [P, STAGES, UW])
        w_hi = sb("w_hi", [P, RING, UW], f32r)
        w_lo = sb("w_lo", [P, RING, UW], f32r)
        h = sb("h", [P, NT, D])
        m = sb("m", [P, NT, D])
        e = sb("e", [P, NT, D])
        a_hi = sb("a_hi", [P, KT, T], f32r)
        a_lo = sb("a_lo", [P, KT, T], f32r)
        y_hi = sb("y_hi", [P, KT, T], f32r)
        y_lo = sb("y_lo", [P, KT, T], f32r)
        p_hi = sb("p_hi", [P, PLE_K, T], f32r)
        p_lo = sb("p_lo", [P, PLE_K, T], f32r)
        gain = sb("gain", [P, D])
        sg = sb("sg", [P, NT, BLOCK])
        hid = sb("hid", [P, NT, BLOCK])
        zg = sb("zg", [P, NT, BLOCK])
        ident = sb("ident", [P, P])
        level_mask = sb("level_mask", [P, len(LEVELS), P // 2])
        upper = sb("upper", [P, P])
        rows = sb("rows", [P, P])
        cols = sb("cols", [P, P])
        junk = zg
        ss = sb("ss", [P, NT, NB])
        hss = sb("hss", [P, NT, NB])
        ms = sb("ms", [P, NT * HG])
        minus_half = sb("minus_half", [P, NT * HG])
        r_post = sb("r_post", [P, NT])
        r_pre = sb("r_pre", [P, NT])
        r_head = sb("r_head", [P, NT * HG])
        oss = sb("oss", [P, NT * HG])
        lb = sb("lb", [P, 6, KT])
        bn = sb("bn", [P, NT, NB, 6])
        mv = sb("mv", [P, NT, 2])
        f_g, k_g, q_g, tot = m[:, 0, 0:1024], m[:, 0, 1024:2048], m[:, 1, 0:1024], m[:, 1, 1024:2048]
        v_g = e[:, 0, 0:1024].rearrange("p (t n) -> p t n", t=NT)
        att = e[:, 0, 1024:2048]
        att_x = e[:, 1, 0:512]
        osq = e[:, 1, 1024:2048]
        ws_raw, wsT, ln_b = e[:, 0, :], e[:, 1, :], e[:, 0, :]
        p_tm = e[:, :, 0:PLE_K * P]

        C_MIX, C_FFN = (0, 32), (16, 48)
        C_LB, C_BS, C_ON = 64, 80, 96

        acc = [pb("acc0"), pb("acc1")]
        scr = [pb("scr0"), pb("scr1")]

        w_loaded = [sem(f"w_loaded{s}") for s in range(STAGES)]
        w_hi_ready = sem("w_hi_ready")
        w_lo_ready = sem("w_lo_ready")
        w_used = sem("w_used")
        acc_read = [sem("acc_read0"), sem("acc_read1")]
        job_done = sem("job_done")
        job_read = [sem("job_read0"), sem("job_read1")]
        piece_hi = sem("piece_hi")
        rows_loaded = sem("rows_loaded")
        const_step = sem("const_step")
        x_loaded = sem("x_loaded")
        gain_loaded = sem("gain_loaded")
        p_loaded = sem("p_loaded")
        ws_loaded = sem("ws_loaded")
        ln_b_loaded = sem("ln_b_loaded")
        lb_step = sem("lb_step")
        kq_ready = sem("kq_ready")
        osq_ready = sem("osq_ready")
        hid_ready = sem("hid_ready")
        h_ready = sem("h_ready")
        m_ready = sem("m_ready")
        ln_ready = sem("ln_ready")
        ss_ready = sem("ss_ready")
        hss_ready = sem("hss_ready")
        ms_ready = sem("ms_ready")
        rstd_ready = sem("rstd_ready")
        m_zeroed = sem("m_zeroed")
        gain_free = sem("gain_free")
        out_stored = sem("out_stored")

        block = ctx.enter_context(nc.Block())

        def unit_src(w, k0, n0):
            return w[k0 * P:(k0 + KU) * P, bass.ds(n0, BLOCK)].rearrange("(k p) n -> p k n", p=P)

        OUT_ORDER = ([(0, q) for q in range(6)] + [(1, q) for q in range(6)]
                     + [(0, 6), (0, 7), (1, 6), (1, 7)] + [(t, q) for t in (2, 3) for q in range(8)])
        IN_ORDER = [(t, q) for t in range(4) for q in range(8)]

        @block.sync
        def _(sp):
            def load(num, k, src):
                if num.first("unit", k) >= STAGES:
                    sp.wait_ge(w_lo_ready, num.of("unit", k) + 1 - STAGES)
                s = num.first("unit", k) % STAGES
                sp.dma_start(stage[:, s, :].rearrange("p (k n) -> p k n", k=KU), src).then_inc(w_loaded[s], 16)

            sp.dma_start(h[:], x[0].rearrange("(t p) d -> p t d", p=P)).then_inc(x_loaded, 16)

            w = hg_w_in[0]
            order = (1, 0, 2, 3)
            for k, (t, q) in enumerate(IN_ORDER):
                load(Numbers("hg_first"), k, unit_src(w, KU * q, order[t] * D))
            with sp.Fori(0, 3) as it:
                for k, (t, q) in enumerate(IN_ORDER):
                    load(Numbers("hg_loop", it), k, unit_src(w, KU * q, it * BLOCK + (order[t] * D + BLOCK)))

            def second_projection(phase, w):
                for k, (t, q) in enumerate(OUT_ORDER):
                    load(Numbers(phase), k, unit_src(w, KU * q, t * BLOCK))

            def down_src(layer, j, k):
                row = j * BLOCK + (k % 2) * KU * P
                return ffn_w_down[layer][bass.ds(row, KU * P), (k // 2) * BLOCK:(k // 2 + 1) * BLOCK] \
                    .rearrange("(k p) n -> p k n", p=P)

            def layer_tail(layer):
                s = str(layer)
                gate, up = ffn_w_gate[layer], ffn_w_up[layer]
                for k in range(8):
                    load(Numbers("ffn_first" + s), k, unit_src(gate, KU * k, 0))
                for k in range(8):
                    load(Numbers("ffn_first" + s), 8 + k, unit_src(up, KU * k, 0))
                with sp.Fori(0, HB - 1) as it:
                    num = Numbers("ffn_loop" + s, it)
                    for k in range(8):
                        load(num, k, unit_src(gate, KU * k, it * BLOCK + BLOCK))
                    for k in range(8):
                        load(num, 8 + k, down_src(layer, it, k))
                    for k in range(8):
                        load(num, 16 + k, unit_src(up, KU * k, it * BLOCK + BLOCK))
                num = Numbers("ffn_last" + s)
                for k in range(4):
                    load(num, k, unit_src(ple_w_proj[layer], 0, k * BLOCK))
                for k in range(8):
                    load(num, 4 + k, down_src(layer, HB - 1, k))
                for k, (t, q) in enumerate(IN_ORDER):
                    load(Numbers("ple" + s), k, unit_src(ple_w_gate[layer], KU * q, t * BLOCK))

            second_projection("hg_out", hg_w_out[0])
            layer_tail(0)
            for phase, half in (("gm_v", 1), ("gm_u", 0)):
                for k, (t, q) in enumerate(IN_ORDER):
                    load(Numbers(phase), k, unit_src(gm_w_in[0], KU * q, half * D + t * BLOCK))
            second_projection("gm_out", gm_w_out[0])
            layer_tail(1)
            for nb in range(NB):
                sp.wait_ge(h_ready, NB * NORMS["ple_norm1"] + nb + 1)
                sp.dma_start(out[0].rearrange("(t p) d -> p t d", p=P)[:, :, nb * BLOCK:(nb + 1) * BLOCK],
                             h[:, :, nb * BLOCK:(nb + 1) * BLOCK]).then_inc(out_stored, 16)
            sp.wait_ge(out_stored, 16 * NB)

        @block.gpsimd
        def _(pool):
            pool.memset(rows[:], 0.0).then_inc(const_step, 1)
            pool.memset(ident[:], 0.0).then_inc(const_step, 1)
            pool.memset(minus_half[:], -0.5).then_inc(const_step, 1)
            pool.memset(upper[:], 1.0).then_inc(const_step, 1)
            pool.memset(level_mask[:], 1.0).then_inc(const_step, 1)
            pool.wait_ge(const_step, 5)
            pool.affine_select(out=ident[:], in_=ident[:], compare_op=ALU.not_equal, fill=1.0, base=0,
                               pattern=[[-1, P]], channel_multiplier=1).then_inc(const_step, 1)
            pool.affine_select(out=upper[:], in_=upper[:], compare_op=ALU.is_ge, fill=0.0, base=0,
                               pattern=[[1, P]], channel_multiplier=-1).then_inc(const_step, 1)
            for i, seg in enumerate(LEVELS):
                cells = level_mask[:, i, :].rearrange("p (n r) -> p n r", r=seg)
                pool.affine_select(out=cells, in_=cells, compare_op=ALU.is_ge, fill=0.0, base=0,
                                   pattern=[[-2 * seg, P // 2 // seg], [0, seg]],
                                   channel_multiplier=1).then_inc(const_step, 1)
            pool.wait_ge(const_step, 14)
            for i, seg in enumerate(LEVELS):
                cells = level_mask[:, i, :].rearrange("p (n r) -> p n r", r=seg)
                pool.affine_select(out=cells, in_=cells, compare_op=ALU.is_ge, fill=0.0, base=seg - 1,
                                   pattern=[[2 * seg, P // 2 // seg], [0, seg]],
                                   channel_multiplier=-1).then_inc(const_step, 1)

            def power(num, k, dst, n):
                pool.wait_ge(ms_ready, num.of("rstd", k) + 1)
                pool.tensor_tensor(out=dst, in0=ms[:, 0:n], in1=minus_half[:, 0:n], op=ALU.pow) \
                    .then_inc(rstd_ready, 1)

            power(Numbers("start"), 0, r_pre[:], NT)
            with pool.Fori(0, 3) as it:
                power(Numbers("hg_loop", it), 0, r_head[:], NT * HG)
            power(Numbers("hg_out"), 0, r_head[:], NT * HG)

            def layer_tail(layer):
                s = str(layer)
                power(Numbers("mix_norm" + s), 0, r_post[:], NT)
                pool.wait_ge(h_ready, NB * (NORMS["mix_norm" + s] + 1))
                pool.memset(m[:], 0.0).then_inc(m_zeroed, 1)
                power(Numbers("mix_norm" + s), 1, r_pre[:], NT)
                power(Numbers("ffn_norm" + s), 0, r_post[:], NT)
                power(Numbers("ple_norm" + s), 0, r_post[:], NT)

            layer_tail(0)
            power(Numbers("ple_norm0"), 1, r_pre[:], NT)
            power(Numbers("gm_u"), 0, r_head[:, 0:NT], NT)
            layer_tail(1)

        @block.scalar
        def _(act):
            def split(num, k):
                s, r = num.first("unit", k) % STAGES, num.first("unit", k) % RING
                act.wait_ge(w_loaded[s], 16 * num.rounds("unit", k, STAGES))
                if num.first("unit", k) >= RING:
                    act.wait_ge(w_used, num.of("unit", k) + 1 - RING)
                act.activation(w_hi[:, r, :], stage[:, s, :], ACT.Copy).then_inc(w_hi_ready, 1)

            def units(num, ks, steps):
                for k in ks:
                    split(num, k)
                    for step in steps.get(k, ()):
                        step()

            def take(num, task, last_unit, dst, func, scale=1.0):
                act.wait_ge(w_used, num.of("unit", last_unit) + 1)
                pair = num.first("task", task) % 2
                for t in range(NT):
                    i = act.activation(dst[:, t, :], acc[pair][:, t, :], func,
                                       scale=r_pre[:, t:t + 1] if scale is None else scale)
                i.then_inc(acc_read[pair], 1)

            def piece(num, job, hi, scales=None):
                act.wait_ge(job_done, num.of("job", job) + 1)
                src = scr[num.first("job", job) % 2][:, 0, :]
                if scales is None:
                    i = act.activation(hi.rearrange("p k t -> p (k t)"), src, ACT.Copy)
                else:
                    for c in range(KU):
                        i = act.activation(hi[:, c, :], src[:, c * T:(c + 1) * T], ACT.Copy,
                                           scale=scales[:, c:c + 1])
                i.then_inc(piece_hi, 1)

            def square_block(src, sums, nb, done=None):
                act.drain()
                for t in range(NT):
                    i = act.activation(junk[:, t, :], src[:, t, nb * BLOCK:(nb + 1) * BLOCK], ACT.Square,
                                       accum_out=sums[:, t, nb:nb + 1])
                if done is not None:
                    i.then_inc(done, 1)

            def m_squares(num, task, nb):
                act.wait_ge(acc_read[num.first("task", task) % 2], num.rounds("task", task, 2))
                square_block(m, ss, nb, ss_ready)

            def load_gain(vec):
                act.dma_start(gain[:], vec.rearrange("(a n) -> a n", a=1).broadcast_to([P, D])) \
                    .then_inc(gain_loaded, 16)

            def operand(name, nxt, scale_col):
                num, job0 = Numbers(name), 1 if name == "start" else 0
                for blk in range(NB):
                    for pc in (2 * blk, 2 * blk + 1):
                        piece(num, job0 + pc, a_hi[:, KU * pc:KU * pc + KU, :],
                              None if scale_col is None else cols[:, scale_col + KU * pc:scale_col + KU * pc + KU])
                    if scale_col is not None:
                        square_block(h, hss, blk, hss_ready if blk == NB - 1 else None)
                    if blk >= 1:
                        split(nxt, 3 + blk)
                split(nxt, 7)

            act.wait_ge(const_step, 1)
            for r, src in ((C_MIX[0], norm_mix_pre[0]), (C_FFN[0], norm_ffn_pre[0]), (C_MIX[1], norm_mix_pre[1]),
                           (C_FFN[1], norm_ffn_pre[1]), (C_LB, hg_lb_logits[0])):
                act.dma_start(rows[r:r + KT, :], src.rearrange("(k p) -> k p", p=P)).then_inc(rows_loaded, 16)
            act.dma_start(rows[C_BS:C_BS + KT, :], gm_b_s[0]).then_inc(rows_loaded, 16)
            act.dma_start(rows[C_ON:C_ON + 1, :], hg_out_norm).then_inc(rows_loaded, 16)
            load_gain(norm_mix_post[0])
            first = Numbers("hg_first")
            for k in range(4):
                split(first, k)
            act.wait_ge(job_done, 1)
            act.activation(cols[:], scr[0][:, 0, 0:P], ACT.Copy).then_inc(job_read[0], 1)
            act.wait_ge(x_loaded, 16)
            act.wait_ge(job_read[0], 1)
            operand("start", first, C_MIX[0])
            act.wait_ge(lb_step, 1)
            act.activation(lb[:, 1, :], lb[:, 0, :], ACT.Exp).then_inc(lb_step, 1)

            def flat(pair):
                return scr[pair][:].rearrange("p t n -> p (t n)")

            def gates(num, job):
                act.wait_ge(job_done, num.of("job", job) + 1)
                pair = num.first("job", job) % 2
                act.activation(f_g, flat(pair), ACT.Sigmoid)
                act.activation(k_g, flat(pair), ACT.Sigmoid, scale=-1.0).then_inc(job_read[pair], 1)

            def query(num, job):
                act.wait_ge(job_done, num.of("job", job) + 1)
                pair = num.first("job", job) % 2
                act.activation(q_g, flat(pair), ACT.Silu).then_inc(job_read[pair], 1)

            def out_squares(num, job):
                act.wait_ge(job_done, num.of("job", job) + 1)
                act.activation(osq, flat(num.first("job", job) % 2), ACT.Square).then_inc(osq_ready, 1)

            def y_pieces(num, jobs, kt0):
                for c, job in enumerate(jobs):
                    act.wait_ge(job_done, num.of("job", job) + 1)
                    act.activation(y_hi[:, bass.ds(kt0 + KU * c, KU), :].rearrange("p k t -> p (k t)"),
                                   scr[num.first("job", job) % 2][:, 0, :], ACT.Copy,
                                   scale=cols[:, C_ON:C_ON + 1]).then_inc(piece_hi, 1)

            def own_steps(num, zf_job, zq_job):
                return {10: [lambda: take(num, 0, 7, sg, ACT.Copy, None)],
                        15: [lambda: gates(num, zf_job)],
                        18: [lambda: take(num, 1, 15, sg, ACT.Copy, None)],
                        21: [lambda: query(num, zq_job)],
                        26: [lambda: take(num, 2, 23, v_g, ACT.Copy, None)]}

            act.wait_ge(rstd_ready, 1)
            units(first, range(8, 32), own_steps(first, 0, 1))
            with act.Fori(0, 3) as it:
                num = Numbers("hg_loop", it)
                steps = own_steps(num, 6, 8)
                steps[2] = [lambda: take(num, -1, -1, zg, ACT.Silu, None)]
                steps[16] = [lambda: out_squares(num, 7)]
                steps[25] = [lambda: y_pieces(num, (9, 10), it * HG)]
                units(num, range(32), steps)
            out_num = Numbers("hg_out")
            units(out_num, range(32), {
                2: [lambda: take(out_num, -1, -1, zg, ACT.Silu, None)],
                12: [lambda: out_squares(out_num, 6), lambda: y_pieces(out_num, (7, 8), 3 * HG)],
                20: [lambda: m_squares(out_num, 0, 0)], 22: [lambda: m_squares(out_num, 1, 1)],
                29: [lambda: m_squares(out_num, 2, 2)]})

            def layer_tail(layer, out_num):
                s = str(layer)
                first, last, ple = Numbers("ffn_first" + s), Numbers("ffn_last" + s), Numbers("ple" + s)
                for k in range(4):
                    split(first, k)
                m_squares(out_num, 3, 3)
                operand("mix_norm" + s, first, C_FFN[layer])
                act.dma_start(p_tm, p[layer, 0].rearrange("(t p) d -> p t d", p=P)).then_inc(p_loaded, 16)
                act.wait_ge(gain_free, 1 + 3 * layer)
                load_gain(norm_ffn_post[layer])
                act.wait_ge(rstd_ready, Numbers("mix_norm" + s).of("rstd", 1) + 1)
                units(first, range(8, 16), {10: [lambda: take(first, 0, 7, sg, ACT.Silu, None)],
                                            12: [lambda: piece(first, 0, p_hi[:])]})
                with act.Fori(0, HB - 1) as it:
                    body = Numbers("ffn_loop" + s, it)
                    units(body, range(24),
                          {7: [lambda c=c: piece(body, c, y_hi[:, KU * c:KU * c + KU, :]) for c in range(2)],
                           10: [lambda: take(body, 0, 7, sg, ACT.Silu, None)]})

                def take_e(nb):
                    take(last, nb, nb, e[:, :, nb * BLOCK:(nb + 1) * BLOCK], ACT.Copy)
                units(last, range(12),
                      {3: [lambda: take_e(0)], 4: [lambda: take_e(1)],
                       5: [lambda: take_e(2)] + [lambda c=c: piece(last, c, y_hi[:, KU * c:KU * c + KU, :])
                                                 for c in range(2)],
                       6: [lambda: take_e(3)],
                       9: [lambda: m_squares(last, 4, 0)], 11: [lambda: m_squares(last, 5, 1)]})
                units(ple, range(4), {1: [lambda: m_squares(last, 6, 2)], 3: [lambda: m_squares(last, 7, 3)]})
                operand("ffn_norm" + s, ple, None)
                act.wait_ge(gain_free, 2 + 3 * layer)
                load_gain(ple_norm[layer])

                def gate(nb):
                    if nb > 0:
                        act.wait_ge(m_ready, nb + NB * layer)
                    take(ple, nb, 8 * nb + 7, sg, ACT.Sigmoid)

                def gated_squares(nb):
                    act.wait_ge(m_ready, nb + 1 + NB * layer)
                    square_block(m, ss, nb, ss_ready)
                units(ple, range(8, 32), {10: [lambda: gate(0)], 13: [lambda: gated_squares(0)],
                                          18: [lambda: gate(1)], 21: [lambda: gated_squares(1)],
                                          26: [lambda: gate(2)], 29: [lambda: gated_squares(2)]})
                if layer == 0:
                    units(Numbers("gm_v"), range(4), {})
                gate(3)
                gated_squares(3)
                if layer == 0:
                    operand("ple_norm0", Numbers("gm_v"), C_MIX[1])

            layer_tail(0, out_num)

            gv, gu, go = Numbers("gm_v"), Numbers("gm_u"), Numbers("gm_out")
            act.dma_start(ws_raw.rearrange("p (g s) -> p g s", g=KT), gm_w_s[0].rearrange("g t s -> t g s")) \
                .then_inc(ws_loaded, 16)
            act.wait_ge(gain_free, 3)
            load_gain(gm_ln_g[0])
            act.wait_ge(rstd_ready, Numbers("ple_norm0").of("rstd", 1) + 1)

            def take_v(num, task, last_unit, nb):
                take(num, task, last_unit, m[:, :, nb * BLOCK:(nb + 1) * BLOCK], ACT.Gelu, None)

            def load_ln_b():
                act.wait_ge(job_read[gv.first("job", 3) % 2], gv.rounds("job", 3, 2))
                act.dma_start(ln_b, gm_ln_b[0].rearrange("(a n) -> a n", a=1).broadcast_to([P, D])) \
                    .then_inc(ln_b_loaded, 16)

            def take_u(num, task, last_unit, nb):
                if nb > 0:
                    job = 3 * (nb - 1)
                    act.wait_ge(job_read[gu.first("job", job) % 2], gu.rounds("job", job, 2))
                take(num, task, last_unit, sg, ACT.Gelu, None)

            def gm_pieces(num, jobs, nb):
                for c, job in enumerate(jobs):
                    piece(num, job, y_hi[:, GC * nb + KU * c:GC * nb + KU * c + KU, :])

            def load_gain_mix1():
                act.wait_ge(ln_ready, NB)
                load_gain(norm_mix_post[1])
            units(gv, range(8, 32), {10: [lambda: take_v(gv, 0, 7, 0)], 18: [lambda: take_v(gv, 1, 15, 1)],
                                     20: [load_ln_b], 26: [lambda: take_v(gv, 2, 23, 2)]})
            units(gu, range(32), {2: [lambda: take_v(gu, -1, -1, 3)],
                                  10: [lambda: take_u(gu, 0, 7, 0)], 15: [lambda: gm_pieces(gu, (1, 2), 0)],
                                  17: [load_gain_mix1],
                                  18: [lambda: take_u(gu, 1, 15, 1)], 23: [lambda: gm_pieces(gu, (4, 5), 1)],
                                  26: [lambda: take_u(gu, 2, 23, 2)], 31: [lambda: gm_pieces(gu, (7, 8), 2)]})
            units(go, range(32), {2: [lambda: take_u(go, -1, -1, 3)], 7: [lambda: gm_pieces(go, (1, 2), 3)],
                                  20: [lambda: m_squares(go, 0, 0)], 22: [lambda: m_squares(go, 1, 1)],
                                  29: [lambda: m_squares(go, 2, 2)]})
            layer_tail(1, go)

        @block.vector
        def _(dve):
            def split(num, k):
                s, r = num.first("unit", k) % STAGES, num.first("unit", k) % RING
                dve.wait_ge(w_hi_ready, num.of("unit", k) + 1)
                dve.tensor_tensor(out=w_lo[:, r, :], in0=stage[:, s, :], in1=w_hi[:, r, :].bitcast(f32),
                                  op=ALU.subtract).then_inc(w_lo_ready, 1)

            def units(num, ks, steps):
                for k in ks:
                    split(num, k)
                    for step in steps.get(k, ()):
                        step()

            def piece(num, nth, job, hi, lo, scales=None):
                dve.wait_ge(piece_hi, num.of("piece", nth) + 1)
                pair = num.first("job", job) % 2
                src = scr[pair][:, 0, :]
                if scales is None:
                    i = dve.tensor_tensor(out=lo.rearrange("p k t -> p (k t)"), in0=src,
                                          in1=hi.rearrange("p k t -> p (k t)").bitcast(f32), op=ALU.subtract)
                else:
                    for c in range(KU):
                        i = dve.scalar_tensor_tensor(out=lo[:, c, :], in0=src[:, c * T:(c + 1) * T],
                                                     scalar=scales[:, c:c + 1], in1=hi[:, c, :].bitcast(f32),
                                                     op0=ALU.mult, op1=ALU.subtract)
                i.then_inc(job_read[pair], 1)

            def mean_squares(sums, n, count):
                dve.tensor_reduce(ms[:, 0:n], sums, AX.X, ALU.add)
                dve.drain()
                dve.tensor_scalar(ms[:, 0:n], ms[:, 0:n], 1.0 / count, EPS, ALU.mult, ALU.add).then_inc(ms_ready, 1)

            def operand(name, nxt, scale_col, update):
                num, job0 = Numbers(name), 1 if name == "start" else 0
                update(0)
                for blk in range(NB):
                    if blk + 1 < NB:
                        update(blk + 1)
                    for pc in (2 * blk, 2 * blk + 1):
                        piece(num, pc, job0 + pc, a_hi[:, KU * pc:KU * pc + KU, :], a_lo[:, KU * pc:KU * pc + KU, :],
                              None if scale_col is None else cols[:, scale_col + KU * pc:scale_col + KU * pc + KU])
                    if blk >= 1:
                        split(nxt, 3 + blk)
                split(nxt, 7)
                if scale_col is not None:
                    dve.wait_ge(hss_ready, PRE_NORMS[name] + 1)
                    mean_squares(hss[:], NT, D)

            def gain_of(nb):
                return gain[:, nb * BLOCK:(nb + 1) * BLOCK].unsqueeze(1).broadcast_to([P, NT, BLOCK])

            def blk_of(x_, nb):
                return x_[:, :, nb * BLOCK:(nb + 1) * BLOCK]

            def times_gain(norm, nb):
                if nb < NB - 1:
                    dve.wait_ge(ss_ready, NB * NORMS[norm] + nb + 1)
                which = norm.replace("_norm", "")
                dve.wait_ge(gain_loaded, 16 * (GAINS[which] + 1))
                i = dve.tensor_tensor(out=blk_of(m, nb) if nb < NB - 1 else hid[:], in0=blk_of(m, nb),
                                      in1=gain_of(nb), op=ALU.mult)
                if nb == NB - 1:
                    i.then_inc(gain_free, 1)

            def norm_factor(norm):
                dve.wait_ge(ss_ready, NB * NORMS[norm] + NB)
                mean_squares(ss[:], NT, D)
                dve.wait_ge(rstd_ready, Numbers(norm).of("rstd", 0) + 1)

            def add_block(nb):
                for t in range(NT):
                    cs = slice(nb * BLOCK, (nb + 1) * BLOCK)
                    i = dve.scalar_tensor_tensor(out=h[:, t, cs], in0=m[:, t, cs] if nb < NB - 1 else hid[:, t, :],
                                                 scalar=r_post[:, t:t + 1], in1=h[:, t, cs],
                                                 op0=ALU.mult, op1=ALU.add)
                i.then_inc(h_ready, 1)

            def take_m(num, task, last_unit, nb, add=False):
                dve.wait_ge(w_used, num.of("unit", last_unit) + 1)
                pair = num.first("task", task) % 2
                if add:
                    i = dve.tensor_tensor(out=blk_of(m, nb), in0=acc[pair][:], in1=blk_of(m, nb), op=ALU.add)
                else:
                    i = dve.tensor_copy(blk_of(m, nb), acc[pair][:])
                i.then_inc(acc_read[pair], 1)

            first = Numbers("hg_first")
            units(first, range(4), {})
            dve.wait_ge(job_read[0], 1)
            logits = cols[:, C_LB:C_LB + KT]
            dve.tensor_tensor(out=lb[:, 0, :], in0=logits, in1=logits, op=ALU.subtract).then_inc(lb_step, 1)
            operand("start", first, C_MIX[0], lambda nb: None)
            dve.wait_ge(lb_step, 2)
            dve.reciprocal(lb[:, 2, :], lb[:, 1, :])
            dve.drain()
            dve.tensor_tensor(out=lb[:, 3, :], in0=lb[:, 1, :], in1=lb[:, 2, :], op=ALU.mult)
            dve.drain()
            dve.tensor_tensor(out=lb[:, 4, :], in0=lb[:, 3, :], in1=lb[:, 3, :], op=ALU.subtract)
            dve.drain()
            lb_low, lb_rest = lb[:, 5, :], lb[:, 0, :]
            dve.tensor_scalar(lb_low, lb[:, 4, :], LB_FLOOR, None, ALU.max)
            dve.tensor_scalar(lb_rest, lb[:, 4, :], -1.0, 1.0, ALU.mult, ALU.add)
            dve.drain()

            TOT = {1: f_g}
            at = 0
            for seg in LEVELS[1:]:
                n = HG * T // seg
                TOT[seg] = tot[:, at:at + n]
                at += n

            def fk(num, zf_job, group):
                dve.wait_ge(job_read[num.first("job", zf_job) % 2], num.rounds("job", zf_job, 2))
                for hd in range(HG):
                    col = bass.ds(group * HG + hd, 1)
                    dve.tensor_scalar(f_g[:, hd * T:(hd + 1) * T], f_g[:, hd * T:(hd + 1) * T],
                                      lb_rest[:, col], lb_low[:, col], ALU.mult, ALU.add)
                for hd in range(HG):
                    col = bass.ds(group * HG + hd, 1)
                    i = dve.tensor_scalar(k_g[:, hd * T:(hd + 1) * T], k_g[:, hd * T:(hd + 1) * T],
                                          lb_rest[:, col], None, ALU.mult)
                i.then_inc(kq_ready, 1)

            def totals():
                for seg in LEVELS[1:]:
                    dve.drain()
                    halves = TOT[seg // 2].rearrange("p (n two) -> p n two", two=2)
                    dve.tensor_tensor(out=TOT[seg], in0=halves[:, :, 0], in1=halves[:, :, 1], op=ALU.mult)

            def diagonal(num, job):
                dve.wait_ge(job_done, num.of("job", job) + 1)
                pair = num.first("job", job) % 2
                dve.tensor_tensor(out=q_g, in0=q_g, in1=f_g, op=ALU.mult).then_inc(kq_ready, 1)
                b = NT * HG
                dve.tensor_tensor(out=att.rearrange("p (b t) -> p b t", b=b),
                                  in0=scr[pair][:].rearrange("p two (b t) -> p (two b) t", t=P),
                                  in1=ident[:].unsqueeze(1).broadcast_to([P, b, P]), op=ALU.mult) \
                    .then_inc(job_read[pair], 1)

            def level(num, lev, job):
                seg = LEVELS[lev]
                pair = num.first("job", job) % 2
                dve.wait_ge(job_done, num.of("job", job) + 1)
                dve.wait_ge(job_read[1 - pair], num.rounds("job", job - 1, 2))
                q2 = q_g.rearrange("p (n two r) -> p n two r", two=2, r=seg)
                k2 = k_g.rearrange("p (n two r) -> p n two r", two=2, r=seg)
                t2 = TOT[seg].rearrange("p (n two) -> p n two", two=2)
                n = HG * T // (2 * seg)
                dve.tensor_tensor(out=q2[:, :, 1, :], in0=q2[:, :, 1, :],
                                  in1=t2[:, :, 0].unsqueeze(2).broadcast_to([P, n, seg]), op=ALU.mult)
                dve.tensor_tensor(out=k2[:, :, 0, :], in0=k2[:, :, 0, :],
                                  in1=t2[:, :, 1].unsqueeze(2).broadcast_to([P, n, seg]), op=ALU.mult) \
                    .then_inc(kq_ready, 1)
                b, ns = NT * HG, P // 2 // seg
                dve.copy_predicated(
                    att.rearrange("p (b n two r) -> p b n two r", b=b, two=2, r=seg)[:, :, :, 1, :],
                    level_mask[:, lev, :].bitcast(i32).rearrange("p (n r) -> p n r", r=seg)
                    .unsqueeze(1).broadcast_to([P, b, ns, seg]),
                    scr[pair][:, 0, :].rearrange("p (b n r) -> p b n r", b=b, r=seg)).then_inc(job_read[pair], 1)

            def cross(num, job):
                dve.wait_ge(job_done, num.of("job", job) + 1)
                pair = num.first("job", job) % 2
                dve.tensor_copy(att_x, scr[pair][:, 0, :]).then_inc(job_read[pair], 1)

            def head_mean_squares(num):
                dve.wait_ge(osq_ready, num.of("grp", 0) + 1)
                mean_squares(osq.rearrange("p (b v) -> p b v", b=NT * HG), NT * HG, HD)

            def head_outputs(num, job):
                dve.wait_ge(rstd_ready, num.of("rstd", 0) + 1)
                pair = num.first("job", job) % 2
                dve.tensor_tensor(out=hid[:].rearrange("p c (h v) -> p h c v", h=HG),
                                  in0=scr[pair][:].rearrange("p two (h c v) -> p (two h) c v", c=NT, v=HD),
                                  in1=r_head[:].rearrange("p (h c) -> p h c", c=NT).unsqueeze(3)
                                  .broadcast_to([P, HG, NT, HD]), op=ALU.mult).then_inc(job_read[pair], 1)
                dve.drain()
                dve.tensor_tensor(out=hid[:], in0=hid[:], in1=zg[:], op=ALU.mult).then_inc(hid_ready, 1)

            def y_pieces(num, jobs, kt0):
                for c, job in enumerate(jobs):
                    dve.wait_ge(piece_hi, num.of("piece", c) + 1)
                    pair = num.first("job", job) % 2
                    kts = bass.ds(kt0 + KU * c, KU)
                    dve.scalar_tensor_tensor(out=y_lo[:, kts, :].rearrange("p k t -> p (k t)"),
                                             in0=scr[pair][:, 0, :], scalar=cols[:, C_ON:C_ON + 1],
                                             in1=y_hi[:, kts, :].bitcast(f32).rearrange("p k t -> p (k t)"),
                                             op0=ALU.mult, op1=ALU.subtract).then_inc(job_read[pair], 1)

            def own_steps(num, group, zf_job, diag_job):
                return {17: [lambda: fk(num, zf_job, group)], 19: [totals],
                        28: [lambda: diagonal(num, diag_job)],
                        30: [lambda: level(num, 0, diag_job + 1)]}

            units(first, range(8, 32), own_steps(first, 0, 0, 2))
            with dve.Fori(0, 3) as it:
                num = Numbers("hg_loop", it)
                steps = own_steps(num, it + 1, 6, 11)
                for lev in range(1, len(LEVELS)):
                    steps[2 * lev - 2] = [lambda lev=lev: level(num, lev, lev - 2)]
                steps[12] = [lambda: cross(num, 5)]
                steps[16] = [lambda: head_mean_squares(num)]
                steps[18] = [lambda: head_outputs(num, 7)]
                steps[25] = [lambda: y_pieces(num, (9, 10), it * HG)]
                units(num, range(32), steps)
            out_num = Numbers("hg_out")
            steps = {2 * lev - 2: [lambda lev=lev: level(out_num, lev, lev - 2)] for lev in range(1, len(LEVELS))}
            steps[11] = [lambda: cross(out_num, 5)]
            steps[12] = [lambda: head_mean_squares(out_num), lambda: head_outputs(out_num, 6),
                         lambda: y_pieces(out_num, (7, 8), 3 * HG)]

            def out_steps(num, norm):
                return {16: [lambda: take_m(num, 0, 13, 0)], 18: [lambda: take_m(num, 1, 15, 1)],
                        22: [lambda: times_gain(norm, 0)], 24: [lambda: times_gain(norm, 1)],
                        26: [lambda: take_m(num, 2, 23, 2)], 31: [lambda: times_gain(norm, 2)]}
            steps.update(out_steps(out_num, "mix_norm0"))
            units(out_num, range(32), steps)

            def layer_tail(layer, out_num):
                s = str(layer)
                first, last, ple = Numbers("ffn_first" + s), Numbers("ffn_last" + s), Numbers("ple" + s)
                units(first, range(4), {})
                take_m(out_num, 3, 31, 3)
                dve.drain()
                times_gain("mix_norm" + s, 3)
                norm_factor("mix_norm" + s)
                operand("mix_norm" + s, first, C_FFN[layer], add_block)
                units(first, range(8, 16), {12: [lambda: piece(first, 0, 0, p_hi[:], p_lo[:])]})

                def hidden(num):
                    dve.wait_ge(w_used, num.of("unit", 0))
                    pair = num.first("task", -1) % 2
                    for t in range(NT):
                        i = dve.scalar_tensor_tensor(out=hid[:, t, :], in0=acc[pair][:, t, :],
                                                     scalar=r_pre[:, t:t + 1], in1=sg[:, t, :],
                                                     op0=ALU.mult, op1=ALU.mult)
                    i.then_inc(acc_read[pair], 1)

                def hid_pieces(num):
                    for c in range(2):
                        piece(num, c, c, y_hi[:, KU * c:KU * c + KU, :], y_lo[:, KU * c:KU * c + KU, :])

                dve.wait_ge(m_zeroed, layer + 1)
                with dve.Fori(0, HB - 1) as it:
                    body = Numbers("ffn_loop" + s, it)
                    units(body, range(24),
                          {2: [lambda: hidden(body)], 7: [lambda: hid_pieces(body)]}
                          | {12 + 2 * nb: [lambda nb=nb: take_m(body, 1 + nb, 9 + 2 * nb, nb, True)]
                             for nb in range(NB)})
                norm = "ffn_norm" + s
                units(last, range(12), {2: [lambda: hidden(last)], 5: [lambda: hid_pieces(last)],
                                        8: [lambda: take_m(last, 4, 5, 0, True)],
                                        10: [lambda: take_m(last, 5, 7, 1, True)],
                                        11: [lambda: times_gain(norm, 0)]})
                units(ple, range(4), {0: [lambda: take_m(last, 6, 9, 2, True)],
                                      2: [lambda: times_gain(norm, 1)],
                                      3: [lambda: times_gain(norm, 2), lambda: take_m(last, 7, 11, 3, True)]})
                dve.drain()
                times_gain(norm, 3)
                norm_factor(norm)
                operand(norm, ple, None, add_block)
                norm = "ple_norm" + s

                def gated(nb):
                    pair = ple.first("task", nb) % 2
                    dve.wait_ge(acc_read[pair], ple.rounds("task", nb, 2))
                    dve.tensor_tensor(out=blk_of(m, nb), in0=blk_of(e, nb), in1=sg[:], op=ALU.mult) \
                        .then_inc(m_ready, 1)
                units(ple, range(8, 32), {11: [lambda: gated(0)], 15: [lambda: times_gain(norm, 0)],
                                          19: [lambda: gated(1)], 23: [lambda: times_gain(norm, 1)],
                                          27: [lambda: gated(2)], 31: [lambda: times_gain(norm, 2)]})
                if layer == 0:
                    units(Numbers("gm_v"), range(4), {})
                gated(3)
                dve.drain()
                times_gain(norm, 3)
                norm_factor(norm)
                if layer == 0:
                    operand(norm, Numbers("gm_v"), C_MIX[1], add_block)
                else:
                    for nb in range(NB):
                        add_block(nb)

            layer_tail(0, out_num)

            gv, gu, go = Numbers("gm_v"), Numbers("gm_u"), Numbers("gm_out")

            def v_stats(num, task, nb):
                pair = num.first("task", task) % 2
                dve.wait_ge(acc_read[pair], num.rounds("task", task, 2))
                for t in range(NT):
                    dve.bn_stats(bn[:, t, nb, :], m[:, t, nb * BLOCK:(nb + 1) * BLOCK])

            def spatial_weights(job):
                dve.wait_ge(job_done, gv.of("job", job) + 1)
                pair = gv.first("job", job) % 2
                dve.tensor_tensor(out=wsT[:, job * BLOCK:(job + 1) * BLOCK].rearrange("p (g t) -> p g t", t=P),
                                  in0=scr[pair][:, 0, :].rearrange("p (g t) -> p g t", t=P),
                                  in1=upper[:].unsqueeze(1).broadcast_to([P, GC, P]), op=ALU.mult) \
                    .then_inc(job_read[pair], 1)

            def v_factor():
                dve.drain()
                for t in range(NT):
                    dve.bn_aggr(mv[:, t, :], bn[:, t, :, :].rearrange("p a b -> p (a b)"))
                dve.drain()
                dve.tensor_scalar(ms[:, 0:NT], mv[:, :, 1], EPS, None, ALU.add).then_inc(ms_ready, 1)

            def layer_norm(nb):
                if nb == 0:
                    dve.wait_ge(rstd_ready, gu.of("rstd", 0) + 1)
                    dve.wait_ge(gain_loaded, 16 * (GAINS["ln"] + 1))
                    dve.wait_ge(ln_b_loaded, 16)
                for t in range(NT):
                    cs = slice(nb * BLOCK, (nb + 1) * BLOCK)
                    dve.tensor_scalar(m[:, t, cs], m[:, t, cs], mv[:, t, 0:1], r_head[:, t:t + 1],
                                      ALU.subtract, ALU.mult)
                dve.drain()
                dve.tensor_tensor(out=blk_of(m, nb), in0=blk_of(m, nb), in1=gain_of(nb), op=ALU.mult)
                dve.drain()
                dve.tensor_tensor(out=blk_of(m, nb), in0=blk_of(m, nb),
                                  in1=ln_b[:, nb * BLOCK:(nb + 1) * BLOCK].unsqueeze(1).broadcast_to([P, NT, BLOCK]),
                                  op=ALU.add).then_inc(ln_ready, 1)

            def gm_outputs(num, task, job, nb):
                dve.wait_ge(acc_read[num.first("task", task) % 2], num.rounds("task", task, 2))
                dve.wait_ge(job_done, num.of("job", job) + 1)
                pair = num.first("job", job) % 2
                for g in range(GC):
                    cs = slice(g * P, (g + 1) * P)
                    i = dve.scalar_tensor_tensor(out=hid[:, :, cs], in0=scr[pair][:, :, cs],
                                                 scalar=cols[:, C_BS + GC * nb + g:C_BS + GC * nb + g + 1],
                                                 in1=sg[:, :, cs], op0=ALU.add, op1=ALU.mult)
                i.then_inc(job_read[pair], 1)

            def gm_pieces(num, nth, jobs, nb):
                for c, job in enumerate(jobs):
                    kts = slice(GC * nb + KU * c, GC * nb + KU * c + KU)
                    piece(num, nth + c, job, y_hi[:, kts, :], y_lo[:, kts, :])

            units(gv, range(8, 32), {11: [lambda: v_stats(gv, 0, 0)], 19: [lambda: v_stats(gv, 1, 1)],
                                     27: [lambda: v_stats(gv, 2, 2)]}
                  | {14 + j: [lambda j=j: spatial_weights(j)] for j in range(NB)})
            units(gu, range(32), {3: [lambda: v_stats(gu, -1, 3), v_factor], 4: [lambda: layer_norm(0)],
                                  6: [lambda: layer_norm(1)], 9: [lambda: layer_norm(2)],
                                  13: [lambda: layer_norm(3)],
                                  11: [lambda: gm_outputs(gu, 0, 0, 0)], 15: [lambda: gm_pieces(gu, 0, (1, 2), 0)],
                                  19: [lambda: gm_outputs(gu, 1, 3, 1)], 23: [lambda: gm_pieces(gu, 2, (4, 5), 1)],
                                  27: [lambda: gm_outputs(gu, 2, 6, 2)], 31: [lambda: gm_pieces(gu, 4, (7, 8), 2)]})
            units(go, range(32), {3: [lambda: gm_outputs(go, -1, 0, 3)], 7: [lambda: gm_pieces(go, 0, (1, 2), 3)]}
                  | out_steps(go, "mix_norm1"))
            layer_tail(1, go)

        @block.tensor
        def _(pe):
            def unit(num, k, task, x_hi, x_lo, kt, is_first, is_last):
                pair = num.first("task", task) % 2
                if is_first and num.first("task", task) >= 2:
                    pe.wait_ge(acc_read[pair], num.rounds("task", task, 2) - 1)
                pe.wait_ge(w_lo_ready, num.of("unit", k) + 1)
                r = num.first("unit", k) % RING
                for c in range(KU):
                    wh, wl = (w[:, r, c * BLOCK:(c + 1) * BLOCK] for w in (w_hi, w_lo))
                    for t in range(NT):
                        ts = slice(t * P, (t + 1) * P)
                        xh, xl = x_hi[:, kt + c, ts], x_lo[:, kt + c, ts]
                        for n, (a, b) in enumerate(((xh, wl), (xh, wh), (xl, wh))):
                            i = pe.matmul(acc[pair][:, t, :], a, b, start=is_first and c == 0 and n == 0,
                                          stop=is_last and c == KU - 1 and n == 2)
                i.then_inc(w_used, 1)

            def in_unit(num, k, x_hi=a_hi, x_lo=a_lo, unit0=0, task0=0):
                t, q = k // 8, k % 8
                unit(num, unit0 + k, task0 + t, x_hi, x_lo, KU * q, q == 0, q == 7)

            def job_begin(num, job):
                pair = num.first("job", job) % 2
                if num.first("job", job) >= 2:
                    pe.wait_ge(job_read[pair], num.rounds("job", job, 2) - 1)
                return scr[pair]

            def transpose_piece(num, job, src):
                s = job_begin(num, job)
                for c in range(KU):
                    for t in range(NT):
                        i = pe.transpose(s[:, 0, c * T + t * P:c * T + (t + 1) * P], src(c, t), ident[:])
                i.then_inc(job_done, 1)

            def operand(name, nxt):
                num, job0 = Numbers(name), 1 if name == "start" else 0

                def transpose(pc):
                    if name != "start":
                        pe.wait_ge(h_ready, NB * NORMS[name] + pc // 2 + 1)
                    transpose_piece(num, job0 + pc,
                                    lambda c, t: h[:, t, (KU * pc + c) * P:(KU * pc + c + 1) * P])
                transpose(0)
                for pc in range(8):
                    if pc < 7:
                        transpose(pc + 1)
                    piece_ready(num, job0 + pc)
                    in_unit(nxt, pc)

            def piece_ready(num, job):
                pe.wait_ge(job_read[num.first("job", job) % 2], num.rounds("job", job, 2))

            pe.wait_ge(const_step, 6)
            pe.wait_ge(rows_loaded, 16 * 7)
            pe.transpose(scr[0][:, 0, 0:P], rows[:], ident[:]).then_inc(job_done, 1)
            pe.wait_ge(x_loaded, 16)
            first = Numbers("hg_first")
            operand("start", first)

            B = NT * HG

            def transpose_group(num, job, task):
                pair = num.first("task", task) % 2
                pe.wait_ge(acc_read[pair], num.rounds("task", task, 2))
                s = job_begin(num, job)
                for hd in range(HG):
                    for t in range(NT):
                        col = hd * T + t * P
                        i = pe.transpose(s[:, col // BLOCK, col % BLOCK:col % BLOCK + P],
                                         sg[:, t, hd * P:(hd + 1) * P], ident[:])
                i.then_inc(job_done, 1)

            def kq_wait(num, nth):
                pe.wait_ge(kq_ready, num.of("kq", nth) + 1)

            def diagonal(num, job, zq_job, kq):
                kq_wait(num, kq)
                pe.wait_ge(job_read[num.first("job", zq_job) % 2], num.rounds("job", zq_job, 2))
                s = job_begin(num, job)
                for b in range(B):
                    cs = slice(b * P, (b + 1) * P)
                    i = pe.matmul(s[:, b // HG, b % HG * P:(b % HG + 1) * P], k_g[:, cs], q_g[:, cs],
                                  start=True, stop=True)
                i.then_inc(job_done, 1)

            def level(num, lev, job, kq):
                kq_wait(num, kq)
                s = job_begin(num, job)
                seg = LEVELS[lev]
                for b in range(B):
                    odd = q_g[:, b * P:(b + 1) * P].rearrange("p (n two r) -> p n two r", two=2, r=seg)[:, :, 1, :]
                    i = pe.matmul(s[:, 0, b * P // 2:(b + 1) * P // 2], k_g[:, b * P:(b + 1) * P], odd,
                                  start=True, stop=True)
                i.then_inc(job_done, 1)

            def cross(num, job, kq):
                kq_wait(num, kq)
                s = job_begin(num, job)
                for hd in range(HG):
                    i = pe.matmul(s[:, 0, hd * P:(hd + 1) * P], k_g[:, hd * T:hd * T + P],
                                  q_g[:, hd * T + P:(hd + 1) * T], start=True, stop=True)
                i.then_inc(job_done, 1)

            def outputs(num, job, cross_job):
                pe.wait_ge(job_read[num.first("job", cross_job) % 2], num.rounds("job", cross_job, 2))
                s = job_begin(num, job)
                for hd in range(HG):
                    v0, v1 = (v_g[:, t, hd * P:(hd + 1) * P] for t in range(NT))
                    for t in range(NT):
                        b = NT * hd + t
                        dst = s[:, b // HG, b % HG * P:(b % HG + 1) * P]
                        i = pe.matmul(dst, att[:, b * P:(b + 1) * P], (v0, v1)[t], start=True, stop=t == 0)
                        if t == 1:
                            i = pe.matmul(dst, att_x[:, hd * P:(hd + 1) * P], v0, start=False, stop=True)
                i.then_inc(job_done, 1)

            def group_transposes(num, jobs):
                pe.wait_ge(hid_ready, num.of("grp", 0) + 1)
                for c2, job in enumerate(jobs):
                    transpose_piece(num, job, lambda c, t: hid[:, t, (KU * c2 + c) * P:(KU * c2 + c + 1) * P])

            def own_steps(num, zf, zq, diag, kq):
                return {11: [lambda: transpose_group(num, zf, 0)], 17: [lambda: transpose_group(num, zq, 1)],
                        26: [lambda: diagonal(num, diag, zq, kq)], 28: [lambda: level(num, 0, diag + 1, kq + 1)],
                        30: [lambda: level(num, 1, diag + 2, kq + 2)]}

            def in_units(num, ks, steps, **kw):
                for k in ks:
                    in_unit(num, k, **kw)
                    for step in steps.get(k, ()):
                        step()

            def out_units(num, steps, ready):
                for k, (t, q) in enumerate(OUT_ORDER):
                    if q in (6, 7) and t == 0:
                        piece_ready(num, ready[q - 6])
                    unit(num, k, t, y_hi, y_lo, KU * q, q == 0, q == 7)
                    for step in steps.get(k, ()):
                        step()

            in_units(first, range(8, 32), own_steps(first, 0, 1, 2, 0))
            with pe.Fori(0, 3) as it:
                num = Numbers("hg_loop", it)
                steps = own_steps(num, 6, 8, 11, 6)
                for lev in range(2, len(LEVELS)):
                    steps[2 * lev - 4] = [lambda lev=lev: level(num, lev, lev - 2, lev - 2)]
                steps[10] = [lambda: cross(num, 5, 5)]
                steps[13] = [lambda: outputs(num, 7, 5)]
                steps[22] = [lambda: group_transposes(num, (9, 10))]
                in_units(num, range(32), steps)
            num = Numbers("hg_out")
            steps = {2 * lev - 4: [lambda lev=lev: level(num, lev, lev - 2, lev - 2)]
                     for lev in range(2, len(LEVELS))}
            steps[10] = [lambda: cross(num, 5, 5)]
            steps[11] = [lambda: outputs(num, 6, 5), lambda: group_transposes(num, (7, 8))]
            out_units(num, steps, (7, 8))

            def layer_tail(layer):
                s = str(layer)
                first, last, ple = Numbers("ffn_first" + s), Numbers("ffn_last" + s), Numbers("ple" + s)
                operand("mix_norm" + s, first)

                def p_transposes():
                    pe.wait_ge(p_loaded, 16 * (layer + 1))
                    transpose_piece(first, 0, lambda c, t: p_tm[:, t, c * P:(c + 1) * P])
                in_units(first, range(8, 16), {9: [p_transposes]})

                def hid_transposes(num):
                    pair = num.first("task", -1) % 2
                    pe.wait_ge(acc_read[pair], num.rounds("task", -1, 2))
                    for c2 in range(2):
                        transpose_piece(num, c2, lambda c, t: hid[:, t, (KU * c2 + c) * P:(KU * c2 + c + 1) * P])

                def down(num, unit0, task0):
                    for job in range(2):
                        piece_ready(num, job)
                    for nb in range(NB):
                        for q in range(2):
                            unit(num, unit0 + 2 * nb + q, task0 + nb, y_hi, y_lo, KU * q, q == 0, q == 1)

                with pe.Fori(0, HB - 1) as it:
                    body = Numbers("ffn_loop" + s, it)
                    in_units(body, range(8), {4: [lambda: hid_transposes(body)]})
                    down(body, 8, 1)
                    in_units(body, range(8), {}, unit0=16, task0=5)
                piece_ready(first, 0)
                for nb in range(NB):
                    unit(last, nb, nb, p_hi, p_lo, 0, True, True)
                hid_transposes(last)
                down(last, 4, 4)
                operand("ffn_norm" + s, ple)
                in_units(ple, range(8, 32), {})

            layer_tail(0)

            gv, gu, go = Numbers("gm_v"), Numbers("gm_u"), Numbers("gm_out")
            operand("ple_norm0", gv)

            def ws_transposes(job):
                pe.wait_ge(ws_loaded, 16)
                s = job_begin(gv, job)
                for g in range(GC):
                    cs = slice((GC * job + g) * P, (GC * job + g + 1) * P)
                    i = pe.transpose(s[:, 0, g * P:(g + 1) * P], ws_raw[:, cs], ident[:])
                i.then_inc(job_done, 1)

            def spatial(num, job, nb):
                pe.wait_ge(ln_ready, nb + 1)
                s = job_begin(num, job)
                for g in range(GC):
                    cs = slice((GC * nb + g) * P, (GC * nb + g + 1) * P)
                    for t in range(NT):
                        i = pe.matmul(s[:, t, g * P:(g + 1) * P], wsT[:, cs], m[:, t, cs], start=True, stop=True)
                i.then_inc(job_done, 1)

            def gm_transposes(num, sv_job):
                piece_ready(num, sv_job)
                for c2 in range(2):
                    transpose_piece(num, sv_job + 1 + c2,
                                    lambda c, t: hid[:, t, (KU * c2 + c) * P:(KU * c2 + c + 1) * P])
            in_units(gv, range(8, 32), {12 + j: [lambda j=j: ws_transposes(j)] for j in range(NB)})
            in_units(gu, range(32), {8: [lambda: spatial(gu, 0, 0)], 12: [lambda: gm_transposes(gu, 0)],
                                     16: [lambda: spatial(gu, 3, 1)], 20: [lambda: gm_transposes(gu, 3)],
                                     24: [lambda: spatial(gu, 6, 2)], 28: [lambda: gm_transposes(gu, 6)]})
            out_units(go, {0: [lambda: spatial(go, 0, 3)], 4: [lambda: gm_transposes(go, 0)]}, (1, 2))
            layer_tail(1)


_INS = ["x", "p", "hg_w_in", "hg_lb_logits", "hg_out_norm", "hg_w_out", "gm_w_in", "gm_ln_g", "gm_ln_b",
        "gm_w_s", "gm_b_s", "gm_w_out", "norm_mix_pre", "norm_mix_post", "norm_ffn_pre", "norm_ffn_post",
        "ffn_w_gate", "ffn_w_up", "ffn_w_down", "ple_w_proj", "ple_w_gate", "ple_norm"]


def kernel(**inputs):
    import numpy as np
    import concourse.bacc as bacc
    from concourse.bass_utils import run_bass_kernel_spmd

    nc = bacc.Bacc("TRN2", target_bir_lowering=False, num_devices=1)
    arrays, args = {}, []
    for name in _INS:
        a = np.ascontiguousarray(inputs[name])
        arrays[f"in_{name}"] = a
        args.append(nc.dram_tensor(f"in_{name}", a.shape, mybir.dt.from_np(a.dtype), kind="ExternalInput").ap())
    shape = inputs["x"].shape
    args.append(nc.dram_tensor("out_h", shape, mybir.dt.float32, kind="ExternalOutput").ap())
    trunk(nc, *args)
    r = run_bass_kernel_spmd(nc, [arrays], core_ids=[0])
    return r.results[0]["out_h"]
```

```python
import concourse.bass as bass
from concourse import mybir
from contextlib import ExitStack

P = 128
STAGES = 8
RING = 4
BLOCK = 512
KU = 2


KINDS = ("unit", "task", "job", "piece", "rstd", "kq", "grp")


def plan(phases):
    at, count = {}, dict.fromkeys(KINDS, 0)
    for name, times, *sizes in phases:
        at[name] = dict(count)
        for key, n in zip(KINDS, sizes):
            count[key] += times * n
    return at


def layer_tail_phases(layer):
    return [(name + str(layer), *sizes) for name, *sizes in (
        ("mix_norm", 1, 2, 2, 8, 8, 2),
        ("ffn_first", 1, 16, 2),
        ("ffn_loop", 9, 24, 6, 2, 2),
        ("ffn_last", 1, 32, 6, 4, 4),
        ("ffn_norm", 1, 2, 2, 8, 8, 1),
        ("ple", 1, 32, 4))]


PHASES = [
    ("start", 1, 0, 0, 9, 8, 1),
    ("hg_first", 1, 32, 4, 5, 0, 0, 3, 0),
    ("hg_loop", 3, 32, 4, 14, 2, 1, 9, 1),
    ("hg_out", 1, 32, 4, 10, 3, 1, 6, 1),
    *layer_tail_phases(0),
    ("ple_norm0", 1, 0, 0, 8, 8, 2),
    ("gm_v", 1, 32, 4, 4),
    ("gm_u", 1, 32, 4, 9, 6, 1),
    ("gm_out", 1, 32, 4, 4, 3),
    *layer_tail_phases(1),
    ("ple_norm1", 1, 0, 0, 0, 0, 1),
]
AT = plan(PHASES)
SIZE = {name: dict(zip(KINDS, [*sizes, *[0] * (len(KINDS) - len(sizes))])) for name, _, *sizes in PHASES}
NORMS = {name: n for n, name in enumerate(
    ["mix_norm0", "ffn_norm0", "ple_norm0", "mix_norm1", "ffn_norm1", "ple_norm1"])}
PRE_NORMS = {name: n for n, name in enumerate(["start", "mix_norm0", "ple_norm0", "mix_norm1"])}
H_STEPS = 5
GAINS = {name: n for n, name in enumerate(["mix0", "ffn0", "ple0", "ln", "mix1", "ffn1", "ple1"])}


class Numbers:

    def __init__(self, phase, it=0):
        self.at, self.size, self.it = AT[phase], SIZE[phase], it

    def of(self, kind, k):
        base = self.at[kind] + k
        return base if isinstance(self.it, int) and self.it == 0 else self.it * self.size[kind] + base

    def first(self, kind, k):
        return self.at[kind] + k

    def rounds(self, kind, k, ring):
        base = self.first(kind, k) // ring + 1
        if isinstance(self.it, int) and self.it == 0:
            return base
        assert self.size[kind] % ring == 0
        return self.it * (self.size[kind] // ring) + base


def trunk(nc, x, p, hg_w_in, hg_lb_logits, hg_out_norm, hg_w_out, gm_w_in, gm_ln_g, gm_ln_b, gm_w_s,
          gm_b_s, gm_w_out, norm_mix_pre, norm_mix_post, norm_ffn_pre, norm_ffn_post, ffn_w_gate,
          ffn_w_up, ffn_w_down, ple_w_proj, ple_w_gate, ple_norm, out):
    f32, f32r, i32 = mybir.dt.float32, mybir.dt.float32r, mybir.dt.int32
    ALU, ACT, AX = mybir.AluOpType, mybir.ActivationFunctionType, mybir.AxisListType

    D = x.shape[2]
    T = x.shape[1]
    NT = T // P
    KT = D // P
    NB = D // BLOCK
    HB = ffn_w_gate.shape[2] // BLOCK
    HD = hg_out_norm.shape[1]
    HG = BLOCK // HD
    GC = BLOCK // P
    LEVELS = [1 << i for i in range(7)]
    EPS, LB_FLOOR = 1e-6, 1e-30
    UW = KU * BLOCK
    PLE_K = p.shape[3] // P
    assert (D, T, HB, HD, PLE_K) == (2048, 256, 11, P, KU)

    ctx = ExitStack()
    with ctx:
        def sb(name, shape, dt=f32):
            return ctx.enter_context(nc.sbuf_tensor(name, shape, dt))

        def pb(name):
            return ctx.enter_context(nc.psum_tensor(name, [P, NT, BLOCK], f32))

        def sem(name):
            return ctx.enter_context(nc.semaphore(name))

        stage = sb("stage", [P, STAGES, UW])
        w_hi = sb("w_hi", [P, RING, UW], f32r)
        w_lo = sb("w_lo", [P, RING, UW], f32r)
        h = sb("h", [P, NT, D])
        m = sb("m", [P, NT, D])
        e = sb("e", [P, NT, D])
        a_hi = sb("a_hi", [P, KT, T], f32r)
        a_lo = sb("a_lo", [P, KT, T], f32r)
        y_hi = sb("y_hi", [P, KT, T], f32r)
        y_lo = sb("y_lo", [P, KT, T], f32r)
        p_hi = sb("p_hi", [P, PLE_K, T], f32r)
        p_lo = sb("p_lo", [P, PLE_K, T], f32r)
        gain = sb("gain", [P, D])
        sg = sb("sg", [P, NT, BLOCK])
        hid = sb("hid", [P, NT, BLOCK])
        zg = sb("zg", [P, NT, BLOCK])
        ident = sb("ident", [P, P])
        level_mask = sb("level_mask", [P, len(LEVELS), P // 2])
        upper = sb("upper", [P, P])
        rows = sb("rows", [P, P])
        cols = sb("cols", [P, P])
        junk = zg
        ss = sb("ss", [P, NT, NB])
        hss = sb("hss", [P, NT, NB])
        ss_part = sb("ss_part", [P, NT])
        ms = sb("ms", [P, NT * HG])
        minus_half = sb("minus_half", [P, NT * HG])
        r_post = sb("r_post", [P, NT])
        r_pre = sb("r_pre", [P, NT])
        r_head = sb("r_head", [P, NT * HG])
        oss = sb("oss", [P, NT * HG])
        lb = sb("lb", [P, 6, KT])
        bn = sb("bn", [P, NT, NB, 6])
        mv = sb("mv", [P, NT, 2])
        f_g, k_g, q_g, tot = m[:, 0, 0:1024], m[:, 0, 1024:2048], m[:, 1, 0:1024], m[:, 1, 1024:2048]
        v_g = e[:, 0, 0:1024].rearrange("p (t n) -> p t n", t=NT)
        att = e[:, 0, 1024:2048]
        att_x = e[:, 1, 0:512]
        osq = e[:, 1, 1024:2048]
        ws_raw, wsT, ln_b = e[:, 0, :], e[:, 1, :], e[:, 0, :]
        p_tm = [a.rearrange("p (t d) -> p t d", t=NT) for a in (e[:, 1, 512:1024], e[:, 0, 1536:2048])]

        C_MIX, C_FFN = (0, 16), (32, 48)
        C_LB, C_BS, C_ON = 64, 80, 96

        acc = [pb("acc0"), pb("acc1")]
        scr = [pb("scr0"), pb("scr1")]

        w_loaded = [sem(f"w_loaded{s}") for s in range(STAGES)]
        w_hi_ready = sem("w_hi_ready")
        w_lo_ready = sem("w_lo_ready")
        w_used = sem("w_used")
        acc_read = [sem("acc_read0"), sem("acc_read1")]
        job_done = sem("job_done")
        job_read = [sem("job_read0"), sem("job_read1")]
        piece_hi = sem("piece_hi")
        rows_loaded = sem("rows_loaded")
        const_step = sem("const_step")
        x_loaded = [sem(f"x_loaded{nb}") for nb in range(NB)]
        gain_loaded = sem("gain_loaded")
        p_loaded = sem("p_loaded")
        ws_loaded = sem("ws_loaded")
        ln_b_loaded = sem("ln_b_loaded")
        lb_step = sem("lb_step")
        kq_ready = sem("kq_ready")
        osq_ready = sem("osq_ready")
        hid_ready = sem("hid_ready")
        h_ready = sem("h_ready")
        gate_ready = sem("gate_ready")
        m_ready = sem("m_ready")
        ln_ready = sem("ln_ready")
        tail_squared = sem("tail_squared")
        tail_scaled = sem("tail_scaled")
        ss_ready = sem("ss_ready")
        hss_ready = sem("hss_ready")
        ms_ready = sem("ms_ready")
        rstd_ready = sem("rstd_ready")
        m_zeroed = sem("m_zeroed")
        gain_free = sem("gain_free")
        out_stored = sem("out_stored")

        block = ctx.enter_context(nc.Block())

        def unit_src(w, k0, n0):
            return w[k0 * P:(k0 + KU) * P, bass.ds(n0, BLOCK)].rearrange("(k p) n -> p k n", p=P)

        OUT_ORDER = ([(0, q) for q in range(6)] + [(1, q) for q in range(6)]
                     + [(0, 6), (0, 7), (1, 6), (1, 7)] + [(t, q) for t in (2, 3) for q in range(8)])
        IN_ORDER = [(t, q) for t in range(4) for q in range(8)]

        @block.sync
        def _(sp):
            def load(num, k, src):
                if num.first("unit", k) >= STAGES:
                    sp.wait_ge(w_lo_ready, num.of("unit", k) + 1 - STAGES)
                s = num.first("unit", k) % STAGES
                sp.dma_start(stage[:, s, :].rearrange("p (k n) -> p k n", k=KU), src).then_inc(w_loaded[s], 16)

            def load_x(nb):
                cs = slice(nb * BLOCK, (nb + 1) * BLOCK)
                sp.dma_start(h[:, :, cs], x[0].rearrange("(t p) d -> p t d", p=P)[:, :, cs]).then_inc(x_loaded[nb], 16)
            load_x(0)

            w = hg_w_in[0]
            order = (1, 0, 2, 3)
            for k, (t, q) in enumerate(IN_ORDER):
                load(Numbers("hg_first"), k, unit_src(w, KU * q, order[t] * D))
                if k < NB - 1:
                    load_x(k + 1)
            with sp.Fori(0, 3) as it:
                for k, (t, q) in enumerate(IN_ORDER):
                    load(Numbers("hg_loop", it), k, unit_src(w, KU * q, it * BLOCK + (order[t] * D + BLOCK)))

            def second_projection(phase, w):
                for k, (t, q) in enumerate(OUT_ORDER):
                    load(Numbers(phase), k, unit_src(w, KU * q, t * BLOCK))

            def embedding(layer, phase, nb0):
                for nb in (nb0, nb0 + 1):
                    load(Numbers(phase), nb - nb0, unit_src(ple_w_proj[layer], 0, nb * BLOCK))

            def layer_tail(layer):
                s = str(layer)
                gate, up, down = ffn_w_gate[layer], ffn_w_up[layer], ffn_w_down[layer]
                embedding(layer, "mix_norm" + s, 0)
                for k in range(8):
                    load(Numbers("ffn_first" + s), k, unit_src(gate, KU * k, 0))
                for k in range(8):
                    load(Numbers("ffn_first" + s), 8 + k, unit_src(up, KU * k, 0))
                with sp.Fori(0, HB - 2) as it:
                    num = Numbers("ffn_loop" + s, it)
                    for k in range(8):
                        load(num, k, unit_src(gate, KU * k, it * BLOCK + BLOCK))
                    for k in range(8):
                        rows_ = bass.ds(it * BLOCK + (k % 2) * KU * P, KU * P)
                        load(num, 8 + k, down[rows_, (k // 2) * BLOCK:(k // 2 + 1) * BLOCK]
                             .rearrange("(k p) n -> p k n", p=P))
                    for k in range(8):
                        load(num, 16 + k, unit_src(up, KU * k, it * BLOCK + BLOCK))
                num = Numbers("ffn_last" + s)
                for k in range(8):
                    load(num, k, unit_src(gate, KU * k, (HB - 1) * BLOCK))
                for k in range(8):
                    load(num, 8 + k, unit_src(up, KU * k, (HB - 1) * BLOCK))
                for k in range(16):
                    load(num, 16 + k, unit_src(down, (HB - 2) * BLOCK // P + KU * (k % 4), (k // 4) * BLOCK))
                embedding(layer, "ffn_norm" + s, 2)
                for k, (t, q) in enumerate(IN_ORDER):
                    load(Numbers("ple" + s), k, unit_src(ple_w_gate[layer], KU * q, t * BLOCK))

            second_projection("hg_out", hg_w_out[0])
            layer_tail(0)
            for phase, half in (("gm_v", 1), ("gm_u", 0)):
                for k, (t, q) in enumerate(IN_ORDER):
                    load(Numbers(phase), k, unit_src(gm_w_in[0], KU * q, half * D + t * BLOCK))
            second_projection("gm_out", gm_w_out[0])
            layer_tail(1)
            for nb in range(NB):
                sp.wait_ge(h_ready, H_STEPS * NORMS["ple_norm1"] + nb + 2)
                sp.dma_start(out[0].rearrange("(t p) d -> p t d", p=P)[:, :, nb * BLOCK:(nb + 1) * BLOCK],
                             h[:, :, nb * BLOCK:(nb + 1) * BLOCK]).then_inc(out_stored, 16)
            sp.wait_ge(out_stored, 16 * NB)

        @block.gpsimd
        def _(pool):
            pool.memset(rows[:], 0.0).then_inc(const_step, 1)
            pool.memset(ident[:], 0.0).then_inc(const_step, 1)
            pool.memset(minus_half[:], -0.5).then_inc(const_step, 1)
            pool.memset(upper[:], 1.0).then_inc(const_step, 1)
            pool.memset(level_mask[:], 1.0).then_inc(const_step, 1)
            pool.wait_ge(const_step, 5)
            pool.affine_select(out=ident[:], in_=ident[:], compare_op=ALU.not_equal, fill=1.0, base=0,
                               pattern=[[-1, P]], channel_multiplier=1).then_inc(const_step, 1)
            pool.affine_select(out=upper[:], in_=upper[:], compare_op=ALU.is_ge, fill=0.0, base=0,
                               pattern=[[1, P]], channel_multiplier=-1).then_inc(const_step, 1)
            for i, seg in enumerate(LEVELS):
                cells = level_mask[:, i, :].rearrange("p (n r) -> p n r", r=seg)
                pool.affine_select(out=cells, in_=cells, compare_op=ALU.is_ge, fill=0.0, base=0,
                                   pattern=[[-2 * seg, P // 2 // seg], [0, seg]],
                                   channel_multiplier=1).then_inc(const_step, 1)
            pool.wait_ge(const_step, 14)
            for i, seg in enumerate(LEVELS):
                cells = level_mask[:, i, :].rearrange("p (n r) -> p n r", r=seg)
                pool.affine_select(out=cells, in_=cells, compare_op=ALU.is_ge, fill=0.0, base=seg - 1,
                                   pattern=[[2 * seg, P // 2 // seg], [0, seg]],
                                   channel_multiplier=-1).then_inc(const_step, 1)

            def power(num, k, dst, n):
                pool.wait_ge(ms_ready, num.of("rstd", k) + 1)
                pool.tensor_tensor(out=dst, in0=ms[:, 0:n], in1=minus_half[:, 0:n], op=ALU.pow) \
                    .then_inc(rstd_ready, 1)

            power(Numbers("start"), 0, r_pre[:], NT)
            with pool.Fori(0, 3) as it:
                power(Numbers("hg_loop", it), 0, r_head[:], NT * HG)
            power(Numbers("hg_out"), 0, r_head[:], NT * HG)

            def layer_tail(layer):
                s = str(layer)
                power(Numbers("mix_norm" + s), 0, r_post[:], NT)
                pool.wait_ge(h_ready, H_STEPS * (NORMS["mix_norm" + s] + 1))
                pool.memset(m[:], 0.0).then_inc(m_zeroed, 1)
                power(Numbers("mix_norm" + s), 1, r_pre[:], NT)
                power(Numbers("ffn_norm" + s), 0, r_post[:], NT)
                power(Numbers("ple_norm" + s), 0, r_post[:], NT)

            layer_tail(0)
            power(Numbers("ple_norm0"), 1, r_pre[:], NT)
            power(Numbers("gm_u"), 0, r_head[:, 0:NT], NT)
            layer_tail(1)

        BOUNDARY = {
            False: [("split", 3), ("piece", 0), ("update", 1), ("piece", 1), ("split", 4), ("piece", 2),
                    ("update", 2), ("piece", 3), ("split", 5), ("piece", 4), ("update", 3), ("piece", 5),
                    ("split", 6), ("piece", 6), ("piece", 7), ("split", 7)],
            True: [("split", 3), ("split", 4), ("piece", 0), ("update", 1), ("piece", 1), ("split", 5),
                   ("piece", 2), ("update", 2), ("piece", 3), ("split", 6), ("piece", 4), ("update", 3),
                   ("piece", 5), ("split", 7), ("piece", 6), ("split", 8), ("piece", 7), ("split", 9)],
        }

        def boundary_split(split, num, nxt, i, emb):
            if emb and i < 2:
                split(num, i)
            else:
                split(nxt, i - 2 if emb else i)

        def boundary_splits(split, num, nxt, which, emb):
            for i in which:
                boundary_split(split, num, nxt, i, emb)

        TAILS = {"mix_norm0": (None, 1), "ffn_norm0": (2, None), "ple_norm0": (3, 4),
                 "mix_norm1": (None, 5), "ffn_norm1": (6, None), "ple_norm1": (7, 8)}

        @block.scalar
        def _(act):
            def split(num, k):
                s, r = num.first("unit", k) % STAGES, num.first("unit", k) % RING
                act.wait_ge(w_loaded[s], 16 * num.rounds("unit", k, STAGES))
                if num.first("unit", k) >= RING:
                    act.wait_ge(w_used, num.of("unit", k) + 1 - RING)
                act.activation(w_hi[:, r, :], stage[:, s, :], ACT.Copy).then_inc(w_hi_ready, 1)

            def units(num, ks, steps):
                for k in ks:
                    split(num, k)
                    for step in steps.get(k, ()):
                        step()

            def take(num, task, last_unit, dst, func, scale=1.0):
                act.wait_ge(w_used, num.of("unit", last_unit) + 1)
                pair = num.first("task", task) % 2
                for t in range(NT):
                    i = act.activation(dst[:, t, :], acc[pair][:, t, :], func,
                                       scale=r_pre[:, t:t + 1] if scale is None else scale)
                i.then_inc(acc_read[pair], 1)

            def piece(num, job, hi, scales=None):
                act.wait_ge(job_done, num.of("job", job) + 1)
                src = scr[num.first("job", job) % 2][:, 0, :]
                if scales is None:
                    i = act.activation(hi.rearrange("p k t -> p (k t)"), src, ACT.Copy)
                else:
                    for c in range(KU):
                        i = act.activation(hi[:, c, :], src[:, c * T:(c + 1) * T], ACT.Copy,
                                           scale=scales[:, c:c + 1])
                i.then_inc(piece_hi, 1)

            def square_block(src, sums, nb, done=None):
                act.drain()
                for t in range(NT):
                    i = act.activation(junk[:, t, :], src[:, t, nb * BLOCK:(nb + 1) * BLOCK], ACT.Square,
                                       accum_out=sums[:, t, nb:nb + 1])
                if done is not None:
                    i.then_inc(done, 1)

            def m_squares(num, task, nb):
                act.wait_ge(acc_read[num.first("task", task) % 2], num.rounds("task", task, 2))
                square_block(m, ss, nb, ss_ready)

            def load_gain(vec):
                act.dma_start(gain[:], vec.rearrange("(a n) -> a n", a=1).broadcast_to([P, D])) \
                    .then_inc(gain_loaded, 16)

            def operand(name, nxt, scale_col, emb=()):
                num, job0 = Numbers(name), 1 if name == "start" else 0
                for what, i in BOUNDARY[bool(emb)]:
                    if what == "split":
                        boundary_split(split, num, nxt, i, emb)
                        if emb and i == 3:
                            emb[0]()
                    elif what == "piece":
                        piece(num, job0 + i, a_hi[:, KU * i:KU * i + KU, :],
                              None if scale_col is None else cols[:, scale_col + KU * i:scale_col + KU * i + KU])
                        if emb and i == 1:
                            emb[1]()
                        if scale_col is not None and i % 2:
                            square_block(h, hss, i // 2, hss_ready if i == 7 else None)

            act.wait_ge(const_step, 1)
            for r, src in ((C_MIX[0], norm_mix_pre), (C_FFN[0], norm_ffn_pre), (C_LB, hg_lb_logits)):
                act.dma_start(rows[r:r + src.shape[0] * KT, :],
                              src.rearrange("l (k p) -> (l k) p", p=P)).then_inc(rows_loaded, 16)
            act.dma_start(rows[C_BS:C_BS + KT, :], gm_b_s[0]).then_inc(rows_loaded, 16)
            act.dma_start(rows[C_ON:C_ON + 1, :], hg_out_norm).then_inc(rows_loaded, 16)
            first = Numbers("hg_first")
            act.wait_ge(job_done, 1)
            act.activation(cols[:], scr[0][:, 0, 0:P], ACT.Copy).then_inc(job_read[0], 1)
            for k in range(3):
                split(first, k)
            for nb in range(NB):
                act.wait_ge(x_loaded[nb], 16)
            act.wait_ge(job_read[0], 1)
            operand("start", first, C_MIX[0])
            act.wait_ge(lb_step, 1)
            act.activation(lb[:, 1, :], lb[:, 0, :], ACT.Exp).then_inc(lb_step, 1)

            def flat(pair):
                return scr[pair][:].rearrange("p t n -> p (t n)")

            def gates(num, job):
                act.wait_ge(job_done, num.of("job", job) + 1)
                pair = num.first("job", job) % 2
                act.activation(f_g, flat(pair), ACT.Sigmoid)
                act.activation(k_g, flat(pair), ACT.Sigmoid, scale=-1.0).then_inc(job_read[pair], 1)

            def query(num, job):
                act.wait_ge(job_done, num.of("job", job) + 1)
                pair = num.first("job", job) % 2
                act.activation(q_g, flat(pair), ACT.Silu).then_inc(job_read[pair], 1)

            def out_squares(num, job):
                act.wait_ge(job_done, num.of("job", job) + 1)
                act.activation(osq, flat(num.first("job", job) % 2), ACT.Square).then_inc(osq_ready, 1)

            def y_pieces(num, jobs, kt0):
                for c, job in enumerate(jobs):
                    act.wait_ge(job_done, num.of("job", job) + 1)
                    act.activation(y_hi[:, bass.ds(kt0 + KU * c, KU), :].rearrange("p k t -> p (k t)"),
                                   scr[num.first("job", job) % 2][:, 0, :], ACT.Copy,
                                   scale=cols[:, C_ON:C_ON + 1]).then_inc(piece_hi, 1)

            def own_steps(num, zf_job, zq_job):
                return {10: [lambda: take(num, 0, 7, sg, ACT.Copy, None)],
                        15: [lambda: gates(num, zf_job)],
                        18: [lambda: take(num, 1, 15, sg, ACT.Copy, None)],
                        21: [lambda: query(num, zq_job)],
                        26: [lambda: take(num, 2, 23, v_g, ACT.Copy, None)]}

            def pre_factor_ready(name, k):
                act.wait_ge(rstd_ready, Numbers(name).of("rstd", k) + 1)

            def load_first():
                load_gain(norm_mix_post[0])
                act.dma_start(p_tm[0], p[0, 0].rearrange("(t p) d -> p t d", p=P)).then_inc(p_loaded, 16)
            steps = own_steps(first, 0, 1)
            steps[10].insert(0, lambda: pre_factor_ready("start", 0))
            steps[12] = [load_first]
            units(first, range(8, 32), steps)
            with act.Fori(0, 3) as it:
                num = Numbers("hg_loop", it)
                steps = own_steps(num, 6, 8)
                steps[2] = [lambda: take(num, -1, -1, zg, ACT.Silu, None)]
                steps[16] = [lambda: out_squares(num, 7)]
                steps[25] = [lambda: y_pieces(num, (9, 10), it * HG)]
                units(num, range(32), steps)
            out_num = Numbers("hg_out")
            units(out_num, range(32), {
                2: [lambda: take(out_num, -1, -1, zg, ACT.Silu, None)],
                8: [lambda: out_squares(out_num, 6)], 11: [lambda: y_pieces(out_num, (7, 8), 3 * HG)],
                17: [lambda: piece(out_num, 9, p_hi[:])],
                20: [lambda: m_squares(out_num, 0, 0)], 22: [lambda: m_squares(out_num, 1, 1)],
                29: [lambda: m_squares(out_num, 2, 2)]})

            def layer_tail(layer, out_num):
                s = str(layer)
                mix, ffn = Numbers("mix_norm" + s), Numbers("ffn_norm" + s)
                first, last, ple = Numbers("ffn_first" + s), Numbers("ffn_last" + s), Numbers("ple" + s)

                def take_e(num, nb):
                    take(num, nb % 2, nb % 2, e[:, :, nb * BLOCK:(nb + 1) * BLOCK], ACT.Copy)

                def tail_squares(src, norm):
                    act.drain()
                    for t in range(NT):
                        i = act.activation(junk[:, t, :], src(t), ACT.Square, accum_out=ss[:, t, NB - 1:NB])
                        if t == 0:
                            i.then_inc(tail_squared, 1)
                    i.then_inc(ss_ready, 1)

                boundary_splits(split, mix, first, range(3), True)
                pair = out_num.first("task", 3) % 2

                def out_bank(t):
                    if t == 0:
                        act.wait_ge(w_used, out_num.of("unit", 31) + 1)
                    else:
                        act.wait_ge(tail_scaled, TAILS["mix_norm" + s][1])
                    return acc[pair][:, t, :]
                tail_squares(out_bank, "mix_norm" + s)
                operand("mix_norm" + s, first, C_FFN[layer], [lambda: take_e(mix, 0), lambda: take_e(mix, 1)])

                def load_gain_ffn():
                    act.wait_ge(acc_read[pair], out_num.rounds("task", 3, 2))
                    load_gain(norm_ffn_post[layer])
                units(first, range(8, 16), {9: [load_gain_ffn],
                                            10: [lambda: pre_factor_ready("mix_norm" + s, 1),
                                                 lambda: take(first, 0, 7, sg, ACT.Silu, None)]})

                def hid_pieces(num, job, kt):
                    for c in range(2):
                        piece(num, job + c, y_hi[:, kt + KU * c:kt + KU * c + KU, :])
                with act.Fori(0, HB - 2) as it:
                    body = Numbers("ffn_loop" + s, it)
                    units(body, range(24), {7: [lambda: hid_pieces(body, 0, 0)],
                                            10: [lambda: take(body, 0, 7, sg, ACT.Silu, None)]})
                units(last, range(32),
                      {7: [lambda: hid_pieces(last, 0, 0)], 10: [lambda: take(last, 0, 7, sg, ACT.Silu, None)],
                       18: [lambda: hid_pieces(last, 2, GC)],
                       24: [lambda: m_squares(last, 2, 0)], 28: [lambda: m_squares(last, 3, 1)],
                       31: [lambda: m_squares(last, 4, 2)]})

                boundary_splits(split, ffn, ple, range(3), True)

                def m_tile(norm):
                    def tile(t):
                        if TAILS[norm][t] is not None:
                            act.wait_ge(tail_scaled, TAILS[norm][t])
                        else:
                            act.wait_ge(acc_read[last.first("task", 5) % 2], last.rounds("task", 5, 2))
                        return m[:, t, (NB - 1) * BLOCK:]
                    return tile
                tail_squares(m_tile("ffn_norm" + s), "ffn_norm" + s)
                operand("ffn_norm" + s, ple, None, [lambda: take_e(ffn, 2), lambda: take_e(ffn, 3)])

                def load_gain_ple():
                    act.wait_ge(gain_free, 1 + 2 * layer)
                    load_gain(ple_norm[layer])

                def gate(nb):
                    if nb > 0:
                        act.wait_ge(m_ready, nb + (NB - 1) * layer)
                    take(ple, nb, 8 * nb + 7, sg, ACT.Sigmoid)

                def gated_squares(nb):
                    act.wait_ge(m_ready, nb + 1 + (NB - 1) * layer)
                    square_block(m, ss, nb, ss_ready)
                units(ple, range(8, 32), {9: [load_gain_ple],
                                          10: [lambda: gate(0)], 13: [lambda: gated_squares(0)],
                                          18: [lambda: gate(1)], 21: [lambda: gated_squares(1)],
                                          26: [lambda: gate(2)], 29: [lambda: gated_squares(2)]})

                norm = "ple_norm" + s
                if layer == 0:
                    boundary_splits(split, None, Numbers("gm_v"), range(3), False)
                act.wait_ge(m_ready, NB - 1 + (NB - 1) * layer)
                act.wait_ge(w_used, ple.of("unit", 31) + 1)
                pair = ple.first("task", 3) % 2
                act.activation(sg[:, 0, :], acc[pair][:, 0, :], ACT.Sigmoid).then_inc(gate_ready, 1)
                act.activation(sg[:, 1, :], acc[pair][:, 1, :], ACT.Sigmoid).then_inc(acc_read[pair], 1)
                tail_squares(m_tile(norm), norm)
                if layer == 0:
                    operand("ple_norm0", Numbers("gm_v"), C_MIX[1])

            layer_tail(0, out_num)

            gv, gu, go = Numbers("gm_v"), Numbers("gm_u"), Numbers("gm_out")

            def load_spatial():
                act.dma_start(ws_raw.rearrange("p (g s) -> p g s", g=KT), gm_w_s[0].rearrange("g t s -> t g s")) \
                    .then_inc(ws_loaded, 16)
                act.wait_ge(gain_free, 2)
                load_gain(gm_ln_g[0])

            def take_v(num, task, last_unit, nb):
                take(num, task, last_unit, m[:, :, nb * BLOCK:(nb + 1) * BLOCK], ACT.Gelu, None)

            def load_ln_b():
                act.wait_ge(job_read[gv.first("job", 3) % 2], gv.rounds("job", 3, 2))
                act.dma_start(ln_b, gm_ln_b[0].rearrange("(a n) -> a n", a=1).broadcast_to([P, D])) \
                    .then_inc(ln_b_loaded, 16)

            def take_u(num, task, last_unit, nb):
                if nb > 0:
                    job = 3 * (nb - 1)
                    act.wait_ge(job_read[gu.first("job", job) % 2], gu.rounds("job", job, 2))
                take(num, task, last_unit, sg, ACT.Gelu, None)

            def gm_pieces(num, jobs, nb):
                for c, job in enumerate(jobs):
                    piece(num, job, y_hi[:, GC * nb + KU * c:GC * nb + KU * c + KU, :])

            def load_gain_mix1():
                act.wait_ge(ln_ready, NB)
                load_gain(norm_mix_post[1])
                act.dma_start(p_tm[1], p[1, 0].rearrange("(t p) d -> p t d", p=P)).then_inc(p_loaded, 16)
            units(gv, range(8, 32), {9: [load_spatial],
                                     10: [lambda: pre_factor_ready("ple_norm0", 1), lambda: take_v(gv, 0, 7, 0)], 18: [lambda: take_v(gv, 1, 15, 1)],
                                     20: [load_ln_b], 26: [lambda: take_v(gv, 2, 23, 2)]})
            units(gu, range(32), {2: [lambda: take_v(gu, -1, -1, 3)],
                                  10: [lambda: take_u(gu, 0, 7, 0)], 15: [lambda: gm_pieces(gu, (1, 2), 0)],
                                  17: [load_gain_mix1],
                                  18: [lambda: take_u(gu, 1, 15, 1)], 23: [lambda: gm_pieces(gu, (4, 5), 1)],
                                  26: [lambda: take_u(gu, 2, 23, 2)], 31: [lambda: gm_pieces(gu, (7, 8), 2)]})
            units(go, range(32), {2: [lambda: take_u(go, -1, -1, 3)], 7: [lambda: gm_pieces(go, (1, 2), 3)],
                                  17: [lambda: piece(go, 3, p_hi[:])],
                                  20: [lambda: m_squares(go, 0, 0)], 22: [lambda: m_squares(go, 1, 1)],
                                  29: [lambda: m_squares(go, 2, 2)]})
            layer_tail(1, go)

        @block.vector
        def _(dve):
            def split(num, k):
                s, r = num.first("unit", k) % STAGES, num.first("unit", k) % RING
                dve.wait_ge(w_hi_ready, num.of("unit", k) + 1)
                dve.tensor_tensor(out=w_lo[:, r, :], in0=stage[:, s, :], in1=w_hi[:, r, :].bitcast(f32),
                                  op=ALU.subtract).then_inc(w_lo_ready, 1)

            def units(num, ks, steps):
                for k in ks:
                    split(num, k)
                    for step in steps.get(k, ()):
                        step()

            def piece(num, nth, job, hi, lo, scales=None):
                dve.wait_ge(piece_hi, num.of("piece", nth) + 1)
                pair = num.first("job", job) % 2
                src = scr[pair][:, 0, :]
                if scales is None:
                    i = dve.tensor_tensor(out=lo.rearrange("p k t -> p (k t)"), in0=src,
                                          in1=hi.rearrange("p k t -> p (k t)").bitcast(f32), op=ALU.subtract)
                else:
                    for c in range(KU):
                        i = dve.scalar_tensor_tensor(out=lo[:, c, :], in0=src[:, c * T:(c + 1) * T],
                                                     scalar=scales[:, c:c + 1], in1=hi[:, c, :].bitcast(f32),
                                                     op0=ALU.mult, op1=ALU.subtract)
                i.then_inc(job_read[pair], 1)

            def mean_squares(sums, n, count):
                dve.tensor_reduce(ms[:, 0:n], sums, AX.X, ALU.add)
                dve.drain()
                dve.tensor_scalar(ms[:, 0:n], ms[:, 0:n], 1.0 / count, EPS, ALU.mult, ALU.add).then_inc(ms_ready, 1)

            def operand(name, nxt, scale_col, update, emb=False):
                num, job0 = Numbers(name), 1 if name == "start" else 0
                update(0)
                for what, i in BOUNDARY[emb]:
                    if what == "split":
                        boundary_split(split, num, nxt, i, emb)
                    elif what == "update":
                        update(i)
                    else:
                        piece(num, i, job0 + i, a_hi[:, KU * i:KU * i + KU, :], a_lo[:, KU * i:KU * i + KU, :],
                              None if scale_col is None else cols[:, scale_col + KU * i:scale_col + KU * i + KU])

            def pre_factor(name):
                dve.wait_ge(hss_ready, PRE_NORMS[name] + 1)
                mean_squares(hss[:], NT, D)

            def gain_of(nb):
                return gain[:, nb * BLOCK:(nb + 1) * BLOCK].unsqueeze(1).broadcast_to([P, NT, BLOCK])

            def blk_of(x_, nb):
                return x_[:, :, nb * BLOCK:(nb + 1) * BLOCK]

            def wait_gain(norm):
                dve.wait_ge(gain_loaded, 16 * (GAINS[norm.replace("_norm", "")] + 1))

            def times_gain(norm, nb):
                dve.wait_ge(ss_ready, NB * NORMS[norm] + nb + 1)
                wait_gain(norm)
                dve.tensor_tensor(out=blk_of(m, nb), in0=blk_of(m, nb), in1=gain_of(nb), op=ALU.mult)
                if nb == NB - 2:
                    dve.tensor_reduce(ss_part[:], ss[:, :, 0:NB - 1], AX.X, ALU.add)
                    dve.drain()
                    dve.tensor_scalar(ss_part[:], ss_part[:], 1.0 / D, EPS, ALU.mult, ALU.add)

            def mean_square(norm):
                dve.wait_ge(ss_ready, NB * NORMS[norm] + NB)
                dve.scalar_tensor_tensor(out=ms[:, 0:NT], in0=ss[:, :, NB - 1], scalar=1.0 / D, in1=ss_part[:],
                                         op0=ALU.mult, op1=ALU.add).then_inc(ms_ready, 1)

            LAST = slice((NB - 1) * BLOCK, NB * BLOCK)

            def tail_out(norm, num):
                dve.wait_ge(w_used, num.of("unit", 31) + 1)
                wait_gain(norm)
                pair = num.first("task", 3) % 2
                dve.tensor_tensor(out=hid[:, 1, :], in0=acc[pair][:, 1, :], in1=gain[:, LAST], op=ALU.mult) \
                    .then_inc(tail_scaled, 1)
                dve.wait_ge(tail_squared, NORMS[norm] + 1)
                dve.tensor_tensor(out=hid[:, 0, :], in0=acc[pair][:, 0, :], in1=gain[:, LAST], op=ALU.mult) \
                    .then_inc(acc_read[pair], 1)
                mean_square(norm)

            def tail_gains(norm):
                wait_gain(norm)
                for t in range(NT):
                    i = dve.tensor_tensor(out=hid[:, t, :], in0=m[:, t, LAST], in1=gain[:, LAST], op=ALU.mult)
                    if t == 0:
                        mean_square(norm)
                i.then_inc(gain_free, 1)

            def tail_down(norm, num):
                dve.wait_ge(w_used, num.of("unit", 31) + 1)
                pair = num.first("task", 5) % 2
                for t in range(NT):
                    i = dve.tensor_tensor(out=m[:, t, LAST], in0=acc[pair][:, t, :], in1=m[:, t, LAST], op=ALU.add)
                    i.then_inc((tail_scaled, acc_read[pair])[t], 1)
                dve.wait_ge(acc_read[pair], num.rounds("task", 5, 2))
                tail_gains(norm)

            def tail_gated(norm, ple):
                pair = ple.first("task", 3) % 2
                for t in range(NT):
                    if t == 0:
                        dve.wait_ge(gate_ready, int(norm[-1]) + 1)
                    else:
                        dve.wait_ge(acc_read[pair], ple.rounds("task", 3, 2))
                    dve.tensor_tensor(out=m[:, t, LAST], in0=e[:, t, LAST], in1=sg[:, t, :], op=ALU.mult) \
                        .then_inc(tail_scaled, 1)
                dve.wait_ge(tail_scaled, TAILS[norm][1])
                tail_gains(norm)

            def add_block(norm):
                def update(nb):
                    if nb == 0:
                        dve.wait_ge(rstd_ready, Numbers(norm).of("rstd", 0) + 1)
                    width = BLOCK // 2 if nb == 0 else BLOCK
                    for c0 in range(nb * BLOCK, (nb + 1) * BLOCK, width):
                        cs = slice(c0, c0 + width)
                        for t in range(NT):
                            i = dve.scalar_tensor_tensor(
                                out=h[:, t, cs], in0=m[:, t, cs] if nb < NB - 1 else hid[:, t, :],
                                scalar=r_post[:, t:t + 1], in1=h[:, t, cs], op0=ALU.mult, op1=ALU.add)
                        i.then_inc(h_ready, 1)
                return update

            def take_m(num, task, last_unit, nb, add=False):
                dve.wait_ge(w_used, num.of("unit", last_unit) + 1)
                pair = num.first("task", task) % 2
                if add:
                    i = dve.tensor_tensor(out=blk_of(m, nb), in0=acc[pair][:], in1=blk_of(m, nb), op=ALU.add)
                else:
                    i = dve.tensor_copy(blk_of(m, nb), acc[pair][:])
                i.then_inc(acc_read[pair], 1)

            first = Numbers("hg_first")
            units(first, range(3), {})
            dve.wait_ge(job_read[0], 1)
            logits = cols[:, C_LB:C_LB + KT]
            dve.tensor_tensor(out=lb[:, 0, :], in0=logits, in1=logits, op=ALU.subtract).then_inc(lb_step, 1)
            operand("start", first, C_MIX[0], lambda nb: None)
            units(first, range(8, 10), {})
            pre_factor("start")
            dve.wait_ge(lb_step, 2)
            dve.reciprocal(lb[:, 2, :], lb[:, 1, :])
            dve.drain()
            dve.tensor_tensor(out=lb[:, 3, :], in0=lb[:, 1, :], in1=lb[:, 2, :], op=ALU.mult)
            dve.drain()
            dve.tensor_tensor(out=lb[:, 4, :], in0=lb[:, 3, :], in1=lb[:, 3, :], op=ALU.subtract)
            dve.drain()
            lb_low, lb_rest = lb[:, 5, :], lb[:, 0, :]
            dve.tensor_scalar(lb_low, lb[:, 4, :], LB_FLOOR, None, ALU.max)
            dve.tensor_scalar(lb_rest, lb[:, 4, :], -1.0, 1.0, ALU.mult, ALU.add)
            dve.drain()

            TOT = {1: f_g}
            at = 0
            for seg in LEVELS[1:]:
                n = HG * T // seg
                TOT[seg] = tot[:, at:at + n]
                at += n

            def fk(num, zf_job, group):
                dve.wait_ge(job_read[num.first("job", zf_job) % 2], num.rounds("job", zf_job, 2))
                for hd in range(HG):
                    col = bass.ds(group * HG + hd, 1)
                    dve.tensor_scalar(f_g[:, hd * T:(hd + 1) * T], f_g[:, hd * T:(hd + 1) * T],
                                      lb_rest[:, col], lb_low[:, col], ALU.mult, ALU.add)
                for hd in range(HG):
                    col = bass.ds(group * HG + hd, 1)
                    i = dve.tensor_scalar(k_g[:, hd * T:(hd + 1) * T], k_g[:, hd * T:(hd + 1) * T],
                                          lb_rest[:, col], None, ALU.mult)
                i.then_inc(kq_ready, 1)

            def totals():
                for seg in LEVELS[1:]:
                    dve.drain()
                    halves = TOT[seg // 2].rearrange("p (n two) -> p n two", two=2)
                    dve.tensor_tensor(out=TOT[seg], in0=halves[:, :, 0], in1=halves[:, :, 1], op=ALU.mult)

            def diagonal(num, job):
                dve.wait_ge(job_done, num.of("job", job) + 1)
                pair = num.first("job", job) % 2
                dve.tensor_tensor(out=q_g, in0=q_g, in1=f_g, op=ALU.mult).then_inc(kq_ready, 1)
                b = NT * HG
                dve.tensor_tensor(out=att.rearrange("p (b t) -> p b t", b=b),
                                  in0=scr[pair][:].rearrange("p two (b t) -> p (two b) t", t=P),
                                  in1=ident[:].unsqueeze(1).broadcast_to([P, b, P]), op=ALU.mult) \
                    .then_inc(job_read[pair], 1)

            def level(num, lev, job):
                seg = LEVELS[lev]
                pair = num.first("job", job) % 2
                dve.wait_ge(job_done, num.of("job", job) + 1)
                dve.wait_ge(job_read[1 - pair], num.rounds("job", job - 1, 2))
                q2 = q_g.rearrange("p (n two r) -> p n two r", two=2, r=seg)
                k2 = k_g.rearrange("p (n two r) -> p n two r", two=2, r=seg)
                t2 = TOT[seg].rearrange("p (n two) -> p n two", two=2)
                n = HG * T // (2 * seg)
                dve.tensor_tensor(out=q2[:, :, 1, :], in0=q2[:, :, 1, :],
                                  in1=t2[:, :, 0].unsqueeze(2).broadcast_to([P, n, seg]), op=ALU.mult)
                dve.tensor_tensor(out=k2[:, :, 0, :], in0=k2[:, :, 0, :],
                                  in1=t2[:, :, 1].unsqueeze(2).broadcast_to([P, n, seg]), op=ALU.mult) \
                    .then_inc(kq_ready, 1)
                b, ns = NT * HG, P // 2 // seg
                dve.copy_predicated(
                    att.rearrange("p (b n two r) -> p b n two r", b=b, two=2, r=seg)[:, :, :, 1, :],
                    level_mask[:, lev, :].bitcast(i32).rearrange("p (n r) -> p n r", r=seg)
                    .unsqueeze(1).broadcast_to([P, b, ns, seg]),
                    scr[pair][:, 0, :].rearrange("p (b n r) -> p b n r", b=b, r=seg)).then_inc(job_read[pair], 1)

            def cross(num, job):
                dve.wait_ge(job_done, num.of("job", job) + 1)
                pair = num.first("job", job) % 2
                dve.tensor_copy(att_x, scr[pair][:, 0, :]).then_inc(job_read[pair], 1)

            def head_mean_squares(num):
                dve.wait_ge(osq_ready, num.of("grp", 0) + 1)
                mean_squares(osq.rearrange("p (b v) -> p b v", b=NT * HG), NT * HG, HD)

            def head_outputs(num, job):
                dve.wait_ge(rstd_ready, num.of("rstd", 0) + 1)
                pair = num.first("job", job) % 2
                dve.tensor_tensor(out=hid[:].rearrange("p c (h v) -> p h c v", h=HG),
                                  in0=scr[pair][:].rearrange("p two (h c v) -> p (two h) c v", c=NT, v=HD),
                                  in1=r_head[:].rearrange("p (h c) -> p h c", c=NT).unsqueeze(3)
                                  .broadcast_to([P, HG, NT, HD]), op=ALU.mult).then_inc(job_read[pair], 1)
                dve.drain()
                dve.tensor_tensor(out=hid[:], in0=hid[:], in1=zg[:], op=ALU.mult).then_inc(hid_ready, 1)

            def y_pieces(num, jobs, kt0):
                for c, job in enumerate(jobs):
                    dve.wait_ge(piece_hi, num.of("piece", c) + 1)
                    pair = num.first("job", job) % 2
                    kts = bass.ds(kt0 + KU * c, KU)
                    dve.scalar_tensor_tensor(out=y_lo[:, kts, :].rearrange("p k t -> p (k t)"),
                                             in0=scr[pair][:, 0, :], scalar=cols[:, C_ON:C_ON + 1],
                                             in1=y_hi[:, kts, :].bitcast(f32).rearrange("p k t -> p (k t)"),
                                             op0=ALU.mult, op1=ALU.subtract).then_inc(job_read[pair], 1)

            def own_steps(num, group, zf_job, diag_job):
                return {17: [lambda: fk(num, zf_job, group)], 19: [totals],
                        28: [lambda: diagonal(num, diag_job)],
                        30: [lambda: level(num, 0, diag_job + 1)]}

            units(first, range(10, 32), own_steps(first, 0, 0, 2))
            with dve.Fori(0, 3) as it:
                num = Numbers("hg_loop", it)
                steps = own_steps(num, it + 1, 6, 11)
                for lev in range(1, len(LEVELS)):
                    steps[2 * lev - 2] = [lambda lev=lev: level(num, lev, lev - 2)]
                steps[12] = [lambda: cross(num, 5)]
                steps[16] = [lambda: head_mean_squares(num)]
                steps[18] = [lambda: head_outputs(num, 7)]
                steps[25] = [lambda: y_pieces(num, (9, 10), it * HG)]
                units(num, range(32), steps)
            out_num = Numbers("hg_out")
            steps = {lev - 1: [lambda lev=lev: level(out_num, lev, lev - 2)] for lev in range(1, len(LEVELS))}
            steps[6] = [lambda: cross(out_num, 5)]
            steps[8] = [lambda: head_mean_squares(out_num)]
            steps[9] = [lambda: head_outputs(out_num, 6)]
            steps[11] = [lambda: y_pieces(out_num, (7, 8), 3 * HG)]

            def out_steps(num, norm, p_job):
                return {17: [lambda: piece(num, 2, p_job, p_hi[:], p_lo[:])],
                        16: [lambda: take_m(num, 0, 13, 0)], 18: [lambda: take_m(num, 1, 15, 1)],
                        22: [lambda: times_gain(norm, 0)], 24: [lambda: times_gain(norm, 1)],
                        26: [lambda: take_m(num, 2, 23, 2)], 31: [lambda: times_gain(norm, 2)]}
            steps.update(out_steps(out_num, "mix_norm0", 9))
            units(out_num, range(32), steps)

            def layer_tail(layer, out_num):
                s = str(layer)
                mix, ffn = Numbers("mix_norm" + s), Numbers("ffn_norm" + s)
                first, last, ple = Numbers("ffn_first" + s), Numbers("ffn_last" + s), Numbers("ple" + s)

                norm = "mix_norm" + s
                boundary_splits(split, mix, first, range(3), True)
                tail_out(norm, out_num)
                operand(norm, first, C_FFN[layer], add_block(norm), True)
                units(first, range(8, 16), {9: [lambda: pre_factor("mix_norm" + s)]})

                def hidden(num, task, last_unit):
                    dve.wait_ge(w_used, num.of("unit", last_unit) + 1)
                    pair = num.first("task", task) % 2
                    for t in range(NT):
                        i = dve.scalar_tensor_tensor(out=hid[:, t, :], in0=acc[pair][:, t, :],
                                                     scalar=r_pre[:, t:t + 1], in1=sg[:, t, :],
                                                     op0=ALU.mult, op1=ALU.mult)
                    i.then_inc(acc_read[pair], 1)

                def hid_pieces(num, job, kt):
                    for c in range(2):
                        kts = slice(kt + KU * c, kt + KU * c + KU)
                        piece(num, job + c, job + c, y_hi[:, kts, :], y_lo[:, kts, :])

                dve.wait_ge(m_zeroed, layer + 1)
                with dve.Fori(0, HB - 2) as it:
                    body = Numbers("ffn_loop" + s, it)
                    units(body, range(24),
                          {2: [lambda: hidden(body, -1, -1)], 7: [lambda: hid_pieces(body, 0, 0)]}
                          | {12 + 2 * nb: [lambda nb=nb: take_m(body, 1 + nb, 9 + 2 * nb, nb, True)]
                             for nb in range(NB)})
                norm = "ffn_norm" + s
                units(last, range(32), {2: [lambda: hidden(last, -1, -1)], 7: [lambda: hid_pieces(last, 0, 0)],
                                        17: [lambda: hidden(last, 1, 15)], 18: [lambda: hid_pieces(last, 2, GC)],
                                        22: [lambda: take_m(last, 2, 19, 0, True)],
                                        26: [lambda: take_m(last, 3, 23, 1, True)],
                                        27: [lambda: times_gain(norm, 0)],
                                        30: [lambda: take_m(last, 4, 27, 2, True)],
                                        31: [lambda: times_gain(norm, 1)]})

                boundary_splits(split, ffn, ple, range(3), True)
                times_gain(norm, 2)
                dve.drain()
                tail_down(norm, last)
                operand(norm, ple, None, add_block(norm), True)
                norm = "ple_norm" + s

                def gated(nb):
                    pair = ple.first("task", nb) % 2
                    dve.wait_ge(acc_read[pair], ple.rounds("task", nb, 2))
                    dve.tensor_tensor(out=blk_of(m, nb), in0=blk_of(e, nb), in1=sg[:], op=ALU.mult) \
                        .then_inc(m_ready, 1)
                units(ple, range(8, 32), {11: [lambda: gated(0)], 15: [lambda: times_gain(norm, 0)],
                                          19: [lambda: gated(1)], 23: [lambda: times_gain(norm, 1)],
                                          27: [lambda: gated(2)], 31: [lambda: times_gain(norm, 2)]})

                if layer == 0:
                    boundary_splits(split, None, Numbers("gm_v"), range(3), False)
                tail_gated(norm, ple)
                if layer == 0:
                    operand(norm, Numbers("gm_v"), C_MIX[1], add_block(norm))
                else:
                    dve.wait_ge(gain_free, 4)
                    for nb in range(NB):
                        add_block(norm)(nb)

            layer_tail(0, out_num)

            gv, gu, go = Numbers("gm_v"), Numbers("gm_u"), Numbers("gm_out")

            def v_stats(num, task, nb):
                pair = num.first("task", task) % 2
                dve.wait_ge(acc_read[pair], num.rounds("task", task, 2))
                for t in range(NT):
                    dve.bn_stats(bn[:, t, nb, :], m[:, t, nb * BLOCK:(nb + 1) * BLOCK])

            def spatial_weights(job):
                dve.wait_ge(job_done, gv.of("job", job) + 1)
                pair = gv.first("job", job) % 2
                dve.tensor_tensor(out=wsT[:, job * BLOCK:(job + 1) * BLOCK].rearrange("p (g t) -> p g t", t=P),
                                  in0=scr[pair][:, 0, :].rearrange("p (g t) -> p g t", t=P),
                                  in1=upper[:].unsqueeze(1).broadcast_to([P, GC, P]), op=ALU.mult) \
                    .then_inc(job_read[pair], 1)

            def v_factor():
                dve.drain()
                for t in range(NT):
                    dve.bn_aggr(mv[:, t, :], bn[:, t, :, :].rearrange("p a b -> p (a b)"))
                dve.drain()
                dve.tensor_scalar(ms[:, 0:NT], mv[:, :, 1], EPS, None, ALU.add).then_inc(ms_ready, 1)

            def layer_norm(nb):
                if nb == 0:
                    dve.wait_ge(rstd_ready, gu.of("rstd", 0) + 1)
                    dve.wait_ge(gain_loaded, 16 * (GAINS["ln"] + 1))
                    dve.wait_ge(ln_b_loaded, 16)
                for t in range(NT):
                    cs = slice(nb * BLOCK, (nb + 1) * BLOCK)
                    dve.tensor_scalar(m[:, t, cs], m[:, t, cs], mv[:, t, 0:1], r_head[:, t:t + 1],
                                      ALU.subtract, ALU.mult)
                dve.drain()
                dve.tensor_tensor(out=blk_of(m, nb), in0=blk_of(m, nb), in1=gain_of(nb), op=ALU.mult)
                dve.drain()
                dve.tensor_tensor(out=blk_of(m, nb), in0=blk_of(m, nb),
                                  in1=ln_b[:, nb * BLOCK:(nb + 1) * BLOCK].unsqueeze(1).broadcast_to([P, NT, BLOCK]),
                                  op=ALU.add).then_inc(ln_ready, 1)

            def gm_outputs(num, task, job, nb):
                dve.wait_ge(acc_read[num.first("task", task) % 2], num.rounds("task", task, 2))
                dve.wait_ge(job_done, num.of("job", job) + 1)
                pair = num.first("job", job) % 2
                for g in range(GC):
                    cs = slice(g * P, (g + 1) * P)
                    i = dve.scalar_tensor_tensor(out=hid[:, :, cs], in0=scr[pair][:, :, cs],
                                                 scalar=cols[:, C_BS + GC * nb + g:C_BS + GC * nb + g + 1],
                                                 in1=sg[:, :, cs], op0=ALU.add, op1=ALU.mult)
                i.then_inc(job_read[pair], 1)

            def gm_pieces(num, nth, jobs, nb):
                for c, job in enumerate(jobs):
                    kts = slice(GC * nb + KU * c, GC * nb + KU * c + KU)
                    piece(num, nth + c, job, y_hi[:, kts, :], y_lo[:, kts, :])

            units(gv, range(8, 32), {9: [lambda: pre_factor("ple_norm0")], 11: [lambda: v_stats(gv, 0, 0)], 19: [lambda: v_stats(gv, 1, 1)],
                                     27: [lambda: v_stats(gv, 2, 2)]}
                  | {14 + j: [lambda j=j: spatial_weights(j)] for j in range(NB)})
            units(gu, range(32), {3: [lambda: v_stats(gu, -1, 3), v_factor], 4: [lambda: layer_norm(0)],
                                  6: [lambda: layer_norm(1)], 9: [lambda: layer_norm(2)],
                                  13: [lambda: layer_norm(3)],
                                  11: [lambda: gm_outputs(gu, 0, 0, 0)], 15: [lambda: gm_pieces(gu, 0, (1, 2), 0)],
                                  19: [lambda: gm_outputs(gu, 1, 3, 1)], 23: [lambda: gm_pieces(gu, 2, (4, 5), 1)],
                                  27: [lambda: gm_outputs(gu, 2, 6, 2)], 31: [lambda: gm_pieces(gu, 4, (7, 8), 2)]})
            units(go, range(32), {3: [lambda: gm_outputs(go, -1, 0, 3)], 7: [lambda: gm_pieces(go, 0, (1, 2), 3)]}
                  | out_steps(go, "mix_norm1", 3))
            layer_tail(1, go)

        @block.tensor
        def _(pe):
            def unit(num, k, task, x_hi, x_lo, kt, is_first, is_last, x_lo_ready=None):
                pair = num.first("task", task) % 2
                if is_first and num.first("task", task) >= 2:
                    pe.wait_ge(acc_read[pair], num.rounds("task", task, 2) - 1)
                pe.wait_ge(w_lo_ready, num.of("unit", k) + 1)
                r = num.first("unit", k) % RING
                for products in ((0, 1, 2),) if x_lo_ready is None else ((0, 1), (2,)):
                    if products == (2,):
                        x_lo_ready()
                    for c in range(KU):
                        wh, wl = (w[:, r, c * BLOCK:(c + 1) * BLOCK] for w in (w_hi, w_lo))
                        for t in range(NT):
                            ts = slice(t * P, (t + 1) * P)
                            xh, xl = x_hi[:, kt + c, ts], x_lo[:, kt + c, ts]
                            for n in products:
                                a, b = ((xh, wl), (xh, wh), (xl, wh))[n]
                                i = pe.matmul(acc[pair][:, t, :], a, b, start=is_first and c == 0 and n == 0,
                                              stop=is_last and c == KU - 1 and n == 2)
                i.then_inc(w_used, 1)

            def in_unit(num, k, unit0=0, task0=0, x_lo_ready=None):
                t, q = k // 8, k % 8
                unit(num, unit0 + k, task0 + t, a_hi, a_lo, KU * q, q == 0, q == 7, x_lo_ready)

            def job_begin(num, job):
                pair = num.first("job", job) % 2
                if num.first("job", job) >= 2:
                    pe.wait_ge(job_read[pair], num.rounds("job", job, 2) - 1)
                return scr[pair]

            def transpose_piece(num, job, src):
                s = job_begin(num, job)
                for c in range(KU):
                    for t in range(NT):
                        i = pe.transpose(s[:, 0, c * T + t * P:c * T + (t + 1) * P], src(c, t), ident[:])
                i.then_inc(job_done, 1)

            def operand(name, nxt, emb=None):
                num, job0 = Numbers(name), 1 if name == "start" else 0

                def transpose(pc):
                    if name == "start":
                        pe.wait_ge(x_loaded[pc // 2], 16)
                    else:
                        pe.wait_ge(h_ready, H_STEPS * NORMS[name] + (1 if pc == 0 else pc // 2 + 2))
                    transpose_piece(num, job0 + pc,
                                    lambda c, t: h[:, t, (KU * pc + c) * P:(KU * pc + c + 1) * P])

                def embedding(i):
                    if i == 1:
                        pe.wait_ge(ss_ready, NB * NORMS[name] + NB)
                    unit(num, i, i, p_hi, p_lo, 0, True, True)
                if emb is not None:
                    if emb == 0:
                        piece_ready(*{"mix_norm0": (Numbers("hg_out"), 9), "mix_norm1": (Numbers("gm_out"), 3)}[name])
                    embedding(0)
                transpose(0)
                if emb is not None:
                    embedding(1)
                for pc in range(8):
                    if pc < 7:
                        transpose(pc + 1)
                    if pc == 0:
                        pe.wait_ge(piece_hi, num.of("piece", 0) + 1)
                        in_unit(nxt, pc, x_lo_ready=lambda: piece_ready(num, job0))
                    else:
                        piece_ready(num, job0 + pc)
                        in_unit(nxt, pc)

            def piece_ready(num, job):
                pe.wait_ge(job_read[num.first("job", job) % 2], num.rounds("job", job, 2))

            pe.wait_ge(const_step, 6)
            pe.wait_ge(rows_loaded, 16 * 5)
            pe.transpose(scr[0][:, 0, 0:P], rows[:], ident[:]).then_inc(job_done, 1)
            first = Numbers("hg_first")
            operand("start", first)

            B = NT * HG

            def transpose_group(num, job, task):
                pair = num.first("task", task) % 2
                pe.wait_ge(acc_read[pair], num.rounds("task", task, 2))
                s = job_begin(num, job)
                for hd in range(HG):
                    for t in range(NT):
                        col = hd * T + t * P
                        i = pe.transpose(s[:, col // BLOCK, col % BLOCK:col % BLOCK + P],
                                         sg[:, t, hd * P:(hd + 1) * P], ident[:])
                i.then_inc(job_done, 1)

            def kq_wait(num, nth):
                pe.wait_ge(kq_ready, num.of("kq", nth) + 1)

            def diagonal(num, job, zq_job, kq):
                kq_wait(num, kq)
                pe.wait_ge(job_read[num.first("job", zq_job) % 2], num.rounds("job", zq_job, 2))
                s = job_begin(num, job)
                for b in range(B):
                    cs = slice(b * P, (b + 1) * P)
                    i = pe.matmul(s[:, b // HG, b % HG * P:(b % HG + 1) * P], k_g[:, cs], q_g[:, cs],
                                  start=True, stop=True)
                i.then_inc(job_done, 1)

            def level(num, lev, job, kq):
                kq_wait(num, kq)
                s = job_begin(num, job)
                seg = LEVELS[lev]
                for b in range(B):
                    odd = q_g[:, b * P:(b + 1) * P].rearrange("p (n two r) -> p n two r", two=2, r=seg)[:, :, 1, :]
                    i = pe.matmul(s[:, 0, b * P // 2:(b + 1) * P // 2], k_g[:, b * P:(b + 1) * P], odd,
                                  start=True, stop=True)
                i.then_inc(job_done, 1)

            def cross(num, job, kq):
                kq_wait(num, kq)
                s = job_begin(num, job)
                for hd in range(HG):
                    i = pe.matmul(s[:, 0, hd * P:(hd + 1) * P], k_g[:, hd * T:hd * T + P],
                                  q_g[:, hd * T + P:(hd + 1) * T], start=True, stop=True)
                i.then_inc(job_done, 1)

            def outputs(num, job, cross_job):
                pe.wait_ge(job_read[num.first("job", cross_job) % 2], num.rounds("job", cross_job, 2))
                s = job_begin(num, job)
                for hd in range(HG):
                    v0, v1 = (v_g[:, t, hd * P:(hd + 1) * P] for t in range(NT))
                    for t in range(NT):
                        b = NT * hd + t
                        dst = s[:, b // HG, b % HG * P:(b % HG + 1) * P]
                        i = pe.matmul(dst, att[:, b * P:(b + 1) * P], (v0, v1)[t], start=True, stop=t == 0)
                        if t == 1:
                            i = pe.matmul(dst, att_x[:, hd * P:(hd + 1) * P], v0, start=False, stop=True)
                i.then_inc(job_done, 1)

            def group_transposes(num, jobs):
                pe.wait_ge(hid_ready, num.of("grp", 0) + 1)
                for c2, job in enumerate(jobs):
                    transpose_piece(num, job, lambda c, t: hid[:, t, (KU * c2 + c) * P:(KU * c2 + c + 1) * P])

            def own_steps(num, zf, zq, diag, kq):
                return {11: [lambda: transpose_group(num, zf, 0)], 17: [lambda: transpose_group(num, zq, 1)],
                        26: [lambda: diagonal(num, diag, zq, kq)], 28: [lambda: level(num, 0, diag + 1, kq + 1)],
                        30: [lambda: level(num, 1, diag + 2, kq + 2)]}

            def in_units(num, ks, steps, **kw):
                for k in ks:
                    in_unit(num, k, **kw)
                    for step in steps.get(k, ()):
                        step()

            def out_units(num, steps, ready):
                for k, (t, q) in enumerate(OUT_ORDER):
                    if q in (6, 7) and t == 0:
                        piece_ready(num, ready[q - 6])
                    unit(num, k, t, y_hi, y_lo, KU * q, q == 0, q == 7)
                    for step in steps.get(k, ()):
                        step()

            in_units(first, range(8, 32), own_steps(first, 0, 1, 2, 0))
            with pe.Fori(0, 3) as it:
                num = Numbers("hg_loop", it)
                steps = own_steps(num, 6, 8, 11, 6)
                for lev in range(2, len(LEVELS)):
                    steps[2 * lev - 4] = [lambda lev=lev: level(num, lev, lev - 2, lev - 2)]
                steps[10] = [lambda: cross(num, 5, 5)]
                steps[13] = [lambda: outputs(num, 7, 5)]
                steps[22] = [lambda: group_transposes(num, (9, 10))]
                in_units(num, range(32), steps)
            num = Numbers("hg_out")

            def p_transposes(num, job, layer):
                pe.wait_ge(p_loaded, 16 * (layer + 1))
                transpose_piece(num, job, lambda c, t: p_tm[layer][:, t, c * P:(c + 1) * P])
            steps = {lev - 2: [lambda lev=lev: level(num, lev, lev - 2, lev - 2)] for lev in range(2, len(LEVELS))}
            steps[5] = [lambda: cross(num, 5, 5)]
            steps[7] = [lambda: outputs(num, 6, 5)]
            steps[10] = [lambda: group_transposes(num, (7, 8))]
            steps[14] = [lambda: p_transposes(num, 9, 0)]
            out_units(num, steps, (7, 8))

            def layer_tail(layer):
                s = str(layer)
                first, last, ple = Numbers("ffn_first" + s), Numbers("ffn_last" + s), Numbers("ple" + s)
                operand("mix_norm" + s, first, 0)
                in_units(first, range(8, 16), {})

                def hid_transposes(num, task, job):
                    pair = num.first("task", task) % 2
                    pe.wait_ge(acc_read[pair], num.rounds("task", task, 2))
                    for c2 in range(2):
                        transpose_piece(num, job + c2,
                                        lambda c, t: hid[:, t, (KU * c2 + c) * P:(KU * c2 + c + 1) * P])

                with pe.Fori(0, HB - 2) as it:
                    body = Numbers("ffn_loop" + s, it)
                    in_units(body, range(8), {4: [lambda: hid_transposes(body, -1, 0)]})
                    for job in range(2):
                        piece_ready(body, job)
                    for nb in range(NB):
                        for q in range(2):
                            unit(body, 8 + 2 * nb + q, 1 + nb, y_hi, y_lo, KU * q, q == 0, q == 1)
                    in_units(body, range(8), {}, unit0=16, task0=5)
                in_units(last, range(16), {4: [lambda: hid_transposes(last, -1, 0)]})
                for nb in range(NB):
                    for q in range(4):
                        if nb == 0 and q != 1:
                            for job in {0: (0, 1), 2: (2,), 3: (3,)}[q]:
                                piece_ready(last, job)
                        unit(last, 16 + 4 * nb + q, 2 + nb, y_hi, y_lo, KU * q, q == 0, q == 3)
                        if nb == 0 and q == 0:
                            hid_transposes(last, 1, 2)
                operand("ffn_norm" + s, ple, 2)
                in_units(ple, range(8, 32), {})

            layer_tail(0)

            gv, gu, go = Numbers("gm_v"), Numbers("gm_u"), Numbers("gm_out")
            operand("ple_norm0", gv)

            def ws_transposes(job):
                pe.wait_ge(ws_loaded, 16)
                s = job_begin(gv, job)
                for g in range(GC):
                    cs = slice((GC * job + g) * P, (GC * job + g + 1) * P)
                    i = pe.transpose(s[:, 0, g * P:(g + 1) * P], ws_raw[:, cs], ident[:])
                i.then_inc(job_done, 1)

            def spatial(num, job, nb):
                pe.wait_ge(ln_ready, nb + 1)
                s = job_begin(num, job)
                for g in range(GC):
                    cs = slice((GC * nb + g) * P, (GC * nb + g + 1) * P)
                    for t in range(NT):
                        i = pe.matmul(s[:, t, g * P:(g + 1) * P], wsT[:, cs], m[:, t, cs], start=True, stop=True)
                i.then_inc(job_done, 1)

            def gm_transposes(num, sv_job):
                piece_ready(num, sv_job)
                for c2 in range(2):
                    transpose_piece(num, sv_job + 1 + c2,
                                    lambda c, t: hid[:, t, (KU * c2 + c) * P:(KU * c2 + c + 1) * P])
            in_units(gv, range(8, 32), {12 + j: [lambda j=j: ws_transposes(j)] for j in range(NB)})
            in_units(gu, range(32), {8: [lambda: spatial(gu, 0, 0)], 12: [lambda: gm_transposes(gu, 0)],
                                     16: [lambda: spatial(gu, 3, 1)], 20: [lambda: gm_transposes(gu, 3)],
                                     24: [lambda: spatial(gu, 6, 2)], 28: [lambda: gm_transposes(gu, 6)]})
            out_units(go, {0: [lambda: spatial(go, 0, 3)], 4: [lambda: gm_transposes(go, 0)],
                           14: [lambda: p_transposes(go, 3, 1)]}, (1, 2))
            layer_tail(1)


_INS = ["x", "p", "hg_w_in", "hg_lb_logits", "hg_out_norm", "hg_w_out", "gm_w_in", "gm_ln_g", "gm_ln_b",
        "gm_w_s", "gm_b_s", "gm_w_out", "norm_mix_pre", "norm_mix_post", "norm_ffn_pre", "norm_ffn_post",
        "ffn_w_gate", "ffn_w_up", "ffn_w_down", "ple_w_proj", "ple_w_gate", "ple_norm"]


def kernel(**inputs):
    import numpy as np
    import concourse.bacc as bacc
    from concourse.bass_utils import run_bass_kernel_spmd

    nc = bacc.Bacc("TRN2", target_bir_lowering=False, num_devices=1)
    arrays, args = {}, []
    for name in _INS:
        a = np.ascontiguousarray(inputs[name])
        arrays[f"in_{name}"] = a
        args.append(nc.dram_tensor(f"in_{name}", a.shape, mybir.dt.from_np(a.dtype), kind="ExternalInput").ap())
    shape = inputs["x"].shape
    args.append(nc.dram_tensor("out_h", shape, mybir.dt.float32, kind="ExternalOutput").ap())
    trunk(nc, *args)
    r = run_bass_kernel_spmd(nc, [arrays], core_ids=[0])
    return r.results[0]["out_h"]
```

```python
import concourse.bass as bass
from concourse import mybir
from contextlib import ExitStack

P = 128
STAGES = 8
RING = 4
BLOCK = 512
KU = 2


KINDS = ("unit", "task", "job", "piece", "rstd", "kq", "grp")


def plan(phases):
    at, count = {}, dict.fromkeys(KINDS, 0)
    for name, times, *sizes in phases:
        at[name] = dict(count)
        for key, n in zip(KINDS, sizes):
            count[key] += times * n
    return at


def layer_tail_phases(layer):
    return [(name + str(layer), *sizes) for name, *sizes in (
        ("mix_norm", 1, 2, 2, 8, 8, 3),
        ("ffn_first", 1, 16, 2),
        ("ffn_loop", 9, 24, 6, 2, 2),
        ("ffn_last", 1, 32, 6, 4, 4),
        ("ffn_norm", 1, 2, 2, 8, 8, 2),
        ("ple", 1, 32, 4))]


PHASES = [
    ("start", 1, 0, 0, 10, 8, 1),
    ("hg_first", 1, 32, 4, 5, 0, 0, 3, 0),
    ("hg_loop", 3, 32, 4, 14, 2, 1, 9, 1),
    ("hg_out", 1, 32, 4, 10, 3, 1, 6, 1),
    *layer_tail_phases(0),
    ("ple_norm0", 1, 0, 0, 8, 8, 3),
    ("gm_v", 1, 32, 4, 4),
    ("gm_u", 1, 32, 4, 9, 6, 1),
    ("gm_out", 1, 32, 4, 4, 3),
    *layer_tail_phases(1),
    ("ple_norm1", 1, 0, 0, 0, 0, 2),
]
AT = plan(PHASES)
SIZE = {name: dict(zip(KINDS, [*sizes, *[0] * (len(KINDS) - len(sizes))])) for name, _, *sizes in PHASES}
NORMS = {name: n for n, name in enumerate(
    ["mix_norm0", "ffn_norm0", "ple_norm0", "mix_norm1", "ffn_norm1", "ple_norm1"])}
PRE_NORMS = {name: n for n, name in enumerate(["start", "mix_norm0", "ple_norm0", "mix_norm1"])}
SS_STEPS = 5
H_STEPS = 5
GAINS = {name: n for n, name in enumerate(["mix0", "ffn0", "ple0", "ln", "mix1", "ffn1", "ple1"])}


class Numbers:

    def __init__(self, phase, it=0):
        self.at, self.size, self.it = AT[phase], SIZE[phase], it

    def of(self, kind, k):
        base = self.at[kind] + k
        return base if isinstance(self.it, int) and self.it == 0 else self.it * self.size[kind] + base

    def first(self, kind, k):
        return self.at[kind] + k

    def rounds(self, kind, k, ring):
        base = self.first(kind, k) // ring + 1
        if isinstance(self.it, int) and self.it == 0:
            return base
        assert self.size[kind] % ring == 0
        return self.it * (self.size[kind] // ring) + base


def trunk(nc, x, p, hg_w_in, hg_lb_logits, hg_out_norm, hg_w_out, gm_w_in, gm_ln_g, gm_ln_b, gm_w_s,
          gm_b_s, gm_w_out, norm_mix_pre, norm_mix_post, norm_ffn_pre, norm_ffn_post, ffn_w_gate,
          ffn_w_up, ffn_w_down, ple_w_proj, ple_w_gate, ple_norm, out):
    f32, f32r, i32 = mybir.dt.float32, mybir.dt.float32r, mybir.dt.int32
    ALU, ACT, AX = mybir.AluOpType, mybir.ActivationFunctionType, mybir.AxisListType

    D = x.shape[2]
    T = x.shape[1]
    NT = T // P
    KT = D // P
    NB = D // BLOCK
    HB = ffn_w_gate.shape[2] // BLOCK
    HD = hg_out_norm.shape[1]
    HG = BLOCK // HD
    GC = BLOCK // P
    LEVELS = [1 << i for i in range(7)]
    EPS, LB_FLOOR = 1e-6, 1e-30
    UW = KU * BLOCK
    PLE_K = p.shape[3] // P
    assert (D, T, HB, HD, PLE_K) == (2048, 256, 11, P, KU)

    ctx = ExitStack()
    with ctx:
        def sb(name, shape, dt=f32):
            return ctx.enter_context(nc.sbuf_tensor(name, shape, dt))

        def pb(name):
            return ctx.enter_context(nc.psum_tensor(name, [P, NT, BLOCK], f32))

        def sem(name):
            return ctx.enter_context(nc.semaphore(name))

        stage = sb("stage", [P, STAGES, UW])
        w_hi = sb("w_hi", [P, RING, UW], f32r)
        w_lo = sb("w_lo", [P, RING, UW], f32r)
        h = sb("h", [P, NT, D])
        m = sb("m", [P, NT, D])
        e = sb("e", [P, NT, D])
        a_hi = sb("a_hi", [P, KT, T], f32r)
        a_lo = sb("a_lo", [P, KT, T], f32r)
        y_hi = sb("y_hi", [P, KT, T], f32r)
        y_lo = sb("y_lo", [P, KT, T], f32r)
        p_hi = sb("p_hi", [P, PLE_K, T], f32r)
        p_lo = sb("p_lo", [P, PLE_K, T], f32r)
        gain = sb("gain", [P, D])
        sg = sb("sg", [P, NT, BLOCK])
        hid = sb("hid", [P, NT, BLOCK])
        zg = sb("zg", [P, NT, BLOCK])
        ident = sb("ident", [P, P])
        level_mask = sb("level_mask", [P, len(LEVELS), P // 2])
        upper = sb("upper", [P, P])
        rows = sb("rows", [P, P])
        cols = sb("cols", [P, P])
        junk = zg
        ss = sb("ss", [P, NT, NB])
        hss = sb("hss", [P, NT, NB])
        ss_part = sb("ss_part", [P, NT])
        ms = sb("ms", [P, NT * HG])
        minus_half = sb("minus_half", [P, NT * HG])
        r_post = sb("r_post", [P, NT])
        r_pre = sb("r_pre", [P, NT])
        r_head = sb("r_head", [P, NT * HG])
        lb = sb("lb", [P, 6, KT])
        bn = sb("bn", [P, NT, NB, 6])
        mv = sb("mv", [P, NT, 2])
        f_g, k_g, q_g, tot = m[:, 0, 0:1024], m[:, 0, 1024:2048], m[:, 1, 0:1024], m[:, 1, 1024:2048]
        v_g = e[:, 0, 0:1024].rearrange("p (t n) -> p t n", t=NT)
        att = e[:, 0, 1024:2048]
        att_x = e[:, 1, 0:512]
        osq = e[:, 1, 1024:2048]
        ws_raw, wsT, ln_b = e[:, 0, :], e[:, 1, :], e[:, 0, :]
        p_tm = [a.rearrange("p (t d) -> p t d", t=NT) for a in (e[:, 1, 512:1024], e[:, 0, 1536:2048])]

        C_MIX, C_FFN = (0, 16), (32, 48)
        C_LB, C_BS, C_ON = 64, 80, 96

        acc = [pb("acc0"), pb("acc1")]
        scr = [pb("scr0"), pb("scr1")]

        w_loaded = [sem(f"w_loaded{s}") for s in range(STAGES)]
        w_hi_ready = sem("w_hi_ready")
        w_lo_ready = sem("w_lo_ready")
        w_used = sem("w_used")
        acc_read = [sem("acc_read0"), sem("acc_read1")]
        job_done = sem("job_done")
        job_read = [sem("job_read0"), sem("job_read1")]
        piece_hi = sem("piece_hi")
        mix_rows_loaded = sem("mix_rows_loaded")
        rows_loaded = sem("rows_loaded")
        const_step = sem("const_step")
        x_loaded = [sem(f"x_loaded{nb}") for nb in range(NB)]
        gain_loaded = sem("gain_loaded")
        p_loaded = sem("p_loaded")
        ws_loaded = sem("ws_loaded")
        ln_b_loaded = sem("ln_b_loaded")
        lb_step = sem("lb_step")
        kq_ready = sem("kq_ready")
        osq_ready = sem("osq_ready")
        hid_ready = sem("hid_ready")
        h_ready = sem("h_ready")
        tile_done = sem("tile_done")
        gate_ready = sem("gate_ready")
        tail_made = sem("tail_made")
        m_ready = sem("m_ready")
        ln_ready = sem("ln_ready")
        ss_ready = sem("ss_ready")
        hss_ready = sem("hss_ready")
        ms_ready = sem("ms_ready")
        rstd_ready = sem("rstd_ready")
        m_zeroed = sem("m_zeroed")
        gain_free = sem("gain_free")
        out_stored = sem("out_stored")

        block = ctx.enter_context(nc.Block())

        def unit_src(w, k0, n0):
            return w[k0 * P:(k0 + KU) * P, bass.ds(n0, BLOCK)].rearrange("(k p) n -> p k n", p=P)

        OUT_ORDER = ([(0, q) for q in range(6)] + [(1, q) for q in range(6)]
                     + [(0, 6), (0, 7), (1, 6), (1, 7)] + [(t, q) for t in (2, 3) for q in range(8)])
        IN_ORDER = [(t, q) for t in range(4) for q in range(8)]

        @block.sync
        def _(sp):
            def load(num, k, src):
                if num.first("unit", k) >= STAGES:
                    sp.wait_ge(w_lo_ready, num.of("unit", k) + 1 - STAGES)
                s = num.first("unit", k) % STAGES
                sp.dma_start(stage[:, s, :].rearrange("p (k n) -> p k n", k=KU), src).then_inc(w_loaded[s], 16)

            def load_x(nb):
                cs = slice(nb * BLOCK, (nb + 1) * BLOCK)
                sp.dma_start(h[:, :, cs], x[0].rearrange("(t p) d -> p t d", p=P)[:, :, cs]) \
                    .then_inc(x_loaded[nb], 16)
            def load_rows(row, src):
                sp.dma_start(rows[row:row + src.shape[0], :], src).then_inc(rows_loaded, 16)

            load_x(0)
            w = hg_w_in[0]
            order = (1, 0, 2, 3)
            for k, (t, q) in enumerate(IN_ORDER):
                load(Numbers("hg_first"), k, unit_src(w, KU * q, order[t] * D))
                if k < NB - 1:
                    load_x(k + 1)
                if k == STAGES - 1:
                    sp.wait_ge(const_step, 1)
                    for row, src in ((C_FFN[0], norm_ffn_pre), (C_LB, hg_lb_logits)):
                        load_rows(row, src.rearrange("l (k p) -> (l k) p", p=P))
                    load_rows(C_BS, gm_b_s[0])
                    load_rows(C_ON, hg_out_norm)
            with sp.Fori(0, 3) as it:
                for k, (t, q) in enumerate(IN_ORDER):
                    load(Numbers("hg_loop", it), k, unit_src(w, KU * q, it * BLOCK + (order[t] * D + BLOCK)))

            def second_projection(phase, w):
                for k, (t, q) in enumerate(OUT_ORDER):
                    load(Numbers(phase), k, unit_src(w, KU * q, t * BLOCK))

            def embedding(layer, phase, nb0):
                for nb in (nb0, nb0 + 1):
                    load(Numbers(phase), nb - nb0, unit_src(ple_w_proj[layer], 0, nb * BLOCK))

            def layer_tail(layer):
                s = str(layer)
                gate, up, down = ffn_w_gate[layer], ffn_w_up[layer], ffn_w_down[layer]
                embedding(layer, "mix_norm" + s, 0)
                for k in range(8):
                    load(Numbers("ffn_first" + s), k, unit_src(gate, KU * k, 0))
                for k in range(8):
                    load(Numbers("ffn_first" + s), 8 + k, unit_src(up, KU * k, 0))
                with sp.Fori(0, HB - 2) as it:
                    num = Numbers("ffn_loop" + s, it)
                    for k in range(8):
                        load(num, k, unit_src(gate, KU * k, it * BLOCK + BLOCK))
                    for k in range(8):
                        rows_ = bass.ds(it * BLOCK + (k % 2) * KU * P, KU * P)
                        load(num, 8 + k, down[rows_, (k // 2) * BLOCK:(k // 2 + 1) * BLOCK]
                             .rearrange("(k p) n -> p k n", p=P))
                    for k in range(8):
                        load(num, 16 + k, unit_src(up, KU * k, it * BLOCK + BLOCK))
                num = Numbers("ffn_last" + s)
                for k in range(8):
                    load(num, k, unit_src(gate, KU * k, (HB - 1) * BLOCK))
                for k in range(8):
                    load(num, 8 + k, unit_src(up, KU * k, (HB - 1) * BLOCK))
                for k in range(16):
                    load(num, 16 + k, unit_src(down, (HB - 2) * BLOCK // P + KU * (k % 4), (k // 4) * BLOCK))
                embedding(layer, "ffn_norm" + s, 2)
                for k, (t, q) in enumerate(IN_ORDER):
                    load(Numbers("ple" + s), k, unit_src(ple_w_gate[layer], KU * q, t * BLOCK))

            second_projection("hg_out", hg_w_out[0])
            layer_tail(0)
            for phase, half in (("gm_v", 1), ("gm_u", 0)):
                for k, (t, q) in enumerate(IN_ORDER):
                    load(Numbers(phase), k, unit_src(gm_w_in[0], KU * q, half * D + t * BLOCK))
            second_projection("gm_out", gm_w_out[0])
            layer_tail(1)
            for nb in range(NB):
                sp.wait_ge(h_ready, H_STEPS * NORMS["ple_norm1"] + nb + 2)
                sp.dma_start(out[0].rearrange("(t p) d -> p t d", p=P)[:, :, nb * BLOCK:(nb + 1) * BLOCK],
                             h[:, :, nb * BLOCK:(nb + 1) * BLOCK]).then_inc(out_stored, 16)
            sp.wait_ge(out_stored, 16 * NB)

        @block.gpsimd
        def _(pool):
            pool.memset(rows[:], 0.0).then_inc(const_step, 1)
            pool.memset(ident[:], 0.0).then_inc(const_step, 1)
            pool.memset(minus_half[:], -0.5).then_inc(const_step, 1)
            pool.memset(upper[:], 1.0).then_inc(const_step, 1)
            pool.memset(level_mask[:], 1.0).then_inc(const_step, 1)
            pool.wait_ge(const_step, 5)
            pool.affine_select(out=ident[:], in_=ident[:], compare_op=ALU.not_equal, fill=1.0, base=0,
                               pattern=[[-1, P]], channel_multiplier=1).then_inc(const_step, 1)
            pool.affine_select(out=upper[:], in_=upper[:], compare_op=ALU.is_ge, fill=0.0, base=0,
                               pattern=[[1, P]], channel_multiplier=-1).then_inc(const_step, 1)
            for i, seg in enumerate(LEVELS):
                cells = level_mask[:, i, :].rearrange("p (n r) -> p n r", r=seg)
                pool.affine_select(out=cells, in_=cells, compare_op=ALU.is_ge, fill=0.0, base=0,
                                   pattern=[[-2 * seg, P // 2 // seg], [0, seg]],
                                   channel_multiplier=1).then_inc(const_step, 1)
            pool.wait_ge(const_step, 14)
            for i, seg in enumerate(LEVELS):
                cells = level_mask[:, i, :].rearrange("p (n r) -> p n r", r=seg)
                pool.affine_select(out=cells, in_=cells, compare_op=ALU.is_ge, fill=0.0, base=seg - 1,
                                   pattern=[[2 * seg, P // 2 // seg], [0, seg]],
                                   channel_multiplier=-1).then_inc(const_step, 1)

            def power(num, k, dst, n, first=0):
                pool.wait_ge(ms_ready, num.of("rstd", k) + 1)
                pool.tensor_tensor(out=dst, in0=ms[:, first:first + n], in1=minus_half[:, 0:n], op=ALU.pow) \
                    .then_inc(rstd_ready, 1)

            def post_powers(name):
                for t in range(NT):
                    power(Numbers(name), t, r_post[:, t:t + 1], 1, t)

            power(Numbers("start"), 0, r_pre[:], NT)
            with pool.Fori(0, 3) as it:
                power(Numbers("hg_loop", it), 0, r_head[:], NT * HG)
            power(Numbers("hg_out"), 0, r_head[:], NT * HG)

            def layer_tail(layer):
                s = str(layer)
                post_powers("mix_norm" + s)
                pool.wait_ge(h_ready, H_STEPS * (NORMS["mix_norm" + s] + 1))
                pool.memset(m[:], 0.0).then_inc(m_zeroed, 1)
                power(Numbers("mix_norm" + s), NT, r_pre[:], NT)
                post_powers("ffn_norm" + s)
                post_powers("ple_norm" + s)

            layer_tail(0)
            power(Numbers("ple_norm0"), NT, r_pre[:], NT)
            power(Numbers("gm_u"), 0, r_head[:, 0:NT], NT)
            layer_tail(1)

        def steps_of(text):
            return [(word[0], int(word[1:])) for word in text.split()]
        BOUNDARY = {
            "start": steps_of("s0 p0 p1 s1 s2 p2 q0 s3 p3 s4 p4 q1 s5 p5 s6 p6 q2 s7 p7 q3"),
            "plain": steps_of("p0 u1 p1 s2 s3 p2 u2 s4 q0 p3 s5 p4 s6 q1 u3 p5 s7 p6 q2 p7 q3"),
            "emb": steps_of("s3 p0 s4 u1 p1 s5 p2 q0 u2 s6 p3 s7 p4 q1 u3 s8 p5 s9 p6 q2 p7 q3"),
        }

        def boundary_split(split, num, nxt, i, emb):
            if emb and i < 2:
                split(num, i)
            else:
                split(nxt, i - 2 if emb else i)

        def boundary_splits(split, num, nxt, which, emb):
            for i in which:
                boundary_split(split, num, nxt, i, emb)

        TAIL_MADE = {"ffn_norm0": 1, "ple_norm0": 3, "ffn_norm1": 4, "ple_norm1": 6}

        @block.scalar
        def _(act):
            def split(num, k):
                s, r = num.first("unit", k) % STAGES, num.first("unit", k) % RING
                act.wait_ge(w_loaded[s], 16 * num.rounds("unit", k, STAGES))
                if num.first("unit", k) >= RING:
                    act.wait_ge(w_used, num.of("unit", k) + 1 - RING)
                act.activation(w_hi[:, r, :], stage[:, s, :], ACT.Copy).then_inc(w_hi_ready, 1)

            def units(num, ks, steps):
                for k in ks:
                    split(num, k)
                    for step in steps.get(k, ()):
                        step()

            def take(num, task, last_unit, dst, func, scale=1.0):
                act.wait_ge(w_used, num.of("unit", last_unit) + 1)
                pair = num.first("task", task) % 2
                for t in range(NT):
                    i = act.activation(dst[:, t, :], acc[pair][:, t, :], func,
                                       scale=r_pre[:, t:t + 1] if scale is None else scale)
                i.then_inc(acc_read[pair], 1)

            def piece(num, job, hi, scales=None):
                act.wait_ge(job_done, num.of("job", job) + 1)
                src = scr[num.first("job", job) % 2][:, 0, :]
                if scales is None:
                    i = act.activation(hi.rearrange("p k t -> p (k t)"), src, ACT.Copy)
                else:
                    for c in range(KU):
                        i = act.activation(hi[:, c, :], src[:, c * T:(c + 1) * T], ACT.Copy,
                                           scale=scales[:, c:c + 1])
                i.then_inc(piece_hi, 1)

            def square_block(src, sums, nb, done=None):
                act.drain()
                for t in range(NT):
                    i = act.activation(junk[:, t, :], src[:, t, nb * BLOCK:(nb + 1) * BLOCK], ACT.Square,
                                       accum_out=sums[:, t, nb:nb + 1])
                if done is not None:
                    i.then_inc(done, 1)

            def m_squares(num, task, nb):
                act.wait_ge(acc_read[num.first("task", task) % 2], num.rounds("task", task, 2))
                square_block(m, ss, nb, ss_ready)

            def load_gain(vec):
                act.dma_start(gain[:], vec.rearrange("(a n) -> a n", a=1).broadcast_to([P, D])) \
                    .then_inc(gain_loaded, 16)

            def operand(name, nxt, scale_col, emb=()):
                num, job0 = Numbers(name), 1 if name == "start" else 0
                for what, i in BOUNDARY["start" if name == "start" else "emb" if emb else "plain"]:
                    if what == "s":
                        boundary_split(split, num, nxt, i, emb)
                        if emb and i == 3:
                            emb[0]()
                    elif what == "p":
                        piece(num, job0 + i, a_hi[:, KU * i:KU * i + KU, :],
                              None if scale_col is None else cols[:, scale_col + KU * i:scale_col + KU * i + KU])
                        if emb and i == 1:
                            emb[1]()
                    elif what == "q" and scale_col is not None:
                        if name == "start":
                            act.wait_ge(x_loaded[i], 16)
                        square_block(h, hss, i, hss_ready if i == NB - 1 else None)

            act.wait_ge(const_step, 1)
            act.dma_start(rows[C_MIX[0]:C_FFN[0], :], norm_mix_pre.rearrange("l (k p) -> (l k) p", p=P)) \
                .then_inc(mix_rows_loaded, 16)
            first = Numbers("hg_first")
            act.wait_ge(job_done, 1)
            act.activation(cols[:, 0:C_FFN[0]], scr[0][:, 0, 0:C_FFN[0]], ACT.Copy).then_inc(job_read[0], 1)
            act.wait_ge(job_read[0], 1)
            operand("start", first, C_MIX[0])

            def other_cols():
                start = Numbers("start")
                act.wait_ge(job_done, start.of("job", 9) + 1)
                act.activation(cols[:, C_FFN[0]:], scr[1][:, 0, C_FFN[0]:P], ACT.Copy).then_inc(job_read[1], 1)

            def exp_logits():
                act.wait_ge(lb_step, 1)
                act.activation(lb[:, 1, :], lb[:, 0, :], ACT.Exp).then_inc(lb_step, 1)

            def flat(pair):
                return scr[pair][:].rearrange("p t n -> p (t n)")

            def gates(num, job):
                act.wait_ge(job_done, num.of("job", job) + 1)
                pair = num.first("job", job) % 2
                act.activation(f_g, flat(pair), ACT.Sigmoid)
                act.activation(k_g, flat(pair), ACT.Sigmoid, scale=-1.0).then_inc(job_read[pair], 1)

            def query(num, job):
                act.wait_ge(job_done, num.of("job", job) + 1)
                pair = num.first("job", job) % 2
                act.activation(q_g, flat(pair), ACT.Silu).then_inc(job_read[pair], 1)

            def out_squares(num, job):
                act.wait_ge(job_done, num.of("job", job) + 1)
                act.activation(osq, flat(num.first("job", job) % 2), ACT.Square).then_inc(osq_ready, 1)

            def y_pieces(num, jobs, kt0):
                for c, job in enumerate(jobs):
                    act.wait_ge(job_done, num.of("job", job) + 1)
                    act.activation(y_hi[:, bass.ds(kt0 + KU * c, KU), :].rearrange("p k t -> p (k t)"),
                                   scr[num.first("job", job) % 2][:, 0, :], ACT.Copy,
                                   scale=cols[:, C_ON:C_ON + 1]).then_inc(piece_hi, 1)

            def own_steps(num, zf_job, zq_job):
                return {10: [lambda: take(num, 0, 7, sg, ACT.Copy, None)],
                        15: [lambda: gates(num, zf_job)],
                        18: [lambda: take(num, 1, 15, sg, ACT.Copy, None)],
                        21: [lambda: query(num, zq_job)],
                        26: [lambda: take(num, 2, 23, v_g, ACT.Copy, None)]}

            def pre_factor_ready(name, k):
                act.wait_ge(rstd_ready, Numbers(name).of("rstd", k) + 1)

            def load_first():
                load_gain(norm_mix_post[0])
                act.dma_start(p_tm[0], p[0, 0].rearrange("(t p) d -> p t d", p=P)).then_inc(p_loaded, 16)
            steps = own_steps(first, 0, 1)
            steps[10].insert(0, lambda: pre_factor_ready("start", 0))
            steps[11], steps[12], steps[13] = [other_cols], [load_first], [exp_logits]
            units(first, range(8, 32), steps)
            with act.Fori(0, 3) as it:
                num = Numbers("hg_loop", it)
                steps = own_steps(num, 6, 8)
                steps[2] = [lambda: take(num, -1, -1, zg, ACT.Silu, None)]
                steps[16] = [lambda: out_squares(num, 7)]
                steps[25] = [lambda: y_pieces(num, (9, 10), it * HG)]
                units(num, range(32), steps)
            out_num = Numbers("hg_out")
            units(out_num, range(32), {
                2: [lambda: take(out_num, -1, -1, zg, ACT.Silu, None)],
                11: [lambda: out_squares(out_num, 6)], 13: [lambda: y_pieces(out_num, (7, 8), 3 * HG)],
                17: [lambda: piece(out_num, 9, p_hi[:])],
                20: [lambda: m_squares(out_num, 0, 0)], 22: [lambda: m_squares(out_num, 1, 1)],
                29: [lambda: m_squares(out_num, 2, 2)]})

            def layer_tail(layer, out_num):
                s = str(layer)
                mix, ffn = Numbers("mix_norm" + s), Numbers("ffn_norm" + s)
                first, last, ple = Numbers("ffn_first" + s), Numbers("ffn_last" + s), Numbers("ple" + s)

                def take_e(num, nb):
                    take(num, nb % 2, nb % 2, e[:, :, nb * BLOCK:(nb + 1) * BLOCK], ACT.Copy)

                def tail_square(t, src):
                    act.activation(junk[:, t, :], src, ACT.Square, accum_out=ss[:, t, NB - 1:NB]) \
                        .then_inc(ss_ready, 1)

                norm = "mix_norm" + s
                boundary_splits(split, mix, first, range(2), True)
                act.drain()
                pair = out_num.first("task", 3) % 2
                act.wait_ge(tile_done, NORMS[norm] + 1)
                tail_square(0, acc[pair][:, 0, :])
                boundary_split(split, mix, first, 2, True)
                act.wait_ge(w_used, out_num.of("unit", 31) + 1)
                tail_square(1, acc[pair][:, 1, :])
                operand("mix_norm" + s, first, C_FFN[layer], [lambda: take_e(mix, 0), lambda: take_e(mix, 1)])

                def load_gain_ffn():
                    act.wait_ge(acc_read[pair], out_num.rounds("task", 3, 2))
                    load_gain(norm_ffn_post[layer])
                units(first, range(8, 16), {9: [load_gain_ffn],
                                            10: [lambda: pre_factor_ready("mix_norm" + s, NT),
                                                 lambda: take(first, 0, 7, sg, ACT.Silu, None)]})

                def hid_pieces(num, job, kt):
                    for c in range(2):
                        piece(num, job + c, y_hi[:, kt + KU * c:kt + KU * c + KU, :])
                with act.Fori(0, HB - 2) as it:
                    body = Numbers("ffn_loop" + s, it)
                    units(body, range(24), {7: [lambda: hid_pieces(body, 0, 0)],
                                            10: [lambda: take(body, 0, 7, sg, ACT.Silu, None)]})
                units(last, range(32),
                      {7: [lambda: hid_pieces(last, 0, 0)], 10: [lambda: take(last, 0, 7, sg, ACT.Silu, None)],
                       18: [lambda: hid_pieces(last, 2, GC)],
                       24: [lambda: m_squares(last, 2, 0)], 28: [lambda: m_squares(last, 3, 1)],
                       31: [lambda: m_squares(last, 4, 2)]})

                norm = "ffn_norm" + s
                boundary_splits(split, ffn, ple, range(2), True)
                act.drain()
                act.wait_ge(tail_made, TAIL_MADE[norm])
                tail_square(0, m[:, 0, (NB - 1) * BLOCK:])
                boundary_split(split, ffn, ple, 2, True)
                act.wait_ge(acc_read[last.first("task", 5) % 2], last.rounds("task", 5, 2))
                tail_square(1, m[:, 1, (NB - 1) * BLOCK:])
                operand("ffn_norm" + s, ple, None, [lambda: take_e(ffn, 2), lambda: take_e(ffn, 3)])

                def load_gain_ple():
                    act.wait_ge(gain_free, 1 + 2 * layer)
                    load_gain(ple_norm[layer])

                def gate(nb):
                    if nb > 0:
                        act.wait_ge(m_ready, nb + (NB - 1) * layer)
                    take(ple, nb, 8 * nb + 7, sg, ACT.Sigmoid)

                def gated_squares(nb):
                    act.wait_ge(m_ready, nb + 1 + (NB - 1) * layer)
                    square_block(m, ss, nb, ss_ready)
                units(ple, range(8, 32), {9: [load_gain_ple],
                                          10: [lambda: gate(0)], 13: [lambda: gated_squares(0)],
                                          18: [lambda: gate(1)], 21: [lambda: gated_squares(1)],
                                          26: [lambda: gate(2)], 29: [lambda: gated_squares(2)]})

                norm = "ple_norm" + s
                if layer == 0:
                    boundary_splits(split, None, Numbers("gm_v"), range(2), False)
                act.drain()
                act.wait_ge(m_ready, NB - 1 + (NB - 1) * layer)
                pair = ple.first("task", 3) % 2
                for t in range(NT):
                    if t == 0:
                        act.wait_ge(tile_done, NORMS[norm] + 1)
                    else:
                        act.wait_ge(w_used, ple.of("unit", 31) + 1)
                    act.activation(sg[:, t, :], acc[pair][:, t, :], ACT.Sigmoid) \
                        .then_inc((gate_ready, acc_read[pair])[t], 1)
                    act.wait_ge(tail_made, TAIL_MADE[norm] - 1 + t)
                    tail_square(t, m[:, t, (NB - 1) * BLOCK:])
                if layer == 0:
                    operand("ple_norm0", Numbers("gm_v"), C_MIX[1])

            layer_tail(0, out_num)

            gv, gu, go = Numbers("gm_v"), Numbers("gm_u"), Numbers("gm_out")

            def load_spatial():
                act.dma_start(ws_raw.rearrange("p (g s) -> p g s", g=KT), gm_w_s[0].rearrange("g t s -> t g s")) \
                    .then_inc(ws_loaded, 16)
                act.wait_ge(gain_free, 2)
                load_gain(gm_ln_g[0])

            def take_v(num, task, last_unit, nb):
                take(num, task, last_unit, m[:, :, nb * BLOCK:(nb + 1) * BLOCK], ACT.Gelu, None)

            def load_ln_b():
                act.wait_ge(job_read[gv.first("job", 3) % 2], gv.rounds("job", 3, 2))
                act.dma_start(ln_b, gm_ln_b[0].rearrange("(a n) -> a n", a=1).broadcast_to([P, D])) \
                    .then_inc(ln_b_loaded, 16)

            def take_u(num, task, last_unit, nb):
                if nb > 0:
                    job = 3 * (nb - 1)
                    act.wait_ge(job_read[gu.first("job", job) % 2], gu.rounds("job", job, 2))
                take(num, task, last_unit, sg, ACT.Gelu, None)

            def gm_pieces(num, jobs, nb):
                for c, job in enumerate(jobs):
                    piece(num, job, y_hi[:, GC * nb + KU * c:GC * nb + KU * c + KU, :])

            def load_gain_mix1():
                act.wait_ge(ln_ready, NB)
                load_gain(norm_mix_post[1])
                act.dma_start(p_tm[1], p[1, 0].rearrange("(t p) d -> p t d", p=P)).then_inc(p_loaded, 16)
            units(gv, range(8, 32), {9: [load_spatial],
                                     10: [lambda: pre_factor_ready("ple_norm0", NT), lambda: take_v(gv, 0, 7, 0)],
                                     18: [lambda: take_v(gv, 1, 15, 1)],
                                     20: [load_ln_b], 26: [lambda: take_v(gv, 2, 23, 2)]})
            units(gu, range(32), {2: [lambda: take_v(gu, -1, -1, 3)],
                                  10: [lambda: take_u(gu, 0, 7, 0)], 15: [lambda: gm_pieces(gu, (1, 2), 0)],
                                  17: [load_gain_mix1],
                                  18: [lambda: take_u(gu, 1, 15, 1)], 23: [lambda: gm_pieces(gu, (4, 5), 1)],
                                  26: [lambda: take_u(gu, 2, 23, 2)], 31: [lambda: gm_pieces(gu, (7, 8), 2)]})
            units(go, range(32), {2: [lambda: take_u(go, -1, -1, 3)], 7: [lambda: gm_pieces(go, (1, 2), 3)],
                                  17: [lambda: piece(go, 3, p_hi[:])],
                                  20: [lambda: m_squares(go, 0, 0)], 22: [lambda: m_squares(go, 1, 1)],
                                  29: [lambda: m_squares(go, 2, 2)]})
            layer_tail(1, go)

        @block.vector
        def _(dve):
            def split(num, k):
                s, r = num.first("unit", k) % STAGES, num.first("unit", k) % RING
                dve.wait_ge(w_hi_ready, num.of("unit", k) + 1)
                dve.tensor_tensor(out=w_lo[:, r, :], in0=stage[:, s, :], in1=w_hi[:, r, :].bitcast(f32),
                                  op=ALU.subtract).then_inc(w_lo_ready, 1)

            def units(num, ks, steps):
                for k in ks:
                    split(num, k)
                    for step in steps.get(k, ()):
                        step()

            def piece(num, nth, job, hi, lo, scales=None):
                dve.wait_ge(piece_hi, num.of("piece", nth) + 1)
                pair = num.first("job", job) % 2
                src = scr[pair][:, 0, :]
                if scales is None:
                    i = dve.tensor_tensor(out=lo.rearrange("p k t -> p (k t)"), in0=src,
                                          in1=hi.rearrange("p k t -> p (k t)").bitcast(f32), op=ALU.subtract)
                else:
                    for c in range(KU):
                        i = dve.scalar_tensor_tensor(out=lo[:, c, :], in0=src[:, c * T:(c + 1) * T],
                                                     scalar=scales[:, c:c + 1], in1=hi[:, c, :].bitcast(f32),
                                                     op0=ALU.mult, op1=ALU.subtract)
                i.then_inc(job_read[pair], 1)

            def mean_squares(sums, n, count):
                dve.tensor_reduce(ms[:, 0:n], sums, AX.X, ALU.add)
                dve.drain()
                dve.tensor_scalar(ms[:, 0:n], ms[:, 0:n], 1.0 / count, EPS, ALU.mult, ALU.add).then_inc(ms_ready, 1)

            def operand(name, nxt, scale_col, update, emb=False):
                num, job0 = Numbers(name), 1 if name == "start" else 0
                update(0)
                if emb:
                    boundary_split(split, num, nxt, 2, emb)
                for what, i in BOUNDARY["start" if name == "start" else "emb" if emb else "plain"]:
                    if what == "s":
                        boundary_split(split, num, nxt, i, emb)
                    elif what == "u":
                        update(i)
                    elif what == "p":
                        piece(num, i, job0 + i, a_hi[:, KU * i:KU * i + KU, :], a_lo[:, KU * i:KU * i + KU, :],
                              None if scale_col is None else cols[:, scale_col + KU * i:scale_col + KU * i + KU])

            def pre_factor(name):
                dve.wait_ge(hss_ready, PRE_NORMS[name] + 1)
                mean_squares(hss[:], NT, D)

            def gain_of(nb):
                return gain[:, nb * BLOCK:(nb + 1) * BLOCK].unsqueeze(1).broadcast_to([P, NT, BLOCK])

            def blk_of(x_, nb):
                return x_[:, :, nb * BLOCK:(nb + 1) * BLOCK]

            def wait_gain(norm):
                dve.wait_ge(gain_loaded, 16 * (GAINS[norm.replace("_norm", "")] + 1))

            def times_gain(norm, nb):
                dve.wait_ge(ss_ready, SS_STEPS * NORMS[norm] + nb + 1)
                wait_gain(norm)
                dve.tensor_tensor(out=blk_of(m, nb), in0=blk_of(m, nb), in1=gain_of(nb), op=ALU.mult)
                if nb == NB - 2:
                    dve.tensor_reduce(ss_part[:], ss[:, :, 0:NB - 1], AX.X, ALU.add)
                    dve.drain()
                    dve.tensor_scalar(ss_part[:], ss_part[:], 1.0 / D, EPS, ALU.mult, ALU.add)

            def mean_square(norm, t):
                dve.wait_ge(ss_ready, SS_STEPS * NORMS[norm] + NB + t)
                dve.scalar_tensor_tensor(out=ms[:, t:t + 1], in0=ss[:, t, NB - 1:NB], scalar=1.0 / D,
                                         in1=ss_part[:, t:t + 1], op0=ALU.mult, op1=ALU.add).then_inc(ms_ready, 1)

            LAST = slice((NB - 1) * BLOCK, NB * BLOCK)

            def tile_wait(norm, num, t):
                if t == 0:
                    dve.wait_ge(tile_done, NORMS[norm] + 1)
                else:
                    dve.wait_ge(w_used, num.of("unit", 31) + 1)

            def last_tile_gain(t):
                return dve.tensor_tensor(out=hid[:, t, :], in0=m[:, t, LAST], in1=gain[:, LAST], op=ALU.mult)

            def tail_out(norm, num):
                wait_gain(norm)
                dve.drain()
                pair = num.first("task", 3) % 2
                for t in range(NT):
                    mean_square(norm, t)
                    i = dve.tensor_tensor(out=hid[:, t, :], in0=acc[pair][:, t, :], in1=gain[:, LAST], op=ALU.mult)
                    if t == 0:
                        add_tile(norm, 0, 0)
                        add_tile(norm, 1, 0)
                i.then_inc(acc_read[pair], 1)

            def tail_down(norm, num):
                wait_gain(norm)
                dve.drain()
                pair = num.first("task", 5) % 2
                for t in range(NT):
                    tile_wait(norm, num, t)
                    i = dve.tensor_tensor(out=m[:, t, LAST], in0=acc[pair][:, t, :], in1=m[:, t, LAST], op=ALU.add)
                    i.then_inc((tail_made, acc_read[pair])[t], 1)
                    dve.drain()
                    i = last_tile_gain(t)
                    mean_square(norm, t)
                    add_tile(norm, t, 0)
                i.then_inc(gain_free, 1)

            def tail_gated(norm, ple):
                wait_gain(norm)
                dve.drain()
                pair = ple.first("task", 3) % 2
                for t in range(NT):
                    if t == 0:
                        dve.wait_ge(gate_ready, int(norm[-1]) + 1)
                    else:
                        dve.wait_ge(acc_read[pair], ple.rounds("task", 3, 2))
                    dve.tensor_tensor(out=m[:, t, LAST], in0=e[:, t, LAST], in1=sg[:, t, :], op=ALU.mult) \
                        .then_inc(tail_made, 1)
                    dve.drain()
                    i = last_tile_gain(t)
                    mean_square(norm, t)
                i.then_inc(gain_free, 1)
                add_tile(norm, 0, 0)

            def add(norm, cs, t):
                src = hid[:, t, :] if cs == LAST else m[:, t, cs]
                return dve.scalar_tensor_tensor(out=h[:, t, cs], in0=src, scalar=r_post[:, t:t + 1],
                                                in1=h[:, t, cs], op0=ALU.mult, op1=ALU.add)

            def add_tile(norm, nb, t):
                dve.wait_ge(rstd_ready, Numbers(norm).of("rstd", t) + 1)
                add(norm, slice(nb * BLOCK, (nb + 1) * BLOCK), t)

            def add_block(norm, ahead):
                def update(nb):
                    if nb == 0:
                        dve.wait_ge(rstd_ready, Numbers(norm).of("rstd", 1) + 1)
                    width = BLOCK // 2 if nb == 0 else BLOCK
                    for c0 in range(nb * BLOCK, (nb + 1) * BLOCK, width):
                        for t in range(1 if nb < ahead else 0, NT):
                            i = add(norm, slice(c0, c0 + width), t)
                        i.then_inc(h_ready, 1)
                return update

            def take_m(num, task, last_unit, nb, add=False):
                dve.wait_ge(w_used, num.of("unit", last_unit) + 1)
                pair = num.first("task", task) % 2
                if add:
                    i = dve.tensor_tensor(out=blk_of(m, nb), in0=acc[pair][:], in1=blk_of(m, nb), op=ALU.add)
                else:
                    i = dve.tensor_copy(blk_of(m, nb), acc[pair][:])
                i.then_inc(acc_read[pair], 1)

            first = Numbers("hg_first")
            operand("start", first, C_MIX[0], lambda nb: None)
            units(first, range(8, 10), {})
            pre_factor("start")
            units(first, range(10, 12), {})
            dve.wait_ge(job_read[1], Numbers("start").rounds("job", 9, 2))
            logits = cols[:, C_LB:C_LB + KT]
            dve.tensor_tensor(out=lb[:, 0, :], in0=logits, in1=logits, op=ALU.subtract).then_inc(lb_step, 1)
            units(first, range(12, 14), {})
            dve.wait_ge(lb_step, 2)
            dve.reciprocal(lb[:, 2, :], lb[:, 1, :])
            dve.drain()
            dve.tensor_tensor(out=lb[:, 3, :], in0=lb[:, 1, :], in1=lb[:, 2, :], op=ALU.mult)
            dve.drain()
            dve.tensor_tensor(out=lb[:, 4, :], in0=lb[:, 3, :], in1=lb[:, 3, :], op=ALU.subtract)
            dve.drain()
            lb_low, lb_rest = lb[:, 5, :], lb[:, 0, :]
            dve.tensor_scalar(lb_low, lb[:, 4, :], LB_FLOOR, None, ALU.max)
            dve.tensor_scalar(lb_rest, lb[:, 4, :], -1.0, 1.0, ALU.mult, ALU.add)
            dve.drain()

            TOT = {1: f_g}
            at = 0
            for seg in LEVELS[1:]:
                n = HG * T // seg
                TOT[seg] = tot[:, at:at + n]
                at += n

            def fk(num, zf_job, group):
                dve.wait_ge(job_read[num.first("job", zf_job) % 2], num.rounds("job", zf_job, 2))
                for hd in range(HG):
                    col = bass.ds(group * HG + hd, 1)
                    dve.tensor_scalar(f_g[:, hd * T:(hd + 1) * T], f_g[:, hd * T:(hd + 1) * T],
                                      lb_rest[:, col], lb_low[:, col], ALU.mult, ALU.add)
                for hd in range(HG):
                    col = bass.ds(group * HG + hd, 1)
                    i = dve.tensor_scalar(k_g[:, hd * T:(hd + 1) * T], k_g[:, hd * T:(hd + 1) * T],
                                          lb_rest[:, col], None, ALU.mult)
                i.then_inc(kq_ready, 1)

            def totals():
                for seg in LEVELS[1:]:
                    dve.drain()
                    halves = TOT[seg // 2].rearrange("p (n two) -> p n two", two=2)
                    dve.tensor_tensor(out=TOT[seg], in0=halves[:, :, 0], in1=halves[:, :, 1], op=ALU.mult)

            def diagonal(num, job):
                dve.wait_ge(job_done, num.of("job", job) + 1)
                pair = num.first("job", job) % 2
                dve.tensor_tensor(out=q_g, in0=q_g, in1=f_g, op=ALU.mult).then_inc(kq_ready, 1)
                b = NT * HG
                dve.tensor_tensor(out=att.rearrange("p (b t) -> p b t", b=b),
                                  in0=scr[pair][:].rearrange("p two (b t) -> p (two b) t", t=P),
                                  in1=ident[:].unsqueeze(1).broadcast_to([P, b, P]), op=ALU.mult) \
                    .then_inc(job_read[pair], 1)

            def level(num, lev, job):
                seg = LEVELS[lev]
                pair = num.first("job", job) % 2
                dve.wait_ge(job_done, num.of("job", job) + 1)
                dve.wait_ge(job_read[1 - pair], num.rounds("job", job - 1, 2))
                q2 = q_g.rearrange("p (n two r) -> p n two r", two=2, r=seg)
                k2 = k_g.rearrange("p (n two r) -> p n two r", two=2, r=seg)
                t2 = TOT[seg].rearrange("p (n two) -> p n two", two=2)
                n = HG * T // (2 * seg)
                dve.tensor_tensor(out=q2[:, :, 1, :], in0=q2[:, :, 1, :],
                                  in1=t2[:, :, 0].unsqueeze(2).broadcast_to([P, n, seg]), op=ALU.mult)
                dve.tensor_tensor(out=k2[:, :, 0, :], in0=k2[:, :, 0, :],
                                  in1=t2[:, :, 1].unsqueeze(2).broadcast_to([P, n, seg]), op=ALU.mult) \
                    .then_inc(kq_ready, 1)
                b, ns = NT * HG, P // 2 // seg
                dve.copy_predicated(
                    att.rearrange("p (b n two r) -> p b n two r", b=b, two=2, r=seg)[:, :, :, 1, :],
                    level_mask[:, lev, :].bitcast(i32).rearrange("p (n r) -> p n r", r=seg)
                    .unsqueeze(1).broadcast_to([P, b, ns, seg]),
                    scr[pair][:, 0, :].rearrange("p (b n r) -> p b n r", b=b, r=seg)).then_inc(job_read[pair], 1)

            def cross(num, job):
                dve.wait_ge(job_done, num.of("job", job) + 1)
                pair = num.first("job", job) % 2
                dve.tensor_copy(att_x, scr[pair][:, 0, :]).then_inc(job_read[pair], 1)

            def head_mean_squares(num):
                dve.wait_ge(osq_ready, num.of("grp", 0) + 1)
                mean_squares(osq.rearrange("p (b v) -> p b v", b=NT * HG), NT * HG, HD)

            def head_outputs(num, job):
                dve.wait_ge(rstd_ready, num.of("rstd", 0) + 1)
                pair = num.first("job", job) % 2
                dve.tensor_tensor(out=hid[:].rearrange("p c (h v) -> p h c v", h=HG),
                                  in0=scr[pair][:].rearrange("p two (h c v) -> p (two h) c v", c=NT, v=HD),
                                  in1=r_head[:].rearrange("p (h c) -> p h c", c=NT).unsqueeze(3)
                                  .broadcast_to([P, HG, NT, HD]), op=ALU.mult).then_inc(job_read[pair], 1)
                dve.drain()
                dve.tensor_tensor(out=hid[:], in0=hid[:], in1=zg[:], op=ALU.mult).then_inc(hid_ready, 1)

            def y_pieces(num, jobs, kt0):
                for c, job in enumerate(jobs):
                    dve.wait_ge(piece_hi, num.of("piece", c) + 1)
                    pair = num.first("job", job) % 2
                    kts = bass.ds(kt0 + KU * c, KU)
                    dve.scalar_tensor_tensor(out=y_lo[:, kts, :].rearrange("p k t -> p (k t)"),
                                             in0=scr[pair][:, 0, :], scalar=cols[:, C_ON:C_ON + 1],
                                             in1=y_hi[:, kts, :].bitcast(f32).rearrange("p k t -> p (k t)"),
                                             op0=ALU.mult, op1=ALU.subtract).then_inc(job_read[pair], 1)

            def own_steps(num, group, zf_job, diag_job):
                return {17: [lambda: fk(num, zf_job, group)], 19: [totals],
                        28: [lambda: diagonal(num, diag_job)],
                        30: [lambda: level(num, 0, diag_job + 1)]}

            units(first, range(14, 32), own_steps(first, 0, 0, 2))
            with dve.Fori(0, 3) as it:
                num = Numbers("hg_loop", it)
                steps = own_steps(num, it + 1, 6, 11)
                for lev in range(1, len(LEVELS)):
                    steps[2 * lev - 2] = [lambda lev=lev: level(num, lev, lev - 2)]
                steps[12] = [lambda: cross(num, 5)]
                steps[16] = [lambda: head_mean_squares(num)]
                steps[18] = [lambda: head_outputs(num, 7)]
                steps[25] = [lambda: y_pieces(num, (9, 10), it * HG)]
                units(num, range(32), steps)
            out_num = Numbers("hg_out")
            steps = {lev - 1: [lambda lev=lev: level(out_num, lev, lev - 2)] for lev in range(1, len(LEVELS))}
            steps[6] = [lambda: cross(out_num, 5)]
            steps[11] = [lambda: head_mean_squares(out_num), lambda: head_outputs(out_num, 6)]
            steps[13] = [lambda: y_pieces(out_num, (7, 8), 3 * HG)]

            def out_steps(num, norm, p_job):
                return {17: [lambda: piece(num, 2, p_job, p_hi[:], p_lo[:])],
                        16: [lambda: take_m(num, 0, 13, 0)], 18: [lambda: take_m(num, 1, 15, 1)],
                        22: [lambda: times_gain(norm, 0)], 24: [lambda: times_gain(norm, 1)],
                        26: [lambda: take_m(num, 2, 23, 2)], 31: [lambda: times_gain(norm, 2)]}
            steps.update(out_steps(out_num, "mix_norm0", 9))
            units(out_num, range(32), steps)

            def layer_tail(layer, out_num):
                s = str(layer)
                mix, ffn = Numbers("mix_norm" + s), Numbers("ffn_norm" + s)
                first, last, ple = Numbers("ffn_first" + s), Numbers("ffn_last" + s), Numbers("ple" + s)

                norm = "mix_norm" + s
                boundary_splits(split, mix, first, range(2), True)
                tail_out(norm, out_num)
                operand(norm, first, C_FFN[layer], add_block(norm, 2), True)
                units(first, range(8, 16), {9: [lambda: pre_factor("mix_norm" + s)]})

                def hidden(num, task, last_unit):
                    dve.wait_ge(w_used, num.of("unit", last_unit) + 1)
                    pair = num.first("task", task) % 2
                    for t in range(NT):
                        i = dve.scalar_tensor_tensor(out=hid[:, t, :], in0=acc[pair][:, t, :],
                                                     scalar=r_pre[:, t:t + 1], in1=sg[:, t, :],
                                                     op0=ALU.mult, op1=ALU.mult)
                    i.then_inc(acc_read[pair], 1)

                def hid_pieces(num, job, kt):
                    for c in range(2):
                        kts = slice(kt + KU * c, kt + KU * c + KU)
                        piece(num, job + c, job + c, y_hi[:, kts, :], y_lo[:, kts, :])

                dve.wait_ge(m_zeroed, layer + 1)
                with dve.Fori(0, HB - 2) as it:
                    body = Numbers("ffn_loop" + s, it)
                    units(body, range(24),
                          {2: [lambda: hidden(body, -1, -1)], 7: [lambda: hid_pieces(body, 0, 0)]}
                          | {12 + 2 * nb: [lambda nb=nb: take_m(body, 1 + nb, 9 + 2 * nb, nb, True)]
                             for nb in range(NB)})
                norm = "ffn_norm" + s
                units(last, range(32), {2: [lambda: hidden(last, -1, -1)], 7: [lambda: hid_pieces(last, 0, 0)],
                                        17: [lambda: hidden(last, 1, 15)], 18: [lambda: hid_pieces(last, 2, GC)],
                                        22: [lambda: take_m(last, 2, 19, 0, True)],
                                        26: [lambda: take_m(last, 3, 23, 1, True)],
                                        27: [lambda: times_gain(norm, 0)],
                                        30: [lambda: take_m(last, 4, 27, 2, True)],
                                        31: [lambda: times_gain(norm, 1)]})

                boundary_split(split, ffn, ple, 0, True)
                times_gain(norm, 2)
                boundary_split(split, ffn, ple, 1, True)
                tail_down(norm, last)
                operand(norm, ple, None, add_block(norm, 2), True)
                norm = "ple_norm" + s

                def gated(nb):
                    pair = ple.first("task", nb) % 2
                    dve.wait_ge(acc_read[pair], ple.rounds("task", nb, 2))
                    dve.tensor_tensor(out=blk_of(m, nb), in0=blk_of(e, nb), in1=sg[:], op=ALU.mult) \
                        .then_inc(m_ready, 1)
                units(ple, range(8, 32), {11: [lambda: gated(0)], 15: [lambda: times_gain(norm, 0)],
                                          19: [lambda: gated(1)], 23: [lambda: times_gain(norm, 1)],
                                          27: [lambda: gated(2)], 31: [lambda: times_gain(norm, 2)]})

                if layer == 0:
                    boundary_splits(split, None, Numbers("gm_v"), range(2), False)
                tail_gated(norm, ple)
                if layer == 0:
                    operand(norm, Numbers("gm_v"), C_MIX[1], add_block(norm, 1))
                else:
                    for nb in range(NB):
                        add_block(norm, 1)(nb)

            layer_tail(0, out_num)

            gv, gu, go = Numbers("gm_v"), Numbers("gm_u"), Numbers("gm_out")

            def v_stats(num, task, nb):
                pair = num.first("task", task) % 2
                dve.wait_ge(acc_read[pair], num.rounds("task", task, 2))
                for t in range(NT):
                    dve.bn_stats(bn[:, t, nb, :], m[:, t, nb * BLOCK:(nb + 1) * BLOCK])

            def spatial_weights(job):
                dve.wait_ge(job_done, gv.of("job", job) + 1)
                pair = gv.first("job", job) % 2
                dve.tensor_tensor(out=wsT[:, job * BLOCK:(job + 1) * BLOCK].rearrange("p (g t) -> p g t", t=P),
                                  in0=scr[pair][:, 0, :].rearrange("p (g t) -> p g t", t=P),
                                  in1=upper[:].unsqueeze(1).broadcast_to([P, GC, P]), op=ALU.mult) \
                    .then_inc(job_read[pair], 1)

            def v_factor():
                dve.drain()
                for t in range(NT):
                    dve.bn_aggr(mv[:, t, :], bn[:, t, :, :].rearrange("p a b -> p (a b)"))
                dve.drain()
                dve.tensor_scalar(ms[:, 0:NT], mv[:, :, 1], EPS, None, ALU.add).then_inc(ms_ready, 1)

            def layer_norm(nb):
                if nb == 0:
                    dve.wait_ge(rstd_ready, gu.of("rstd", 0) + 1)
                    dve.wait_ge(gain_loaded, 16 * (GAINS["ln"] + 1))
                    dve.wait_ge(ln_b_loaded, 16)
                for t in range(NT):
                    cs = slice(nb * BLOCK, (nb + 1) * BLOCK)
                    dve.tensor_scalar(m[:, t, cs], m[:, t, cs], mv[:, t, 0:1], r_head[:, t:t + 1],
                                      ALU.subtract, ALU.mult)
                dve.drain()
                dve.tensor_tensor(out=blk_of(m, nb), in0=blk_of(m, nb), in1=gain_of(nb), op=ALU.mult)
                dve.drain()
                dve.tensor_tensor(out=blk_of(m, nb), in0=blk_of(m, nb),
                                  in1=ln_b[:, nb * BLOCK:(nb + 1) * BLOCK].unsqueeze(1).broadcast_to([P, NT, BLOCK]),
                                  op=ALU.add).then_inc(ln_ready, 1)

            def gm_outputs(num, task, job, nb):
                dve.wait_ge(acc_read[num.first("task", task) % 2], num.rounds("task", task, 2))
                dve.wait_ge(job_done, num.of("job", job) + 1)
                pair = num.first("job", job) % 2
                for g in range(GC):
                    cs = slice(g * P, (g + 1) * P)
                    i = dve.scalar_tensor_tensor(out=hid[:, :, cs], in0=scr[pair][:, :, cs],
                                                 scalar=cols[:, C_BS + GC * nb + g:C_BS + GC * nb + g + 1],
                                                 in1=sg[:, :, cs], op0=ALU.add, op1=ALU.mult)
                i.then_inc(job_read[pair], 1)

            def gm_pieces(num, nth, jobs, nb):
                for c, job in enumerate(jobs):
                    kts = slice(GC * nb + KU * c, GC * nb + KU * c + KU)
                    piece(num, nth + c, job, y_hi[:, kts, :], y_lo[:, kts, :])

            units(gv, range(8, 32), {9: [lambda: pre_factor("ple_norm0")], 11: [lambda: v_stats(gv, 0, 0)],
                                     19: [lambda: v_stats(gv, 1, 1)], 27: [lambda: v_stats(gv, 2, 2)]}
                  | {14 + j: [lambda j=j: spatial_weights(j)] for j in range(NB)})
            units(gu, range(32), {3: [lambda: v_stats(gu, -1, 3), v_factor], 4: [lambda: layer_norm(0)],
                                  6: [lambda: layer_norm(1)], 9: [lambda: layer_norm(2)],
                                  13: [lambda: layer_norm(3)],
                                  11: [lambda: gm_outputs(gu, 0, 0, 0)], 15: [lambda: gm_pieces(gu, 0, (1, 2), 0)],
                                  19: [lambda: gm_outputs(gu, 1, 3, 1)], 23: [lambda: gm_pieces(gu, 2, (4, 5), 1)],
                                  27: [lambda: gm_outputs(gu, 2, 6, 2)], 31: [lambda: gm_pieces(gu, 4, (7, 8), 2)]})
            units(go, range(32), {3: [lambda: gm_outputs(go, -1, 0, 3)], 7: [lambda: gm_pieces(go, 0, (1, 2), 3)]}
                  | out_steps(go, "mix_norm1", 3))
            layer_tail(1, go)

        @block.tensor
        def _(pe):
            def unit(num, k, task, x_hi, x_lo, kt, is_first, is_last, x_lo_ready=None):
                pair = num.first("task", task) % 2
                if is_first and num.first("task", task) >= 2:
                    pe.wait_ge(acc_read[pair], num.rounds("task", task, 2) - 1)
                pe.wait_ge(w_lo_ready, num.of("unit", k) + 1)
                r = num.first("unit", k) % RING
                for products in ((0, 1, 2),) if x_lo_ready is None else ((0, 1), (2,)):
                    if products == (2,):
                        x_lo_ready()
                    for c in range(KU):
                        wh, wl = (w[:, r, c * BLOCK:(c + 1) * BLOCK] for w in (w_hi, w_lo))
                        for t in range(NT):
                            ts = slice(t * P, (t + 1) * P)
                            xh, xl = x_hi[:, kt + c, ts], x_lo[:, kt + c, ts]
                            for n in products:
                                a, b = ((xh, wl), (xh, wh), (xl, wh))[n]
                                i = pe.matmul(acc[pair][:, t, :], a, b, start=is_first and c == 0 and n == 0,
                                              stop=is_last and c == KU - 1 and n == 2)
                i.then_inc(w_used, 1)

            def last_units(norm, num, k, task, x_hi, x_lo, kt):
                pair = num.first("task", task) % 2
                for t in range(NT):
                    ts = slice(t * P, (t + 1) * P)
                    for u in range(2):
                        if t == 0:
                            pe.wait_ge(w_lo_ready, num.of("unit", k + u) + 1)
                        r = num.first("unit", k + u) % RING
                        for c in range(KU):
                            wh, wl = (w[:, r, c * BLOCK:(c + 1) * BLOCK] for w in (w_hi, w_lo))
                            xh, xl = (x_[:, kt + KU * u + c, ts] for x_ in (x_hi, x_lo))
                            for n, (a, b) in enumerate(((xh, wl), (xh, wh), (xl, wh))):
                                i = pe.matmul(acc[pair][:, t, :], a, b, start=False,
                                              stop=u == 1 and c == KU - 1 and n == 2)
                        if t == 1:
                            i.then_inc(w_used, 1)
                        elif u == 1:
                            i.then_inc(tile_done, 1)

            def in_unit(num, k, unit0=0, task0=0, x_lo_ready=None):
                t, q = k // 8, k % 8
                unit(num, unit0 + k, task0 + t, a_hi, a_lo, KU * q, q == 0, q == 7, x_lo_ready)

            def job_begin(num, job):
                pair = num.first("job", job) % 2
                if num.first("job", job) >= 2:
                    pe.wait_ge(job_read[pair], num.rounds("job", job, 2) - 1)
                return scr[pair]

            def transpose_piece(num, job, src):
                s = job_begin(num, job)
                for c in range(KU):
                    for t in range(NT):
                        i = pe.transpose(s[:, 0, c * T + t * P:c * T + (t + 1) * P], src(c, t), ident[:])
                i.then_inc(job_done, 1)

            def operand(name, nxt, emb=None):
                num, job0 = Numbers(name), 1 if name == "start" else 0

                def transpose(pc):
                    if name == "start":
                        pe.wait_ge(x_loaded[pc // 2], 16)
                    else:
                        pe.wait_ge(h_ready, H_STEPS * NORMS[name] + (1 if pc == 0 else pc // 2 + 2))
                    transpose_piece(num, job0 + pc,
                                    lambda c, t: h[:, t, (KU * pc + c) * P:(KU * pc + c + 1) * P])

                def embedding(i):
                    unit(num, i, i, p_hi, p_lo, 0, True, True)
                if emb is not None:
                    if emb == 0:
                        piece_ready(*{"mix_norm0": (Numbers("hg_out"), 9), "mix_norm1": (Numbers("gm_out"), 3)}[name])
                    embedding(0)
                transpose(0)
                if emb is not None:
                    embedding(1)
                for pc in range(8):
                    if pc < 7:
                        transpose(pc + 1)
                    if pc == 0:
                        pe.wait_ge(piece_hi, num.of("piece", 0) + 1)
                        in_unit(nxt, pc, x_lo_ready=lambda: piece_ready(num, job0))
                    else:
                        piece_ready(num, job0 + pc)
                        in_unit(nxt, pc)
                    if name == "start" and pc == 6:
                        pe.wait_ge(rows_loaded, 16 * 4)
                        s = job_begin(num, 9)
                        pe.transpose(s[:, 0, 0:P], rows[:], ident[:]).then_inc(job_done, 1)

            def piece_ready(num, job):
                pe.wait_ge(job_read[num.first("job", job) % 2], num.rounds("job", job, 2))

            pe.wait_ge(const_step, 6)
            n = C_FFN[0]
            pe.wait_ge(mix_rows_loaded, 16)
            pe.transpose(scr[0][:, 0, 0:n], rows[0:n, :], ident[0:n, 0:n]).then_inc(job_done, 1)
            first = Numbers("hg_first")
            operand("start", first)

            B = NT * HG

            def transpose_group(num, job, task):
                pair = num.first("task", task) % 2
                pe.wait_ge(acc_read[pair], num.rounds("task", task, 2))
                s = job_begin(num, job)
                for hd in range(HG):
                    for t in range(NT):
                        col = hd * T + t * P
                        i = pe.transpose(s[:, col // BLOCK, col % BLOCK:col % BLOCK + P],
                                         sg[:, t, hd * P:(hd + 1) * P], ident[:])
                i.then_inc(job_done, 1)

            def kq_wait(num, nth):
                pe.wait_ge(kq_ready, num.of("kq", nth) + 1)

            def diagonal(num, job, zq_job, kq):
                kq_wait(num, kq)
                pe.wait_ge(job_read[num.first("job", zq_job) % 2], num.rounds("job", zq_job, 2))
                s = job_begin(num, job)
                for b in range(B):
                    cs = slice(b * P, (b + 1) * P)
                    i = pe.matmul(s[:, b // HG, b % HG * P:(b % HG + 1) * P], k_g[:, cs], q_g[:, cs],
                                  start=True, stop=True)
                i.then_inc(job_done, 1)

            def level(num, lev, job, kq):
                kq_wait(num, kq)
                s = job_begin(num, job)
                seg = LEVELS[lev]
                for b in range(B):
                    odd = q_g[:, b * P:(b + 1) * P].rearrange("p (n two r) -> p n two r", two=2, r=seg)[:, :, 1, :]
                    i = pe.matmul(s[:, 0, b * P // 2:(b + 1) * P // 2], k_g[:, b * P:(b + 1) * P], odd,
                                  start=True, stop=True)
                i.then_inc(job_done, 1)

            def cross(num, job, kq):
                kq_wait(num, kq)
                s = job_begin(num, job)
                for hd in range(HG):
                    i = pe.matmul(s[:, 0, hd * P:(hd + 1) * P], k_g[:, hd * T:hd * T + P],
                                  q_g[:, hd * T + P:(hd + 1) * T], start=True, stop=True)
                i.then_inc(job_done, 1)

            def outputs(num, job, cross_job):
                pe.wait_ge(job_read[num.first("job", cross_job) % 2], num.rounds("job", cross_job, 2))
                s = job_begin(num, job)
                for hd in range(HG):
                    v0, v1 = (v_g[:, t, hd * P:(hd + 1) * P] for t in range(NT))
                    for t in range(NT):
                        b = NT * hd + t
                        dst = s[:, b // HG, b % HG * P:(b % HG + 1) * P]
                        i = pe.matmul(dst, att[:, b * P:(b + 1) * P], (v0, v1)[t], start=True, stop=t == 0)
                        if t == 1:
                            i = pe.matmul(dst, att_x[:, hd * P:(hd + 1) * P], v0, start=False, stop=True)
                i.then_inc(job_done, 1)

            def group_transposes(num, jobs):
                pe.wait_ge(hid_ready, num.of("grp", 0) + 1)
                for c2, job in enumerate(jobs):
                    transpose_piece(num, job, lambda c, t: hid[:, t, (KU * c2 + c) * P:(KU * c2 + c + 1) * P])

            def own_steps(num, zf, zq, diag, kq):
                return {11: [lambda: transpose_group(num, zf, 0)], 17: [lambda: transpose_group(num, zq, 1)],
                        26: [lambda: diagonal(num, diag, zq, kq)], 28: [lambda: level(num, 0, diag + 1, kq + 1)],
                        30: [lambda: level(num, 1, diag + 2, kq + 2)]}

            def in_units(num, ks, steps, **kw):
                for k in ks:
                    in_unit(num, k, **kw)
                    for step in steps.get(k, ()):
                        step()

            def out_units(norm, num, steps, ready):
                for k, (t, q) in enumerate(OUT_ORDER[:-2]):
                    if q in (6, 7) and t == 0:
                        piece_ready(num, ready[q - 6])
                    unit(num, k, t, y_hi, y_lo, KU * q, q == 0, q == 7)
                    for step in steps.get(k, ()):
                        step()
                last_units(norm, num, 30, 3, y_hi, y_lo, KU * 6)

            in_units(first, range(8, 32), own_steps(first, 0, 1, 2, 0))
            with pe.Fori(0, 3) as it:
                num = Numbers("hg_loop", it)
                steps = own_steps(num, 6, 8, 11, 6)
                for lev in range(2, len(LEVELS)):
                    steps[2 * lev - 4] = [lambda lev=lev: level(num, lev, lev - 2, lev - 2)]
                steps[10] = [lambda: cross(num, 5, 5)]
                steps[13] = [lambda: outputs(num, 7, 5)]
                steps[22] = [lambda: group_transposes(num, (9, 10))]
                in_units(num, range(32), steps)
            num = Numbers("hg_out")

            def p_transposes(num, job, layer):
                pe.wait_ge(p_loaded, 16 * (layer + 1))
                transpose_piece(num, job, lambda c, t: p_tm[layer][:, t, c * P:(c + 1) * P])
            steps = {lev - 2: [lambda lev=lev: level(num, lev, lev - 2, lev - 2)] for lev in range(2, len(LEVELS))}
            steps[5] = [lambda: cross(num, 5, 5)]
            steps[7] = [lambda: outputs(num, 6, 5)]
            steps[10] = [lambda: group_transposes(num, (7, 8))]
            steps[14] = [lambda: p_transposes(num, 9, 0)]
            out_units("mix_norm0", num, steps, (7, 8))

            def layer_tail(layer):
                s = str(layer)
                first, last, ple = Numbers("ffn_first" + s), Numbers("ffn_last" + s), Numbers("ple" + s)
                operand("mix_norm" + s, first, 0)
                in_units(first, range(8, 16), {})

                def hid_transposes(num, task, job):
                    pair = num.first("task", task) % 2
                    pe.wait_ge(acc_read[pair], num.rounds("task", task, 2))
                    for c2 in range(2):
                        transpose_piece(num, job + c2,
                                        lambda c, t: hid[:, t, (KU * c2 + c) * P:(KU * c2 + c + 1) * P])

                with pe.Fori(0, HB - 2) as it:
                    body = Numbers("ffn_loop" + s, it)
                    in_units(body, range(8), {4: [lambda: hid_transposes(body, -1, 0)]})
                    for job in range(2):
                        piece_ready(body, job)
                    for nb in range(NB):
                        for q in range(2):
                            unit(body, 8 + 2 * nb + q, 1 + nb, y_hi, y_lo, KU * q, q == 0, q == 1)
                    in_units(body, range(8), {}, unit0=16, task0=5)
                in_units(last, range(16), {4: [lambda: hid_transposes(last, -1, 0)]})
                for nb in range(NB):
                    for q in range(4 if nb < NB - 1 else 2):
                        if nb == 0 and q != 1:
                            for job in {0: (0, 1), 2: (2,), 3: (3,)}[q]:
                                piece_ready(last, job)
                        unit(last, 16 + 4 * nb + q, 2 + nb, y_hi, y_lo, KU * q, q == 0, q == 3)
                        if nb == 0 and q == 0:
                            hid_transposes(last, 1, 2)
                last_units("ffn_norm" + s, last, 30, 5, y_hi, y_lo, KU * 2)
                operand("ffn_norm" + s, ple, 2)
                in_units(ple, range(8, 30), {})
                last_units("ple_norm" + s, ple, 30, 3, a_hi, a_lo, KU * 6)

            layer_tail(0)

            gv, gu, go = Numbers("gm_v"), Numbers("gm_u"), Numbers("gm_out")
            operand("ple_norm0", gv)

            def ws_transposes(job):
                pe.wait_ge(ws_loaded, 16)
                s = job_begin(gv, job)
                for g in range(GC):
                    cs = slice((GC * job + g) * P, (GC * job + g + 1) * P)
                    i = pe.transpose(s[:, 0, g * P:(g + 1) * P], ws_raw[:, cs], ident[:])
                i.then_inc(job_done, 1)

            def spatial(num, job, nb):
                pe.wait_ge(ln_ready, nb + 1)
                s = job_begin(num, job)
                for g in range(GC):
                    cs = slice((GC * nb + g) * P, (GC * nb + g + 1) * P)
                    for t in range(NT):
                        i = pe.matmul(s[:, t, g * P:(g + 1) * P], wsT[:, cs], m[:, t, cs], start=True, stop=True)
                i.then_inc(job_done, 1)

            def gm_transposes(num, sv_job):
                piece_ready(num, sv_job)
                for c2 in range(2):
                    transpose_piece(num, sv_job + 1 + c2,
                                    lambda c, t: hid[:, t, (KU * c2 + c) * P:(KU * c2 + c + 1) * P])
            in_units(gv, range(8, 32), {12 + j: [lambda j=j: ws_transposes(j)] for j in range(NB)})
            in_units(gu, range(32), {8: [lambda: spatial(gu, 0, 0)], 12: [lambda: gm_transposes(gu, 0)],
                                     16: [lambda: spatial(gu, 3, 1)], 20: [lambda: gm_transposes(gu, 3)],
                                     24: [lambda: spatial(gu, 6, 2)], 28: [lambda: gm_transposes(gu, 6)]})
            out_units("mix_norm1", go, {0: [lambda: spatial(go, 0, 3)], 4: [lambda: gm_transposes(go, 0)],
                           14: [lambda: p_transposes(go, 3, 1)]}, (1, 2))
            layer_tail(1)


_INS = ["x", "p", "hg_w_in", "hg_lb_logits", "hg_out_norm", "hg_w_out", "gm_w_in", "gm_ln_g", "gm_ln_b",
        "gm_w_s", "gm_b_s", "gm_w_out", "norm_mix_pre", "norm_mix_post", "norm_ffn_pre", "norm_ffn_post",
        "ffn_w_gate", "ffn_w_up", "ffn_w_down", "ple_w_proj", "ple_w_gate", "ple_norm"]


def kernel(**inputs):
    import numpy as np
    import concourse.bacc as bacc
    from concourse.bass_utils import run_bass_kernel_spmd

    nc = bacc.Bacc("TRN2", target_bir_lowering=False, num_devices=1)
    arrays, args = {}, []
    for name in _INS:
        a = np.ascontiguousarray(inputs[name])
        arrays[f"in_{name}"] = a
        args.append(nc.dram_tensor(f"in_{name}", a.shape, mybir.dt.from_np(a.dtype), kind="ExternalInput").ap())
    shape = inputs["x"].shape
    args.append(nc.dram_tensor("out_h", shape, mybir.dt.float32, kind="ExternalOutput").ap())
    trunk(nc, *args)
    r = run_bass_kernel_spmd(nc, [arrays], core_ids=[0])
    return r.results[0]["out_h"]
```
